# Optimizing a Trainium2 kernel written in Bass

```python
import jax, jax.numpy as jnp
from jax import lax
import numpy as np

D_MODEL = 1024
BATCH = 1
SEQ = 1024
DEPTH = 1
DEC_BATCH = 8
DEC_SEQ = 4
PAST_LEN = 4096
PAGE_SIZE = 128

N_HEADS = 8
HEAD_DIM = 64
N_KV_HEADS = 2
N_IDX_HEADS = 4
IDX_DIM = 64
CONV_DIM = 512
CONV_WIDTH = 3
D_FF = 2816
N_META = 16
TOPK_MAX = 256
TOPK_FRACTION = 4
Q_BLOCK = 128
ROPE_THETA = 500000.0
ROPE_FRACTION = 4
NORM_EPS = 1e-6

kernel_name = "dsa_shortconv_gated_hybrid_step"

def _split_points():
    sizes = [N_HEADS * HEAD_DIM, N_KV_HEADS * HEAD_DIM, N_KV_HEADS * HEAD_DIM,
             N_IDX_HEADS * IDX_DIM, IDX_DIM, N_IDX_HEADS,
             CONV_DIM, CONV_DIM, CONV_DIM, D_MODEL, D_MODEL]
    pts, acc = [], 0
    for s in sizes[:-1]:
        acc += s
        pts.append(acc)
    return pts

def _proj_width():
    return (N_HEADS * HEAD_DIM + 2 * N_KV_HEADS * HEAD_DIM + N_IDX_HEADS * IDX_DIM + IDX_DIM
            + N_IDX_HEADS + 3 * CONV_DIM + 2 * D_MODEL)

def rms_norm(x, g):
    x32 = x.astype(jnp.float32)
    r = lax.rsqrt(jnp.mean(x32 * x32, axis=-1, keepdims=True) + NORM_EPS)
    return (x32 * r).astype(x.dtype) * g

def partial_rope(x, pos):
    rot = x.shape[-1] // ROPE_FRACTION
    half = rot // 2
    inv = jnp.power(ROPE_THETA, -jnp.arange(half, dtype=jnp.float32) * 2.0 / rot)
    ang = pos.astype(jnp.float32)[:, None] * inv[None, :]
    cos = jnp.cos(ang)[:, None, :].astype(x.dtype)
    sin = jnp.sin(ang)[:, None, :].astype(x.dtype)
    x1, x2, xp = x[..., :half], x[..., half:rot], x[..., rot:]
    return jnp.concatenate([x1 * cos - x2 * sin, x2 * cos + x1 * sin, xp], axis=-1)

def causal_dwconv(u, prev, w):
    T = u.shape[1]
    full = jnp.concatenate([prev.astype(u.dtype), u], axis=1)
    out = full[:, 0:T] * w[0]
    for j in range(1, CONV_WIDTH):
        out = out + full[:, j:j + T] * w[j]
    return out, full[:, T:]

def indexer_scores(qi, wi, ki):
    s = jax.nn.relu(jnp.einsum('bqhd,bsd->bqhs', qi, ki))
    return jnp.einsum('bqhs,bqh->bqs', s, wi).astype(jnp.float32)

def sparse_attend(q, k_sel, v_sel, valid):
    Bn, Q = q.shape[0], q.shape[1]
    qg = q.reshape(Bn, Q, N_KV_HEADS, N_HEADS // N_KV_HEADS, HEAD_DIM)
    logits = jnp.einsum('bqngd,bqsnd->bqngs', qg, k_sel).astype(jnp.float32) * (HEAD_DIM ** -0.5)
    logits = jnp.where(valid[:, :, None, None, :], logits, -jnp.inf)
    p = jax.nn.softmax(logits, axis=-1).astype(v_sel.dtype)
    o = jnp.einsum('bqngs,bqsnd->bqngd', p, v_sel)
    return o.reshape(Bn, Q, N_HEADS * HEAD_DIM)

def make_prompt_attend(T, k_top):
    def attend(q, k, v, qi, ki, wi):
        Bn = q.shape[0]
        n_blk = -(-T // Q_BLOCK)
        pad = n_blk * Q_BLOCK - T

        def blocks(a):
            a = jnp.pad(a, [(0, 0), (0, pad)] + [(0, 0)] * (a.ndim - 2))
            return jnp.moveaxis(a.reshape((Bn, n_blk, Q_BLOCK) + a.shape[2:]), 1, 0)

        qpos = jnp.arange(n_blk * Q_BLOCK).reshape(n_blk, Q_BLOCK)
        kpos = jnp.arange(T)
        bidx = jnp.arange(Bn)[:, None, None]

        def one_block(xs):
            qb, qib, wib, qp = xs
            scores = indexer_scores(qib, wib, ki)
            scores = jnp.where(kpos[None, None, :] <= qp[None, :, None], scores, -jnp.inf)
            vals, idx = lax.top_k(scores, k_top)
            return sparse_attend(qb, k[bidx, idx], v[bidx, idx], jnp.isfinite(vals))

        out = lax.map(one_block, (blocks(q), blocks(qi), blocks(wi), qpos))
        return jnp.moveaxis(out, 0, 1).reshape(Bn, n_blk * Q_BLOCK, -1)[:, :T]
    return attend

def make_sample_attend(cache_k_l, cache_v_l, cache_kidx_l, page_table, k_top):
    def attend(q, k, v, qi, ki, wi):
        Bn, DS = q.shape[0], q.shape[1]
        L = PAST_LEN + DS
        ki_past = cache_kidx_l[page_table].reshape(Bn, PAST_LEN, IDX_DIM).astype(ki.dtype)
        ki_all = jnp.concatenate([ki_past, ki], axis=1)
        scores = indexer_scores(qi, wi, ki_all)
        qpos = PAST_LEN + jnp.arange(DS)
        kpos = jnp.arange(L)
        scores = jnp.where(kpos[None, None, :] <= qpos[None, :, None], scores, -jnp.inf)
        vals, idx = lax.top_k(scores, k_top)
        bidx = jnp.arange(Bn)[:, None, None]
        past_i = jnp.minimum(idx, PAST_LEN - 1)
        phys = page_table[bidx, past_i // PAGE_SIZE]
        off = past_i % PAGE_SIZE
        new_i = jnp.clip(idx - PAST_LEN, 0, DS - 1)
        is_new = (idx >= PAST_LEN)[..., None, None]
        k_sel = jnp.where(is_new, k[bidx, new_i], cache_k_l[phys, off].astype(k.dtype))
        v_sel = jnp.where(is_new, v[bidx, new_i], cache_v_l[phys, off].astype(v.dtype))
        return sparse_attend(q, k_sel, v_sel, jnp.isfinite(vals))
    return attend

def trunk_layer(x, pos, attend, conv_prev, ffn_prev, w_in, w_pa, w_pb, w_o, conv_w,
                norm1, norm2, ffn_up, ffn_conv_w, ffn_down):
    Bn, T, _ = x.shape
    hn = rms_norm(x, norm1)
    proj = hn @ w_in
    q, k, v, qi, ki, wi, cb, cc, cx, ga, gb = jnp.split(proj, _split_points(), axis=-1)
    q = partial_rope(q.reshape(Bn, T, N_HEADS, HEAD_DIM), pos)
    k = partial_rope(k.reshape(Bn, T, N_KV_HEADS, HEAD_DIM), pos)
    v = v.reshape(Bn, T, N_KV_HEADS, HEAD_DIM)
    qi = partial_rope(qi.reshape(Bn, T, N_IDX_HEADS, IDX_DIM), pos)
    ki = partial_rope(ki[:, :, None, :], pos)[:, :, 0, :]
    wi = wi * ((N_IDX_HEADS * IDX_DIM) ** -0.5)
    a = attend(q, k, v, qi, ki, wi)
    u, conv_new = causal_dwconv(cc * cx, conv_prev, conv_w)
    b = cb * u
    mixed = jax.nn.sigmoid(ga) * (a @ w_pa) + jax.nn.sigmoid(gb) * (b @ w_pb)
    x = x + mixed @ w_o
    hn2 = rms_norm(x, norm2)
    ua, ub = jnp.split(hn2 @ ffn_up, 2, axis=-1)
    ua_c, ffn_new = causal_dwconv(ua, ffn_prev, ffn_conv_w)
    x = x + (jax.nn.silu(ua_c) * ub) @ ffn_down
    return x, k, v, ki, conv_new, ffn_new

def setup_inputs(seed: int = 0) -> dict:
    key = jax.random.key(seed)
    ks = jax.random.split(key, 24)
    n_pages = PAST_LEN // PAGE_SIZE
    n_used = DEC_BATCH * n_pages
    n_pool = n_used + n_used // 4
    f32 = jnp.float32
    nrm = lambda k, shp, s: jax.random.normal(k, shp, f32) * s
    page_table = jax.random.permutation(ks[0], n_pool)[:n_used].reshape(DEC_BATCH, n_pages).astype(jnp.int32)
    return {
        "x_prompt": nrm(ks[1], (BATCH, SEQ, D_MODEL), 1.0),
        "x_sample": nrm(ks[2], (DEC_BATCH, DEC_SEQ, D_MODEL), 1.0),
        "cache_k": nrm(ks[3], (DEPTH, n_pool, PAGE_SIZE, N_KV_HEADS, HEAD_DIM), 1.0),
        "cache_v": nrm(ks[4], (DEPTH, n_pool, PAGE_SIZE, N_KV_HEADS, HEAD_DIM), 1.0),
        "cache_kidx": nrm(ks[5], (DEPTH, n_pool, PAGE_SIZE, IDX_DIM), 1.0),
        "state_conv": nrm(ks[6], (DEPTH, DEC_BATCH, CONV_WIDTH - 1, CONV_DIM), 1.0),
        "state_ffn_conv": nrm(ks[7], (DEPTH, DEC_BATCH, CONV_WIDTH - 1, D_FF), 1.0),
        "page_table": page_table,
        "meta_tokens": nrm(ks[8], (N_META, D_MODEL), 1.0),
        "w_in": nrm(ks[9], (DEPTH, D_MODEL, _proj_width()), D_MODEL ** -0.5),
        "w_pa": nrm(ks[10], (DEPTH, N_HEADS * HEAD_DIM, D_MODEL), (N_HEADS * HEAD_DIM) ** -0.5),
        "w_pb": nrm(ks[11], (DEPTH, CONV_DIM, D_MODEL), CONV_DIM ** -0.5),
        "w_o": nrm(ks[12], (DEPTH, D_MODEL, D_MODEL), D_MODEL ** -0.5),
        "conv_w": nrm(ks[13], (DEPTH, CONV_WIDTH, CONV_DIM), CONV_WIDTH ** -0.5),
        "norm1": 1.0 + nrm(ks[14], (DEPTH, D_MODEL), 0.01),
        "norm2": 1.0 + nrm(ks[15], (DEPTH, D_MODEL), 0.01),
        "ffn_up": nrm(ks[16], (DEPTH, D_MODEL, 2 * D_FF), D_MODEL ** -0.5),
        "ffn_conv_w": nrm(ks[17], (DEPTH, CONV_WIDTH, D_FF), CONV_WIDTH ** -0.5),
        "ffn_down": nrm(ks[18], (DEPTH, D_FF, D_MODEL), D_FF ** -0.5),
        "norm_final": 1.0 + nrm(ks[19], (D_MODEL,), 0.01),
    }

def reference(x_prompt, x_sample, cache_k, cache_v, cache_kidx, state_conv, state_ffn_conv, page_table,
              meta_tokens, w_in, w_pa, w_pb, w_o, conv_w, norm1, norm2, ffn_up, ffn_conv_w, ffn_down,
              norm_final):
    Bp = x_prompt.shape[0]
    T_p = SEQ + N_META
    k_top_p = min(TOPK_MAX, T_p // TOPK_FRACTION)
    k_top_s = min(TOPK_MAX, (PAST_LEN + DEC_SEQ) // TOPK_FRACTION)
    pos_p = jnp.arange(T_p)
    pos_s = PAST_LEN + jnp.arange(DEC_SEQ)

    meta = jnp.broadcast_to(meta_tokens[None].astype(x_prompt.dtype), (Bp, N_META, D_MODEL))
    h_p = jnp.concatenate([meta, x_prompt], axis=1)
    h_s = x_sample
    prompt_attend = make_prompt_attend(T_p, k_top_p)

    kp, vp, kip, cp, fp = [], [], [], [], []
    ksm, vsm, kism, csm, fsm = [], [], [], [], []
    for l in range(DEPTH):
        weights = (w_in[l], w_pa[l], w_pb[l], w_o[l], conv_w[l], norm1[l], norm2[l],
                   ffn_up[l], ffn_conv_w[l], ffn_down[l])
        zc = jnp.zeros((Bp, CONV_WIDTH - 1, CONV_DIM), h_p.dtype)
        zf = jnp.zeros((Bp, CONV_WIDTH - 1, D_FF), h_p.dtype)
        h_p, k1, v1, ki1, c1, f1 = trunk_layer(h_p, pos_p, prompt_attend, zc, zf, *weights)
        sample_attend = make_sample_attend(cache_k[l], cache_v[l], cache_kidx[l], page_table, k_top_s)
        h_s, k2, v2, ki2, c2, f2 = trunk_layer(h_s, pos_s, sample_attend, state_conv[l],
                                               state_ffn_conv[l], *weights)
        kp.append(k1); vp.append(v1); kip.append(ki1); cp.append(c1); fp.append(f1)
        ksm.append(k2); vsm.append(v2); kism.append(ki2); csm.append(c2); fsm.append(f2)

    y_prompt = rms_norm(h_p, norm_final)[:, N_META:]
    y_sample = rms_norm(h_s, norm_final)
    return (y_prompt, y_sample,
            jnp.stack(kp), jnp.stack(vp), jnp.stack(kip), jnp.stack(cp), jnp.stack(fp),
            jnp.stack(ksm), jnp.stack(vsm), jnp.stack(kism), jnp.stack(csm), jnp.stack(fsm))


_drawn_inputs = setup_inputs


def setup_inputs(seed=0):
    import zlib

    import numpy as np

    out = dict(_drawn_inputs(seed))
    spreads = {}
    factors = {'norm1': 4.08,
     'norm2': 32.346,
     'norm_final': 32.218,
     'cache_k': 4.153,
     'cache_v': 4.668,
     'cache_kidx': 4.337}
    for name, (base, spread) in spreads.items():
        noise = np.random.default_rng([zlib.crc32(name.encode()), seed]).standard_normal(out[name].shape)
        drawn = base * np.exp(spread * noise) if base else spread * noise
        out[name] = __import__('jax').numpy.asarray(drawn.astype(out[name].dtype))
    for name, factor in factors.items():
        out[name] = (out[name] * factor).astype(out[name].dtype)
    return out
```

```python
import numpy as np
import concourse.bass as bass
from concourse import mybir
from contextlib import ExitStack

F32 = mybir.dt.float32
F32R = mybir.dt.float32r
BF16 = mybir.dt.bfloat16
I32 = mybir.dt.int32
U32 = mybir.dt.uint32
ACT = mybir.ActivationFunctionType
ALU = mybir.AluOpType
AX = mybir.AxisListType

D = 1024
SEQ = 1024
META = 16
TP = SEQ + META
NB, DS = 8, 4
NS = NB * DS
PAST, PAGE = 4096, 128
NPAGES = PAST // PAGE
NPOOL = NB * NPAGES * 5 // 4
TOK = TP + NS
CH = 358
TW = 3 * CH
KB = D // 128
H, HD, NKV, G = 8, 64, 2, 4
NIH = 4
CD = 512
CB = CD // 128
FF = 2816
FB = FF // 128
EPS = 1e-6
TOPK = 256
SM = HD ** -0.5
NEG = -3.0e38
BIG = 1.0e30
QC, KC, VC, QIC, KIC, WIC = 0, 512, 640, 768, 1024, 1088
CBC, CCC, CXC, GAC, GBC = 1092, 1604, 2116, 2628, 3652
PW = 4676
NT = 9
ROWS = [128] * 8 + [TOK - 1024]
QROWS = [128] * 8 + [TP - 1024]
NK = [min(128 * (i + 1), TP) for i in range(NT)]
QB0 = TOPK // 128
SOFF = {}
_o = 0
for _i in range(QB0, NT):
    SOFF[_i] = _o
    _o += NK[_i]
SW = _o
MOFF = []
_o = 0
for _i in range(NT):
    MOFF.append(_o)
    _o += NK[_i]
MW = _o
SQ = PAST // 4
SSW = SQ + NS
NSEL = NT - QB0 + 1
GRP = 512
NGRP = PAST // GRP
NST = 16 + 2
BASE = 16640
CONSTS = {}
CONST_W = 0
for _n, _w in (("ident", 128), ("perm", 128), ("fold", 128), ("below", 128), ("place", 256), ("owner", 128),
               ("head", 4), ("newkeep", NS), ("newfill", NS), ("lane", 1), ("bit", 1), ("ones", 128), ("cos", TW), ("sin", TW)):
    CONSTS[_n] = (CONST_W, _w)
    CONST_W += _w
SBUF_END = 229368


class Map:

    R0 = BASE
    R1 = R0 + KB * TW * 4
    W = R1 + 2 * KB * TW * 4
    C = W + 9 * 4096
    R2 = C + 33 * 512
    END = SBUF_END


class At:

    def __init__(self, nc, at, end):
        self.nc, self.at, self.end = nc, at, end

    def __call__(self, name, shape, dtype=F32):
        size = {F32: 4, F32R: 4, BF16: 2, I32: 4, U32: 4}[dtype]
        for s in shape[1:]:
            size *= s
        t = self.nc.alloc_sbuf_tensor_at(name, shape, dtype, offset=self.at)
        self.at += (size + 31) // 32 * 32
        assert self.at <= self.end, (name, self.at, self.end)
        return t


class Sems:

    def __init__(self, nc, ctx, stage):
        self.nc, self.ctx, self.stage = nc, ctx, stage

    def __call__(self, name):
        return self.nc.alloc_semaphore(f"{self.stage}_{name}")


class Chain:

    def __init__(self, eng, sem):
        self.eng, self.sem, self.n = eng, sem, 0

    def link(self, ins):
        self.n += 1
        ins.then_inc(self.sem, 1)
        return self.n

    def sync(self, n=None):
        n = self.n if n is None else n
        if n > 0:
            self.eng.wait_ge(self.sem, n)


def after(eng, sem, n):
    if isinstance(n, int):
        if n > 0:
            eng.wait_ge(sem, n)
    else:
        eng.wait_ge(sem, n)


def chunks(n, size=512):
    return [(a, min(size, n - a)) for a in range(0, n, size)]


class Core:

    def __init__(self, nc, ins, outs):
        self.nc, self.i, self.o = nc, ins, outs
        self.ps = nc.alloc_psum_tensor("ps", [128, 8, 512], F32)
        c = At(nc, Map.C, Map.R2)
        self.cbuf = c("constants", [128, CONST_W])
        self.c = {name: self.cbuf[:, at:at + width] for name, (at, width) in CONSTS.items()}
        self.conv = c("conv_w_and_states", [128, CB, 19])
        self.fconv = c("ffn_conv_w_and_states", [128, FB, 19])
        self.gains = c("gains", [128, KB, 3])
        self.eps = c("eps", [128, 1])
        self.place = c("place_bf16", [128, 2, 128], BF16)
        self.identb = c("ident_bf16", [128, 128], BF16)
        self.rows = c("gather_rows", [128, NB * NGRP], U32)
        self.wi = c("index_weights", [128, NT, NIH])
        self.wsel = c("index_weights_placed", [128, 2, 2, NS])
        self.x = nc.alloc_sbuf_tensor_at("xt", [128, KB, TW], F32, offset=Map.R0)
        self.ah = nc.alloc_sbuf_tensor_at("act_hi", [128, KB, TW], F32R, offset=Map.R1)
        self.al = nc.alloc_sbuf_tensor_at("act_lo", [128, KB, TW], F32R, offset=Map.R1 + KB * TW * 4)
        w = At(nc, Map.W, Map.C)
        self.wr = [w(f"w_raw{s}", [128, 1024]) for s in range(3)]
        self.wh = [w(f"w_hi{s}", [128, 1024], F32R) for s in range(3)]
        self.wl = [w(f"w_lo{s}", [128, 1024], F32R) for s in range(3)]
        x = At(nc, Map.R0, Map.R1)
        self.kit = x("index_keys", [128, TW])
        self.qit = x("index_queries", [128, 2, TW])
        self.qis = nc.alloc_sbuf_tensor_at("index_queries_samples", [128, NIH, NS], F32, offset=Map.R1 - 4096)
        self.qibd = nc.alloc_sbuf_tensor_at("index_queries_diagonal", [128, NB, 32], F32, offset=Map.R1 - 3072)
        self.wis = nc.alloc_sbuf_tensor_at("index_weights_samples", [NS, NIH], F32, offset=Map.R1 - 2048)
        self.wrow = nc.alloc_sbuf_tensor_at("index_weights_rows", [128, 2], F32, offset=Map.R1 - 1024)
        self.wrow4 = nc.alloc_sbuf_tensor_at("index_weights_rows4", [128, 2, 4], F32, offset=Map.R1 - 1024 + 32)
        self.xsave = nc.dram_tensor("x_save", [128, KB * TW], F32)
        self.mixb = nc.dram_tensor("mix_b", [KB, 128, TW], F32)
        self.siga = nc.dram_tensor("sig_a", [KB, 128, TW], F32)

    def acc(self, s):
        return self.ps[:, 3 * s:3 * s + 3, 0:CH]

    def onerow(self, rows, n):
        return self.c["ones"][0:rows, 0:1].broadcast_to([rows, n])

    def flat(self, bank, n, rows=128):
        return self.ps[:].rearrange("p b c -> p (b c)")[0:rows, 512 * bank:512 * bank + n]


def tri(ap):
    return ap.rearrange("p (c n) -> p c n", c=3)


def split_product(pe, core, out_set, kblocks, wh, wl, bh, bl):
    last = None
    for k in range(kblocks):
        for n, (w, b) in enumerate(((wh, bh), (wh, bl), (wl, bh))):
            for c in range(3):
                last = pe.matmul(core.acc(out_set)[:, c, :], w(k), b(k)[:, c * CH:(c + 1) * CH],
                                 start=(k == 0 and n == 0), stop=(k == kblocks - 1 and n == 2))
    return last


def weight_block(t, k, m=128):
    return t[:, k * m:(k + 1) * m]


def constants():
    p = np.arange(128)
    c = {"ident": np.eye(128), "ones": np.ones((128, 128))}
    half = HD // 8
    perm = np.zeros((128, 128))
    for i in p:
        if i % HD < half:
            perm[i + half, i] = -1
        elif i % HD < 2 * half:
            perm[i - half, i] = 1
    c["perm"] = perm
    same = (p[:, None] % NS) == (p[None, :] % NS)
    c["fold"] = same
    c["below"] = same & (p[:, None] < p[None, :])
    place = np.zeros((128, 2, 128))
    owner = np.zeros((128, 2, 2, NS))
    for r in p:
        b4, par, t = r // 32, r // 16 % 2, r % 4
        for sg in range(2):
            token = (sg * 4 + b4) * DS + t
            place[token::NS, sg, r] = 1
            owner[r, sg, par, token] = 1
    c["place"], c["owner"] = place.reshape(128, 256), owner.reshape(128, 128)
    c["head"] = (p[:, None] // 4 % 4) == np.arange(4)[None, :]
    token, key = p[:, None] % NS, np.arange(NS)[None, :]
    keep = (p[:, None] >= 96) & (token // DS == key // DS) & (key % DS <= token % DS)
    c["newkeep"], c["newfill"] = keep, np.where(keep, 0.0, NEG)
    c["lane"] = p[:, None] % 32
    c["bit"] = np.full((128, 1), 2.0)
    pos = np.zeros(TW, np.float32)
    pos[:TP] = np.arange(TP)
    pos[TP:TOK] = PAST + np.arange(NS) % DS
    rot = HD // 4
    inv = np.power(500000.0, -np.arange(half) * 2.0 / rot).astype(np.float32)
    ang = pos[:, None] * inv[None, :]
    cos, sin = np.ones((128, TW)), np.zeros((128, TW))
    for i in p:
        if i % HD < rot:
            cos[i] = np.cos(ang[:, i % half])
            sin[i] = np.sin(ang[:, i % half])
    c["cos"], c["sin"] = cos, sin
    return np.concatenate([np.asarray(c[n], np.float32) for n in CONSTS], 1)


def x_rows(ins, t):
    xp = ins["x_prompt"][0]
    if t == 0:
        return [((0, META), ins["meta_tokens"]), ((META, 128), xp[0:128 - META])]
    if t < NT - 1:
        return [((0, 128), xp[128 * t - META:128 * (t + 1) - META])]
    own = QROWS[-1]
    return [((0, own), xp[SEQ - own:SEQ]), ((own, own + NS), ins["x_sample"].rearrange("b s d -> (b s) d"))]


def load_stage(nc, core):
    r2 = At(nc, Map.R2, Map.END)
    rows = [r2(f"x_rows{s}", [128, D]) for s in range(3)]
    conv_rows = r2("conv_rows", [19, CD])
    fconv_rows = r2("ffn_conv_rows", [19, FF])
    gain_rows = r2("gain_rows", [3, D])
    with ExitStack() as ctx:
        sem = Sems(nc, ctx, "ld")
        consts_in, small_in = sem("consts_in"), sem("small_in")
        x_in = [sem(f"x_in{s}") for s in range(3)]
        turned, small_turned, copied, zeroed = sem("turned"), sem("small_turned"), sem("copied"), sem("zeroed")
        saved, small_copied = sem("saved"), sem("small_copied")
        ins = core.i
        parts = [len(x_rows(ins, t)) for t in range(NT)]
        x_count = [16 * sum(parts[t % 3:t + 1:3]) for t in range(NT)]
        ident = core.c["ident"]
        with nc.Block() as block:

            @block.sync
            def _(sp):
                sp.dma_start(core.cbuf[:], ins["constants"]).then_inc(consts_in, 16)
                for t in range(NT):
                    if t >= 3:
                        sp.wait_ge(turned, t - 2)
                    for (a, b), src in x_rows(ins, t):
                        sp.dma_start(rows[t % 3][a:b, :], src).then_inc(x_in[t % 3], 16)
                sp.wait_ge(copied, NT)
                sp.wait_ge(zeroed, 1)
                sp.dma_start(core.xsave.ap(), core.x[:].rearrange("p k t -> p (k t)")).then_inc(saved, 16)
                sp.wait_ge(saved, 16)

            @block.scalar
            def _(act):
                for dst, src in (
                    (conv_rows[0:16, :], ins["state_conv"][0].rearrange("b w c -> (b w) c")),
                    (conv_rows[16:19, :], ins["conv_w"][0]),
                    (fconv_rows[0:16, :], ins["state_ffn_conv"][0].rearrange("b w c -> (b w) c")),
                    (fconv_rows[16:19, :], ins["ffn_conv_w"][0]),
                    (gain_rows[0:1, :], ins["norm1"]), (gain_rows[1:2, :], ins["norm2"]),
                    (gain_rows[2:3, :], ins["norm_final"].rearrange("(a d) -> a d", a=1)),
                ):
                    act.dma_start(dst, src).then_inc(small_in, 16)
                act.wait_ge(small_turned, 1)
                act.activation(core.conv[:], core.flat(6, CB * 19).rearrange("p (k r) -> p k r", r=19),
                               ACT.Copy).then_inc(small_copied, 1)
                act.activation(core.gains[:], core.flat(6, 200)[:, 100:100 + 3 * KB].rearrange("p (k r) -> p k r", r=3),
                               ACT.Copy).then_inc(small_copied, 1)
                act.activation(core.fconv[:], core.flat(7, FB * 19).rearrange("p (k r) -> p k r", r=19),
                               ACT.Copy).then_inc(small_copied, 1)
                act.wait_ge(consts_in, 16)
                act.mul(core.identb[:], core.c["ident"], BIG)
                act.mul(core.place[:].rearrange("p s r -> p (s r)"), core.c["place"], BIG)

            @block.tensor
            def _(pe):
                pe.wait_ge(consts_in, 16)
                pe.wait_ge(small_in, 16 * 7)
                for k in range(CB):
                    pe.transpose(core.flat(6, CB * 19)[:, 19 * k:19 * k + 19], conv_rows[:, 128 * k:128 * k + 128],
                                 ident[0:19, 0:19])
                for k in range(KB):
                    pe.transpose(core.flat(6, 200)[:, 100 + 3 * k:103 + 3 * k], gain_rows[:, 128 * k:128 * k + 128],
                                 ident[0:3, 0:3])
                for k in range(FB):
                    last = pe.transpose(core.flat(7, FB * 19)[:, 19 * k:19 * k + 19],
                                        fconv_rows[:, 128 * k:128 * k + 128], ident[0:19, 0:19])
                last.then_inc(small_turned, 1)
                for t in range(NT):
                    n = ROWS[t]
                    pe.wait_ge(x_in[t % 3], x_count[t])
                    if t >= 3:
                        pe.wait_ge(copied, t - 2)
                    for k in range(KB):
                        last = pe.transpose(core.flat(2 * (t % 3), 1024)[:, 128 * k:128 * k + n],
                                            rows[t % 3][0:n, 128 * k:128 * k + 128], ident[0:n, 0:n])
                    last.then_inc(turned, 1)

            @block.vector
            def _(dve):
                dve.memset(core.eps[:], EPS)
                dve.memset(core.x[:, :, TOK:TW], 0.0).then_inc(zeroed, 1)
                for t in range(NT):
                    dve.wait_ge(turned, t + 1)
                    src = core.flat(2 * (t % 3), 1024).rearrange("p (k n) -> p k n", k=KB)
                    dve.tensor_copy(core.x[:, :, 128 * t:128 * t + ROWS[t]], src[:, :, 0:ROWS[t]]).then_inc(copied, 1)


def norm_stage(nc, core, which, name, split=True):
    if not split:
        core.y = nc.alloc_sbuf_tensor_at("y", [128, KB, TW], F32, offset=Map.R1)
    normed = core.ah if split else core.y
    r2 = At(nc, Map.R2, Map.END)
    sq = [r2(f"{name}_sq{s}", [128, TW]) for s in range(2)]
    total = r2(f"{name}_total", [128, TW])
    mean = r2(f"{name}_mean", [128, TW])
    root = r2(f"{name}_root", [128, TW])
    fix = r2(f"{name}_fix", [128, TW])
    scale = r2(f"{name}_scale", [128, TW])
    y = [r2(f"{name}_y{s}", [128, TW]) for s in range(2)]
    with ExitStack() as ctx:
        sem = Sems(nc, ctx, name)
        squared, added, summed = sem("squared"), sem("added"), sem("summed")
        rooted, scaled, scale_ok = sem("rooted"), sem("scaled"), sem("scale_ok")
        hi, lo, own = sem("hi"), sem("lo"), sem("own")
        with nc.Block() as block:

            @block.scalar
            def _(act):
                for k in range(KB):
                    if k >= 2:
                        act.wait_ge(added, k - 1)
                    act.activation(sq[k % 2][:], core.x[:, k, :], ACT.Square).then_inc(squared, 1)
                act.wait_ge(own, 1)
                act.activation(root[:], mean[:], ACT.Sqrt).then_inc(rooted, 1)
                for k in range(KB):
                    act.wait_ge(scaled, k + 1)
                    act.mul(normed[:, k, :], y[k % 2][:], core.gains[:, k, which:which + 1]).then_inc(hi, 1)

            @block.vector
            def _(dve):
                for k in range(KB):
                    dve.wait_ge(squared, k + 1)
                    if k == 0:
                        dve.tensor_copy(total[:], sq[0][:]).then_inc(added, 1)
                    else:
                        dve.wait_ge(added, k)
                        dve.tensor_tensor(total[:], total[:], sq[k % 2][:], ALU.add).then_inc(added, 1)
                chain = Chain(dve, own)
                dve.wait_ge(summed, 1)
                chain.link(dve.tensor_scalar(tri(mean[:]), core.acc(0), 1.0 / D, EPS, ALU.mult, ALU.add))
                dve.wait_ge(rooted, 1)
                chain.link(dve.reciprocal(scale[:], root[:]))
                chain.sync()
                chain.link(dve.tensor_tensor(fix[:], scale[:], scale[:], ALU.mult))
                chain.sync()
                chain.link(dve.scalar_tensor_tensor(fix[:], mean[:], -0.5, fix[:], ALU.mult, ALU.mult))
                chain.sync()
                dve.scalar_tensor_tensor(scale[:], fix[:], 1.5, scale[:], ALU.add, ALU.mult).then_inc(scale_ok, 1)
                for k in range(KB if split else 0):
                    dve.wait_ge(scaled, k + 1)
                    dve.wait_ge(hi, k + 1)
                    dve.scalar_tensor_tensor(core.al[:, k, :], y[k % 2][:], core.gains[:, k, which:which + 1],
                                             core.ah[:, k, :].bitcast(F32), ALU.mult, ALU.subtract).then_inc(lo, 1)

            @block.gpsimd
            def _(pool):
                pool.wait_ge(scale_ok, 1)
                for k in range(KB):
                    if k >= 2:
                        pool.wait_ge(lo if split else hi, k - 1)
                    pool.tensor_tensor(y[k % 2][:], core.x[:, k, :], scale[:], ALU.mult).then_inc(scaled, 1)

            @block.tensor
            def _(pe):
                pe.wait_ge(added, KB)
                for c in range(3):
                    last = pe.matmul(core.acc(0)[:, c, :], core.c["ones"], total[:, c * CH:(c + 1) * CH],
                                     start=True, stop=True)
                last.then_inc(summed, 1)


class Weights:

    def __init__(self, core, sem, free, start=0):
        self.core, self.free, self.start = core, free, start
        self.arrived = [sem(f"w_arrived{s}") for s in range(3)]
        self.hi_done, self.lo_done = sem("w_hi"), sem("w_lo")
        self.pieces = [0, 0, 0]

    def fetch(self, sp, n, slot, pieces):
        after(sp, self.lo_done, n - 2)
        for (a, b, m), src in pieces:
            dst = self.core.wr[slot][:, a:b].rearrange("p (k m) -> p k m", m=m)
            sp.dma_start(dst, src).then_inc(self.arrived[slot], 16)

    def hi(self, act, n, slot, arrived, used, width=1024):
        act.wait_ge(self.arrived[slot], arrived)
        after(act, used, self.free(n))
        act.activation(self.core.wh[slot][:, 0:width], self.core.wr[slot][:, 0:width], ACT.Copy)\
            .then_inc(self.hi_done, 1)

    def lo(self, eng, n, slot, width=1024):
        eng.wait_ge(self.hi_done, n + 1)
        eng.tensor_tensor(self.core.wl[slot][:, 0:width], self.core.wr[slot][:, 0:width],
                          self.core.wh[slot][:, 0:width].bitcast(F32), ALU.subtract).then_inc(self.lo_done, 1)

    def product(self, pe, n, slot, out_set, kblocks=KB, bh=None, bl=None, m=128, at=0):
        core = self.core
        pe.wait_ge(self.lo_done, n + 1)
        bh = bh or (lambda k: core.ah[:, k, :])
        bl = bl or (lambda k: core.al[:, k, :])
        return split_product(pe, core, out_set, kblocks,
                             lambda k: core.wh[slot][:, at + k * m:at + (k + 1) * m],
                             lambda k: core.wl[slot][:, at + k * m:at + (k + 1) * m], bh, bl)


def by_rows(w, cols):
    return w.rearrange("(k p) c -> p k c", p=128)[:, :, cols]


class Heads:

    def __init__(self, nc):
        a = At(nc, Map.R2, Map.END)
        self.s = a("scores", [128, SW])
        self.ss = a("sample_scores", [128, SSW])
        b = At(nc, Map.R2, Map.END)
        self.q = b("q", [128, G, TW])
        self.k = b("k", [128, TW])
        self.v = b("v", [128, NT, 128])
        self.vs = b("v_samples", [NS, 128])
        assert b.at <= a.at + 4096
        c = At(nc, max(a.at, b.at), Map.END)
        self.mask = c("mask", [128, MW], BF16)
        self.smask = c("sample_mask", [128, SSW], BF16)
        self.qs = c("q_samples", [128, NB, 32])
        self.end = c.at
        d = At(nc, Map.R2 + 26624, Map.END)
        self.row = [d(f"row{u}", [128, TW + 2]) for u in range(6)]
        self.junk = d("count_junk", [128, SSW], BF16)
        self.count = d("count", [128, NSEL])
        self.kth = d("kth", [128, NSEL], I32)
        self.cand = d("candidate", [128, NSEL], I32)
        self.bit = d("bit", [128, 1], I32)
        self.enough = d("enough", [128, NSEL])
        self.need = d("need", [128, NSEL])
        self.sign = d("sign", [128, NSEL])
        self.need0 = d("need0", [128, NSEL])
        self.need1 = d("need1", [128, NSEL])
        self.p6 = d("conv_samples", [128, NB, 6])
        self.cs = d("conv_states", [128, CB, 18])
        self.after_search = d.at
        self.bh = nc.alloc_sbuf_tensor_at("b_hi", [128, CB, TW], F32R, offset=Map.R0)
        self.raw = [nc.alloc_sbuf_tensor_at(f"raw_qkv{u}", [128, TW], F32, offset=Map.R0 + 4320 * u) for u in range(6)]
        self.bl = nc.alloc_sbuf_tensor_at("b_lo", [128, CB, TW], F32R, offset=Map.R0 + CB * TW * 4)

    def part(self, i):
        if i == NSEL - 1:
            return self.ss[:]
        qb = QB0 + i
        return self.s[0:QROWS[qb], SOFF[qb]:SOFF[qb] + NK[qb]]

    def rows(self, i):
        return 128 if i == NSEL - 1 else QROWS[QB0 + i]


def index_stage(nc, core, hd):
    r = At(nc, hd.end, Map.END)
    rot = [core.kit[:], core.qit[:, 0, :], core.qit[:, 1, :]]
    raw = [nc.alloc_sbuf_tensor_at(f"raw{u}", [128, TW], F32, offset=Map.R0 + 3 * 4320 + u * 4320) for u in range(3)]
    tmp = [nc.alloc_sbuf_tensor_at(f"rtmp{u}", [128, TW], F32, offset=Map.R0 + 6 * 4320 + u * 4320) for u in range(1)]
    relu = [r(f"relu{s}", [128, TP]) for s in range(2)]
    keys_out = r("keys_out", [128, NT, HD])
    with ExitStack() as ctx:
        sem = Sems(nc, ctx, "ix")
        acc_ready, raw_copied, acc_free_d = sem("acc_ready"), sem("raw_copied"), sem("acc_free_d")
        wi_copied = sem("wi_copied")
        cosined, roped, own = sem("cosined"), sem("roped"), sem("own")
        turned, keys_copied, stored = sem("turned"), sem("keys_copied"), sem("stored")
        scored, relued, summed, masked = sem("scored"), sem("relued"), sem("summed"), sem("masked")
        swapped = sem("swapped")
        w = Weights(core, sem, lambda n: n - 2)
        widths = [1024, 1024, 1024, 32]
        win = core.i["w_in"][0]
        blocks = range(QB0, NT)
        with nc.Block() as block:

            @block.sync
            def _(sp):
                ki = by_rows(win, slice(KIC, KIC + HD))
                for half in range(2):
                    dst = core.wr[0][:].rearrange("p (k m) -> p k m", m=128)[:, :, half * HD:(half + 1) * HD]
                    sp.dma_start(dst, ki).then_inc(w.arrived[0], 16)
                for j in range(2):
                    w.fetch(sp, 1 + j, 1 + j, [((0, 1024, 128), by_rows(win, slice(QIC + 128 * j, QIC + 128 * j + 128)))])
                w.fetch(sp, 3, 0, [((0, 32, 4), by_rows(win, slice(WIC, WIC + 4)))])
                sp.wait_ge(roped, 3)
                for j in range(2):
                    for half in range(2):
                        for to in range(2):
                            sp.dma_start(core.qis[64 * to:64 * to + 64, 2 * j + half, :],
                                         core.qit[64 * half:64 * half + 64, j, TP:TOK]).then_inc(swapped, 16)
                sp.wait_ge(keys_copied, 1)
                ko = keys_out
                sp.dma_start(core.o["kidx_prompt"][0, 0, 0:1024].rearrange("(t p) d -> p t d", p=128),
                             ko[:, 0:8, :]).then_inc(stored, 16)
                sp.dma_start(core.o["kidx_prompt"][0, 0, 1024:TP], ko[0:QROWS[8], 8, :]).then_inc(stored, 16)
                sp.dma_start(core.o["kidx_sample"][0].rearrange("b s d -> (b s) d"),
                             ko[QROWS[8]:ROWS[8], 8, :]).then_inc(stored, 16)
                sp.wait_ge(stored, 48)
                sp.wait_ge(swapped, 16 * 8)

            @block.tensor
            def _(pe):
                for u in range(3):
                    if u == 2:
                        pe.wait_ge(raw_copied, 1)
                    w.product(pe, u, u, u % 2).then_inc(acc_ready, 1)
                pe.wait_ge(w.lo_done, 4)
                for t in range(NT):
                    n = min(128, TW - 128 * t)
                    for k in range(KB):
                        for i, (b, x) in enumerate(((core.wh, core.ah), (core.wl, core.ah), (core.wh, core.al))):
                            last = pe.matmul(core.flat(6, 64, n)[:, 4 * t:4 * t + 4],
                                             x[:, k, 128 * t:128 * t + n], b[0][:, 4 * k:4 * k + 4],
                                             start=(k == 0 and i == 0), stop=(k == KB - 1 and i == 2))
                last.then_inc(acc_ready, 1)
                for k in range(KB):
                    for i, (b, x) in enumerate(((core.wh, core.ah), (core.wl, core.ah), (core.wh, core.al))):
                        last = pe.matmul(core.flat(7, 4, NS), x[:, k, TP:TOK], b[0][:, 4 * k:4 * k + 4],
                                         start=(k == 0 and i == 0), stop=(k == KB - 1 and i == 2))
                last.then_inc(acc_ready, 1)
                for u in range(3):
                    s = (u + 1) % 2
                    pe.wait_ge(raw_copied, min(u + 2, 3))
                    if u == 2:
                        pe.wait_ge(acc_free_d, 1)
                    for c in range(3):
                        last = pe.matmul(core.acc(s)[:, c, :], core.c["perm"], raw[u][:, c * CH:(c + 1) * CH],
                                         start=True, stop=True)
                    last.then_inc(acc_ready, 1)
                pe.wait_ge(roped, 1)
                pe.wait_ge(acc_free_d, 2)
                for t in range(NT):
                    last = pe.transpose(core.flat(0, NT * HD, ROWS[t])[:, HD * t:HD * t + HD] if t < 8 else
                                        core.flat(1, HD, ROWS[t]),
                                        core.kit[0:HD, 128 * t:128 * t + ROWS[t]], core.c["ident"][0:HD, 0:HD])
                last.then_inc(turned, 1)
                pe.wait_ge(wi_copied, 1)
                for sg in range(2):
                    last = pe.matmul(core.flat(7, 8)[:, 4 * sg:4 * sg + 4],
                                     core.c["place"].rearrange("p (s r) -> p s r", s=2)[0:NS, sg, :],
                                     core.wis[:], start=True, stop=True)
                last.then_inc(turned, 1)
                pe.wait_ge(roped, 3)
                pe.wait_ge(acc_free_d, 3)
                pe.wait_ge(keys_copied, 1)
                m = 0
                for qb in blocks:
                    n = QROWS[qb]
                    for h in range(NIH):
                        half = 64 * (h % 2)
                        after(pe, relued, m - 1)
                        for a, width in chunks(NK[qb]):
                            last = pe.matmul(core.flat(3 * (m % 2), TP, n)[:, a:a + width],
                                             core.qit[half:half + 64, h // 2, 128 * qb:128 * qb + n],
                                             core.kit[half:half + 64, a:a + width], start=True, stop=True)
                        last.then_inc(scored, 1)
                        m += 1

            @block.scalar
            def _(act):
                arrived = [32, 16, 16, 48]
                for n in range(4):
                    w.hi(act, n, n % 3, arrived[n], acc_ready, widths[n])
                    if n == 1:
                        act.wait_ge(acc_ready, 1)
                        act.activation(tri(raw[0][:]), core.acc(0), ACT.Copy).then_inc(raw_copied, 1)
                for u in (1, 2):
                    act.wait_ge(acc_ready, u + 1)
                    act.activation(tri(raw[u][:]), core.acc(u % 2), ACT.Copy).then_inc(raw_copied, 1)
                act.wait_ge(acc_ready, 4)
                scale = float((NIH * HD) ** -0.5)
                act.mul(core.wi[:, 0:8, :].rearrange("p t h -> p (t h)"), core.flat(6, 32), scale)
                act.wait_ge(acc_ready, 5)
                act.mul(core.wi[0:ROWS[8], 8, :], core.flat(6, 64, ROWS[8])[:, 32:36], scale)
                act.mul(core.wis[:], core.flat(7, 4, NS), scale).then_inc(wi_copied, 1)
                act.wait_ge(turned, 1)
                act.activation(keys_out[:, 0:8, :].rearrange("p t d -> p (t d)"), core.flat(0, 8 * HD), ACT.Copy)
                act.activation(keys_out[0:ROWS[8], 8, :], core.flat(1, HD, ROWS[8]), ACT.Copy).then_inc(keys_copied, 1)
                m = 0
                for qb in blocks:
                    for h in range(NIH):
                        act.wait_ge(scored, m + 1)
                        after(act, summed, m - 1)
                        act.activation(relu[m % 2][0:QROWS[qb], 0:NK[qb]], core.flat(3 * (m % 2), NK[qb], QROWS[qb]),
                                       ACT.Relu).then_inc(relued, 1)
                        m += 1

            @block.vector
            def _(dve):
                for n in range(4):
                    w.lo(dve, n, n % 3, widths[n])
                for u in range(3):
                    dve.wait_ge(acc_ready, 6 + u)
                    dve.wait_ge(cosined, u + 1)
                    dve.tensor_tensor(tri(tmp[0][:]), tri(core.c["sin"]), core.acc((u + 1) % 2), ALU.mult)\
                        .then_inc(acc_free_d, 1)
                    dve.wait_ge(acc_free_d, u + 1)
                    dve.tensor_tensor(rot[u], rot[u], tmp[0][:], ALU.add).then_inc(roped, 1)
                    dve.wait_ge(roped, u + 1)
                m = 0
                for qb in blocks:
                    n, k = QROWS[qb], NK[qb]
                    s = hd.s[0:n, SOFF[qb]:SOFF[qb] + k]
                    for h in range(NIH):
                        wi = core.wi[0:n, qb, h:h + 1]
                        dve.wait_ge(relued, m + 1)
                        if m == 0:
                            dve.wait_ge(wi_copied, 1)
                        if h == 0:
                            dve.tensor_scalar(s, relu[m % 2][0:n, 0:k], wi, None, ALU.mult).then_inc(summed, 1)
                        else:
                            dve.wait_ge(summed, m)
                            dve.scalar_tensor_tensor(s, relu[m % 2][0:n, 0:k], wi, s, ALU.mult, ALU.add)\
                                .then_inc(summed, 1)
                        m += 1
                dve.wait_ge(turned, 2)
                for sg in range(2):
                    dve.tensor_tensor_reduce(out=core.wrow4[:, sg, :], in0=core.c["head"], in1=core.flat(7, 8)[:, 4 * sg:4 * sg + 4],
                                             scale=1.0, scalar=0.0, op0=ALU.mult, op1=ALU.add,
                                             accum_out=core.wrow[:, sg:sg + 1]).then_inc(own, 1)
                dve.wait_ge(own, 2)
                owner = core.c["owner"].rearrange("p (s h n) -> p s h n", s=2, h=2)
                for sg in range(2):
                    dve.tensor_scalar(core.wsel[:, sg, :, :], owner[:, sg, :, :], core.wrow[:, sg:sg + 1], None, ALU.mult)
                dve.memset(core.qibd[:].rearrange("p b n -> p (b n)"), 0.0).then_inc(own, 1)
                dve.wait_ge(own, 3)
                dve.wait_ge(swapped, 16 * 8)
                for half in range(2):
                    p = slice(64 * half, 64 * half + 64)
                    dst = core.qibd[p, :, 16 * half:16 * half + 16].rearrange("p b (h t) -> p b h t", h=NIH)
                    for h in range(NIH):
                        dve.tensor_copy(dst[:, :, h, :], core.qis[p, h, :].rearrange("p (b t) -> p b t", t=DS))

            @block.gpsimd
            def _(pool):
                for u in range(3):
                    pool.wait_ge(raw_copied, u + 1)
                    pool.tensor_tensor(rot[u], raw[u][:], core.c["cos"], ALU.mult).then_inc(cosined, 1)
                for i, qb in enumerate(blocks):
                    n, k = QROWS[qb], NK[qb]
                    pool.wait_ge(summed, NIH * (i + 1))
                    s = hd.s[0:n, SOFF[qb] + 128 * qb:SOFF[qb] + k]
                    pool.affine_select(out=s, in_=s, compare_op=ALU.is_ge, fill=NEG, base=0,
                                       pattern=[[-1, k - 128 * qb]], channel_multiplier=1).then_inc(masked, 1)


def sample_index_stage(nc, core, hd):
    r = At(nc, hd.end, Map.END)
    ring = 8
    kx = [r(f"kidx{s}", [128, 4 * HD]) for s in range(ring)]
    relu = [r(f"sample_relu{s}", [128, 512]) for s in range(2)]
    pages = r("pages", [128, NB * NPAGES], I32)
    r0 = At(nc, Map.R0 + 4 * 4320, Map.R1 - 4096)
    kt = r0("kidx_turned", [128, NB, 256])
    new = r0("new_scores", [128, NS])
    src = core.i["cache_kidx"].rearrange("a n (s q) d -> (a n s) (q d)", q=4)
    with ExitStack() as ctx:
        sem = Sems(nc, ctx, "sx")
        pages_in, rows_ok = sem("pages_in"), sem("rows_ok")
        gathered = [sem(f"gathered{s}") for s in range(ring)]
        turned, copied_a, copied_d = sem("turned"), sem("copied_a"), sem("copied_d")
        scored, relued, summed, placed, own = sem("scored"), sem("relued"), sem("summed"), sem("placed"), sem("own")
        def weighted(pe, ch):
            pe.wait_ge(relued, ch + 1)
            if ch >= 2:
                pe.wait_ge(placed, ch - 1)
            g = ch // 2 if ch < NGRP else 3
            width, halves = (256, 2) if ch < NGRP else (NS, 1)
            for half in range(halves):
                for sg in range(2):
                    last = pe.matmul(core.flat(6 + ch % 2, 512)[32 * g:32 * g + 32, width * half:width * half + width],
                                     core.wsel[:, sg, half, :], relu[ch % 2][:, width * sg:width * sg + width],
                                     start=(sg == 0), stop=(sg == 1))
            last.then_inc(summed, 1)

        def place(dve, ch):
            dve.wait_ge(summed, ch + 1)
            g, c = ch // 2, ch % 2
            dst = hd.ss[32 * g:32 * g + 32, 512 * c:512 * c + 512].rearrange("t (p j a) -> t a j p", j=2, a=2)
            src_ps = core.flat(6 + ch % 2, 512)[32 * g:32 * g + 32, :].rearrange("t (a j p) -> t a j p", a=2, j=2)
            dve.tensor_copy(dst, src_ps).then_inc(placed, 1)

        with nc.Block() as block:

            @block.sync
            def _(sp):
                table = core.i["page_table"].rearrange("b n -> (b n)").rearrange("(a n) -> a n", a=1)
                sp.dma_start(pages[:], table.broadcast_to([128, NB * NPAGES])).then_inc(pages_in, 16)
                sp.wait_ge(pages_in, 16)

            @block.gpsimd
            def _(pool):
                pool.wait_ge(rows_ok, 1)
                n = 0
                for ch in range(NGRP):
                    for b in range(NB):
                        if n >= ring:
                            pool.wait_ge(turned, (n - ring) // 4 + 1)
                        pool.indirect_dma_start(
                            out=kx[b][:], out_offset=None, in_=src,
                            in_offset=bass.IndirectOffsetOnAxis(ap=core.rows[:, b * NGRP + ch:b * NGRP + ch + 1], axis=0),
                        ).then_inc(gathered[b], 16)
                        n += 1
                for b in range(NB):
                    pool.wait_ge(gathered[b], 16 * NGRP)

            @block.tensor
            def _(pe):
                for ch in range(NGRP + 1):
                    if ch >= 2:
                        pe.wait_ge(relued, ch - 1)
                    bank = 4 + ch % 2
                    if ch < NGRP:
                        for sg in range(2):
                            if ch >= 1:
                                pe.wait_ge((copied_a, copied_d)[sg], ch)
                            for b4 in range(4):
                                b = 4 * sg + b4
                                pe.wait_ge(gathered[b], 16 * (ch + 1))
                                for j in range(2):
                                    last = pe.transpose(core.flat(2 * sg, 1024)[:, 256 * b4 + 128 * j:256 * b4 + 128 * j + 128],
                                                        kx[b][:, 128 * j:128 * j + 128], core.c["ident"])
                            last.then_inc(turned, 1)
                        for sg in range(2):
                            pe.wait_ge((copied_a, copied_d)[sg], ch + 1)
                            for b4 in range(4):
                                last = pe.matmul(core.flat(bank, 512)[32 * b4:32 * b4 + 32, 256 * sg:256 * sg + 256],
                                                 core.qibd[:, 4 * sg + b4, :], kt[:, 4 * sg + b4, :], start=True, stop=True)
                    else:
                        for sg in range(2):
                            last = pe.matmul(core.flat(bank, 512)[:, NS * sg:NS * sg + NS],
                                             core.qibd[0:HD, 4 * sg:4 * sg + 4, :].rearrange("p b n -> p (b n)"),
                                             core.kit[0:HD, TP:TOK], start=True, stop=True)
                    last.then_inc(scored, 1)
                    if ch >= 1:
                        weighted(pe, ch - 1)
                weighted(pe, NGRP)

            @block.scalar
            def _(act):
                for ch in range(NGRP + 1):
                    if ch < NGRP:
                        act.wait_ge(turned, 2 * ch + 1)
                        if ch >= 1:
                            act.wait_ge(scored, ch)
                        act.activation(kt[:, 0:4, :].rearrange("p b n -> p (b n)"), core.flat(0, 1024), ACT.Copy)\
                            .then_inc(copied_a, 1)
                    act.wait_ge(scored, ch + 1)
                    if ch >= 2:
                        act.wait_ge(summed, ch - 1)
                    n = 512 if ch < NGRP else 2 * NS
                    act.activation(relu[ch % 2][:, 0:n], core.flat(4 + ch % 2, n), ACT.Relu).then_inc(relued, 1)

            @block.vector
            def _(dve):
                dve.wait_ge(pages_in, 16)
                table = pages[:].rearrange("p (m q) -> p m q", q=4)
                for q in range(4):
                    p = slice(32 * q, 32 * q + 32)
                    last = dve.tensor_scalar(core.rows[p, :], table[p, :, q], 32.0, core.c["lane"][p, :],
                                             ALU.mult, ALU.add)
                last.then_inc(rows_ok, 1)
                dve.memset(hd.ss[0:96, SQ:SSW], NEG)
                for ch in range(NGRP + 1):
                    if ch < NGRP:
                        dve.wait_ge(turned, 2 * ch + 2)
                        if ch >= 1:
                            dve.wait_ge(scored, ch)
                        dve.tensor_copy(kt[:, 4:8, :].rearrange("p b n -> p (b n)"), core.flat(2, 1024)).then_inc(copied_d, 1)
                    if ch >= 1:
                        place(dve, ch - 1)
                dve.wait_ge(summed, NGRP + 1)
                dve.tensor_tensor(new[96:128, :], core.c["newkeep"][96:128, :], core.flat(6, NS)[96:128, :], ALU.mult)\
                    .then_inc(own, 1)
                dve.wait_ge(own, 1)
                dve.tensor_tensor(hd.ss[96:128, SQ:SSW], new[96:128, :], core.c["newfill"][96:128, :], ALU.add)


class Search:

    LINKS = 5 + NSEL - 1

    def __init__(self, core, hd, dve, own, counted, folded):
        self.core, self.hd, self.dve = core, hd, dve
        self.own, self.counted, self.folded = own, counted, folded
        self.at = 0

    def link(self, ins):
        ins.then_inc(self.own, 1)
        self.at = self.at + 1

    def sync(self):
        self.dve.wait_ge(self.own, self.at)

    def count(self, value, nth, op=ALU.is_ge):
        hd = self.hd
        for i in [NSEL - 1, *range(NSEL - 1)]:
            n = hd.rows(i)
            part = hd.part(i)
            ins = self.dve.tensor_scalar(hd.junk[0:n, 0:part.shape[1]], part, value(i, n), None,
                                         op, ALU.add, accum_out=hd.count[0:n, i:i + 1])
            if i == NSEL - 1:
                ins.then_inc(self.counted, 1)
                self.dve.wait_ge(self.counted, nth)
            else:
                self.link(ins)
                self.sync()

    def judge(self, steps):
        hd, last = self.hd, NSEL - 1
        self.dve.wait_ge(self.folded, steps)
        self.sync()
        self.dve.tensor_tensor(hd.enough[:, 0:last], hd.count[:, 0:last], hd.need[:, 0:last], ALU.is_ge)
        self.link(self.dve.tensor_tensor(hd.enough[:, last:], self.core.flat(6, 1), hd.need[:, last:], ALU.is_ge))
        self.sync()

    def start(self):
        hd, dve = self.hd, self.dve
        dve.memset(hd.count[:], 0.0)
        dve.memset(hd.need[:], float(TOPK))
        for i in range(NSEL):
            w = 4 * SSW if i == NSEL - 1 else NK[QB0 + i]
            dve.memset(hd.need0[:, i:i + 1], float(w - TOPK + 1))
            dve.memset(hd.need1[:, i:i + 1], float(TOPK - (w - TOPK + 1)))
        dve.memset(hd.kth[:], 0)
        self.link(dve.tensor_copy(hd.bit[:].bitcast(F32), self.core.c["bit"]))
        self.sync()
        self.count(lambda i, n: 0.0, 1)
        self.judge(1)
        dve.tensor_scalar(hd.sign[:], hd.enough[:], 2.0, -1.0, ALU.mult, ALU.add)
        self.link(dve.tensor_tensor(hd.need[:], hd.enough[:], hd.need1[:], ALU.mult))
        self.sync()
        self.link(dve.tensor_tensor(hd.need[:], hd.need[:], hd.need0[:], ALU.add))
        self.signed()
        self.propose(2)

    def signed(self):
        for i in range(NSEL):
            part, n = self.hd.part(i), self.hd.rows(i)
            self.link(self.dve.tensor_scalar(part, part, self.hd.sign[0:n, i:i + 1], None, ALU.mult))
        self.sync()

    def propose(self, nth):
        hd = self.hd
        self.link(self.dve.tensor_scalar(hd.cand[:], hd.kth[:], hd.bit[:], None, ALU.bitwise_or))
        self.sync()
        self.count(lambda i, n: hd.cand[0:n, i:i + 1].bitcast(F32), nth)

    def settle(self, steps):
        hd = self.hd
        self.judge(steps)
        self.link(self.dve.tensor_scalar(hd.cand[:], hd.enough[:], -1.0, None, ALU.mult))
        self.sync()
        self.link(self.dve.scalar_tensor_tensor(hd.kth[:], hd.cand[:], hd.bit[:], hd.kth[:], ALU.bitwise_and, ALU.bitwise_or))
        self.sync()
        self.link(self.dve.tensor_scalar(hd.bit[:], hd.bit[:], 1, None, ALU.logical_shift_right))
        self.sync()

    def step(self, steps):
        self.settle(steps)
        self.propose(steps + 1)


SEARCH_A = [1, 3, 5, 7, 9, 11]


def gate_stage(nc, core, hd):
    cc, p, u, bf = (hd.row[x][:, 0:TW] for x in range(4))
    p = hd.row[1]
    sg = hd.row[4][:, 0:TW]
    mb = [hd.row[x][:, 0:TW] for x in (5, 0)]
    sa = [hd.row[x][:, 0:TW] for x in (2, 3)]
    eq, cum = hd.row[4], hd.row[5]
    sout = nc.alloc_sbuf_tensor_at("conv_states_out", [18, CD], F32, offset=Map.R1 - 2048)
    r = At(nc, hd.after_search, Map.END)
    above, equal = r("above", [128, NSEL]), r("equal", [128, NSEL])
    opened = r("opened", [128, 4])
    kthf, left = r("kth_signed", [128, NSEL]), r("left", [128, NSEL])
    with ExitStack() as ctx:
        sem = Sems(nc, ctx, "gt")
        ready, free_a, free_d = sem("acc_ready"), sem("acc_free_a"), sem("acc_free_d")
        own, counted, folded = sem("own"), sem("counted"), sem("folded")
        tapped, b_ok, b_hi, b_lo = sem("tapped"), sem("b_ok"), sem("b_hi"), sem("b_lo")
        cx_ok, conv_done, pads = sem("cx_ok"), sem("conv_done"), sem("pads")
        mix_stored = [sem(f"mix_stored{s}") for s in range(2)]
        sig_stored = [sem(f"sig_stored{s}") for s in range(2)]
        states_turned, states_copied, states_stored = sem("states_turned"), sem("states_copied"), sem("states_stored")
        q_first = sem("q_first")
        states_ok, tied, tie_sums, causal = sem("states_ok"), sem("tied"), sem("tie_sums"), sem("causal")
        w = Weights(core, sem, lambda n: n - 2)
        win, wpb = core.i["w_in"][0], core.i["w_pb"][0]
        A = 3 * CB
        B = A + 3 * KB
        first = [CCC, CXC, CBC]
        third = 2 + G
        pairs = KB // 2

        def masks(dve, find):
            find.link(dve.tensor_tensor(kthf[:], hd.kth[:].bitcast(F32), hd.sign[:], ALU.mult))
            find.signed()
            for s in range(2):
                dve.wait_ge(mix_stored[s], 16 * pairs + 1)
                dve.wait_ge(sig_stored[s], 16 * pairs + 1)
            dve.wait_ge(free_a, CB + 2 * KB)
            dve.memset(above[:], 0.0)
            find.link(dve.memset(equal[:], 0.0))
            find.sync()
            last = NSEL - 1
            for i in (last, *range(last)):
                part, n = hd.part(i), hd.rows(i)
                width = part.shape[1]
                e, s, kth = eq[0:n, 0:width], cum[0:n, 0:width], kthf[0:n, i:i + 1]
                dve.tensor_scalar(hd.junk[0:n, 0:width], part, kth, None, ALU.is_gt, ALU.add, accum_out=above[0:n, i:i + 1])
                ins = dve.tensor_scalar(e, part, kth, None, ALU.is_equal, ALU.add, accum_out=equal[0:n, i:i + 1])
                if i == last:
                    ins.then_inc(tied, 1)
                    dve.wait_ge(tied, 1)
                else:
                    find.link(ins)
                    find.sync()
                if i == last:
                    dve.wait_ge(tie_sums, 1)
                    find.link(dve.tensor_scalar(left[:, i:i + 1], core.flat(6, 2)[:, 0:1], -1.0, float(TOPK), ALU.mult, ALU.add))
                    find.sync()
                    find.link(dve.tensor_tensor(left[:, i:i + 1], left[:, i:i + 1], core.flat(6, 2)[:, 1:2], ALU.subtract))
                else:
                    find.link(dve.tensor_scalar(left[0:n, i:i + 1], above[0:n, i:i + 1], -1.0, float(TOPK), ALU.mult, ALU.add))
                find.link(dve.tensor_tensor_scan(s, core.onerow(n, width), e, 0.0, ALU.mult, ALU.add))
                find.sync()
                find.link(dve.scalar_tensor_tensor(s, s, left[0:n, i:i + 1], e, ALU.is_le, ALU.mult))
                find.sync()
                find.link(dve.scalar_tensor_tensor(s, part, kth, s, ALU.is_gt, ALU.add))
                find.sync()
                m = hd.smask[:] if i == last else hd.mask[0:n, MOFF[QB0 + i]:MOFF[QB0 + i] + width]
                find.link(dve.tensor_scalar(m, s, -1.0, None, ALU.add))
                find.sync()

        with nc.Block() as block:

            @block.sync
            def _(sp):
                for n in range(A):
                    col = first[n % 3] + 128 * (n // 3)
                    w.fetch(sp, n, n % 3, [((0, 1024, 128), by_rows(win, slice(col, col + 128)))])
                with sp.Fori(0, pairs) as i:
                    for part in range(6):
                        j, n = 2 * i + part // 3, A + 6 * i + part
                        col = 128 * j + (GBC, 0, GAC)[part % 3]
                        if part % 3 == 1:
                            col = (i + 1) * 256 + 128 * (part // 3) - 256
                            w.fetch(sp, n, 1, [((0, CB * 128, 128), by_rows(wpb, bass.ds(col, 128)))])
                        else:
                            w.fetch(sp, n, part % 3, [((0, 1024, 128), by_rows(win, bass.ds(col, 128)))])
                for m in range(2 + G):
                    n = B + m
                    if m < 2:
                        w.fetch(sp, n, n % 3, [((0, 1024, 128), by_rows(win, slice((KC, VC)[m], (KC, VC)[m] + 128)))])
                        continue
                    sp.wait_ge(w.lo_done, n - 2)
                    dst = core.wr[n % 3][:].rearrange("p (k v d) -> p k v d", k=KB, v=NKV)
                    for v in range(NKV):
                        head = QC + HD * (G * v + m - 2)
                        sp.dma_start(dst[:, :, v, :], by_rows(win, slice(head, head + HD)))\
                            .then_inc(w.arrived[n % 3] if v else q_first, 16)
                        if v == 0:
                            sp.wait_ge(q_first, 16 * (m - 1))
                sp.wait_ge(states_copied, 1)
                sp.dma_start(core.o["conv_prompt"][0, 0], sout[0:2, :]).then_inc(states_stored, 16)
                sp.dma_start(core.o["conv_sample"][0].rearrange("b w c -> (b w) c"), sout[2:18, :])\
                    .then_inc(states_stored, 16)
                sp.wait_ge(states_stored, 32)

            def fold(pe, n):
                pe.wait_ge(counted, n)
                pe.matmul(core.flat(6, 1), core.c["fold"], hd.count[:, NSEL - 1:NSEL], start=True, stop=True)\
                    .then_inc(folded, 1)

            @block.tensor
            def _(pe):
                folds = 1
                fold(pe, 1)
                for n in range(A):
                    if n >= 2:
                        c, k = divmod(n - 2, 3)
                        pe.wait_ge(*((free_a, c + 1) if k == 0 else (free_d, 2 * c + k)))
                    w.product(pe, n, n % 3, n % 2).then_inc(ready, 1)
                    if n == 1 or n - 2 in SEARCH_A:
                        folds += 1
                        fold(pe, folds)
                pe.wait_ge(b_lo, CB)
                assert folds == 7
                with pe.Fori(0, pairs) as i:
                    for part in range(6):
                        n = A + 6 * i + part
                        if part in (0, 3):
                            pe.wait_ge(free_d, 2 * CB + 2 * i + part // 3)
                        elif part == 1:
                            pe.wait_ge(free_a, CB + 4 * i)
                            pe.wait_ge(free_d, 2 * CB)
                        else:
                            pe.wait_ge(free_a, CB + 4 * i + {2: 1, 4: 2, 5: 3}[part])
                        if part % 3 == 1:
                            last = w.product(pe, n, 1, part % 2, CB, lambda k: hd.bh[:, k, :], lambda k: hd.bl[:, k, :])
                        else:
                            last = w.product(pe, n, part % 3, part % 2)
                        last.then_inc(ready, 1)
                        fold(pe, 8 + 6 * i + part)
                for m in range(third):
                    n = B + m
                    if m == 0:
                        pe.wait_ge(free_d, 2 * CB + KB)
                    else:
                        pe.wait_ge(free_a, CB + 2 * KB + m - 1)
                    w.product(pe, n, n % 3, n % 2).then_inc(ready, 1)
                    if m == 1:
                        fold(pe, 8 + 24)
                    if m == 2:
                        pe.wait_ge(tied, 1)
                        pe.matmul(core.flat(6, 2)[:, 0:1], core.c["fold"], above[:, NSEL - 1:NSEL], start=True, stop=True)
                        pe.matmul(core.flat(6, 2)[:, 1:2], core.c["below"], equal[:, NSEL - 1:NSEL], start=True, stop=True)\
                            .then_inc(tie_sums, 1)
                pe.wait_ge(states_ok, CB)
                for c in range(CB):
                    last = pe.transpose(core.flat(7, CD, 18)[:, 128 * c:128 * c + 128], hd.cs[:, c, :], core.c["ident"])
                last.then_inc(states_turned, 1)

            @block.scalar
            def _(act):
                for n in range(3):
                    w.hi(act, n, n, 16, ready)
                for n in range(A):
                    c, k = divmod(n, 3)
                    if k == 0:
                        act.wait_ge(ready, n + 1)
                        after(act, cx_ok, c)
                        act.activation(tri(cc), core.acc(n % 2), ACT.Copy).then_inc(free_a, 1)
                    if k == 2:
                        act.wait_ge(b_ok, c + 1)
                        act.activation(hd.bh[:, c, :], bf, ACT.Copy).then_inc(b_hi, 1)
                    w.hi(act, n + 3, n % 3, 16 * (n // 3 + 2), ready)
                act.wait_ge(b_lo, CB)
                with act.Fori(0, pairs) as i:
                    for part in range(6):
                        n, k, jj = A + 6 * i + part, part % 3, part // 3
                        if k == 0:
                            act.wait_ge(ready, n + 1)
                            act.wait_ge(free_d, 2 * CB + 2 * i + jj)
                            act.activation(tri(sg), core.acc(part % 2), ACT.Sigmoid).then_inc(free_a, 1)
                        if k == 2:
                            act.wait_ge(ready, n + 1)
                            act.wait_ge(sig_stored[jj], 16 * i + 1)
                            act.activation(tri(sa[jj]), core.acc(part % 2), ACT.Sigmoid).then_inc(free_a, 1)
                        w.hi(act, n + 3, k, 16 * (CB + 2 * i + jj + 2), ready)
                        row = act.snap(2 * i + jj)
                        if k == 1:
                            act.wait_ge(free_d, 2 * CB + 2 * i + jj + 1)
                            act.dma_start(core.mixb.ap()[bass.ds(row, 1)].rearrange("a p n -> p (a n)"), mb[jj])\
                                .then_inc(mix_stored[jj], 16)
                        if k == 2:
                            act.wait_ge(free_a, CB + 4 * i + 2 * jj + 2)
                            act.dma_start(core.siga.ap()[bass.ds(row, 1)].rearrange("a p n -> p (a n)"), sa[jj])\
                                .then_inc(sig_stored[jj], 16)
                for m in range(third):
                    n = B + m
                    act.wait_ge(ready, n + 1)
                    act.mul(tri(hd.raw[m][:]), core.acc(n % 2), 1.0 if m < 2 else SM).then_inc(free_a, 1)
                    if m + 3 < third:
                        w.hi(act, n + 3, n % 3, 16 * (B // 3 + 2), ready)
                act.wait_ge(states_turned, 1)
                act.activation(sout[:], core.flat(7, CD, 18), ACT.Copy).then_inc(states_copied, 1)

            @block.gpsimd
            def _(pool):
                pool.memset(p[:, 0:2], 0.0).then_inc(pads, 1)
                for x, stored in enumerate((*mix_stored, *sig_stored)):
                    pool.memset(opened[:, x:x + 1], 0.0).then_inc(stored, 1)
                for n in range(3):
                    w.lo(pool, n, n)
                for n in range(A):
                    c, k = divmod(n, 3)
                    if k == 1:
                        pool.wait_ge(cx_ok, c + 1)
                        after(pool, b_ok, c)
                        pool.tensor_scalar(u[:, 0:TP], p[:, 0:TP], core.conv[:, c, 16:17], None, ALU.mult)\
                            .then_inc(tapped, 1)
                    if k == 2:
                        pool.wait_ge(b_hi, c + 1)
                        pool.tensor_tensor(hd.bl[:, c, :], bf, hd.bh[:, c, :].bitcast(F32), ALU.subtract)\
                            .then_inc(b_lo, 1)
                    w.lo(pool, n + 3, n % 3)
                with pool.Fori(0, pairs) as i:
                    for part in range(6):
                        n, k, jj = A + 6 * i + part, part % 3, part // 3
                        w.lo(pool, n + 3, k)
                for m in range(3):
                    w.lo(pool, B + m + 3, m)
                for s in range(2):
                    pool.wait_ge(mix_stored[s], 16 * pairs + 1)
                    pool.wait_ge(sig_stored[s], 16 * pairs + 1)
                pool.memset(hd.mask[:, 0:MOFF[QB0]], 0.0).then_inc(causal, 1)
                pool.wait_ge(causal, 1)
                for qb in range(QB0):
                    at = MOFF[qb] + 128 * qb
                    last = pool.affine_select(out=hd.mask[:, at:at + 128], in_=hd.mask[:, at:at + 128], compare_op=ALU.is_ge,
                                              fill=-1.0, base=0, pattern=[[-1, 128]], channel_multiplier=1)
                last.then_inc(causal, 1)
                pool.wait_ge(causal, 2)

            @block.vector
            def _(dve):
                find = Search(core, hd, dve, own, counted, folded)
                find.start()
                steps = 1
                dve.wait_ge(pads, 1)
                for n in range(A):
                    c, k = divmod(n, 3)
                    if k == 1:
                        tap = [core.conv[:, c, 16 + x:17 + x] for x in range(3)]
                        dve.wait_ge(ready, n + 1)
                        dve.wait_ge(free_a, c + 1)
                        if c >= 1:
                            find.sync()
                        dve.tensor_tensor(tri(p[:, 2:2 + TW]), tri(cc), core.acc(n % 2), ALU.mult).then_inc(free_d, 1)
                        dve.wait_ge(free_d, 2 * c + 1)
                        dve.tensor_copy(hd.p6[:, :, 0:2], core.conv[:, c, 0:16].rearrange("p (b w) -> p b w", w=2))
                        dve.tensor_copy(hd.p6[:, :, 2:6], p[:, 2 + TP:2 + TOK].rearrange("p (b t) -> p b t", t=DS))\
                            .then_inc(cx_ok, 1)
                        dve.wait_ge(cx_ok, c + 1)
                        dve.tensor_copy(hd.cs[:, c, 0:2], p[:, TP:TP + 2])
                        dve.tensor_copy(hd.cs[:, c, 2:18].rearrange("p (b w) -> p b w", w=2), hd.p6[:, :, 4:6])\
                            .then_inc(states_ok, 1)
                        us = u[:, TP:TOK].rearrange("p (b t) -> p b t", t=DS)
                        if c == 0:
                            find.link(dve.memset(u[:, TOK:TW], 0.0))
                        find.link(dve.tensor_scalar(us, hd.p6[:, :, 0:4], tap[0], None, ALU.mult))
                        dve.wait_ge(tapped, c + 1)
                        for x in (1, 2):
                            find.sync()
                            dve.scalar_tensor_tensor(u[:, 0:TP], p[:, x:x + TP], tap[x], u[:, 0:TP], ALU.mult, ALU.add)
                            find.link(dve.scalar_tensor_tensor(us, hd.p6[:, :, x:x + 4], tap[x], us, ALU.mult, ALU.add))
                    if k == 2:
                        dve.wait_ge(ready, n + 1)
                        find.sync()
                        after(dve, b_lo, c)
                        dve.tensor_tensor(tri(bf), tri(u), core.acc(n % 2), ALU.mult).then_inc(free_d, 1)
                        dve.wait_ge(free_d, 2 * c + 2)
                        dve.tensor_copy(hd.p6[:, 0, 0:1], hd.p6[:, 0, 0:1]).then_inc(b_ok, 1)
                    if n in SEARCH_A:
                        steps += 1
                        find.step(steps)
                at0 = find.at
                with dve.Fori(0, pairs) as i:
                    find.at = at0 + 6 * Search.LINKS * i
                    for part in range(6):
                        n, k, jj = A + 6 * i + part, part % 3, part // 3
                        if k == 1:
                            dve.wait_ge(ready, n + 1)
                            dve.wait_ge(free_a, CB + 4 * i + 2 * jj + 1)
                            dve.wait_ge(mix_stored[jj], 16 * i + 1)
                            dve.tensor_tensor(tri(mb[jj]), tri(sg), core.acc(part % 2), ALU.mult).then_inc(free_d, 1)
                        find.step(8 + 6 * i + part)
                find.at = at0 + 6 * Search.LINKS * pairs
                find.settle(8 + 24)
                masks(dve, find)


def rope_stage(nc, core, hd):
    r1 = At(nc, Map.R1, Map.W)
    tmp = [r1(f"sined{u}", [128, TW]) for u in range(2)]
    k_out = r1("k_out", [128, NT, 128])
    s_out = r1("k_samples_out", [NS, 128])
    raw = [hd.raw[0], *hd.raw[2:]]
    dst = [hd.k[:], *(hd.q[:, g, :] for g in range(G))]
    count = len(raw)
    with ExitStack() as ctx:
        sem = Sems(nc, ctx, "ro")
        partner, sined, cosined, roped = sem("partner"), sem("sined"), sem("cosined"), sem("roped")
        v_turned, v_copied, k_turned, k_copied = sem("v_turned"), sem("v_copied"), sem("k_turned"), sem("k_copied")
        stored, zeroed = sem("stored"), sem("zeroed")

        def turn(pe, src, turned, copied, wait_first):
            for i in range(3):
                if i >= 2 or wait_first:
                    pe.wait_ge(copied, i - 1 if not wait_first else i + 2)
                if i < 2:
                    for t in range(4):
                        last = pe.transpose(core.flat(6 + i, 512)[:, 128 * t:128 * t + 128],
                                            src[:, 512 * i + 128 * t:512 * i + 128 * t + 128], core.c["ident"])
                else:
                    pe.transpose(core.flat(6, 128, ROWS[8]), src[:, 1024:TOK], core.c["ident"])
                    last = pe.transpose(core.flat(6, 256, NS)[:, 128:256], src[:, TP:TOK], core.c["ident"])
                last.then_inc(turned, 1)

        def untwist(act, turned, copied, dst, samples):
            for i in range(2):
                act.wait_ge(turned, i + 1)
                act.activation(dst[:, 4 * i:4 * i + 4, :].rearrange("p t d -> p (t d)"), core.flat(6 + i, 512), ACT.Copy)\
                    .then_inc(copied, 1)
            act.wait_ge(turned, 3)
            act.activation(dst[0:ROWS[8], 8, :], core.flat(6, 128, ROWS[8]), ACT.Copy)
            act.activation(samples, core.flat(6, 256, NS)[:, 128:256], ACT.Copy).then_inc(copied, 1)

        with nc.Block() as block:

            @block.tensor
            def _(pe):
                for u in range(count):
                    if u >= 2:
                        pe.wait_ge(sined, u - 1)
                    for c in range(3):
                        last = pe.matmul(core.acc(u % 2)[:, c, :], core.c["perm"], raw[u][:, c * CH:(c + 1) * CH],
                                         start=True, stop=True)
                    last.then_inc(partner, 1)
                turn(pe, hd.raw[1], v_turned, v_copied, False)
                pe.wait_ge(roped, 1)
                for i in range(3):
                    pe.wait_ge(v_copied, 3)
                    if i == 2:
                        pe.wait_ge(k_copied, 1)
                    if i < 2:
                        for t in range(4):
                            last = pe.transpose(core.flat(6 + i, 512)[:, 128 * t:128 * t + 128],
                                                hd.k[:, 512 * i + 128 * t:512 * i + 128 * t + 128], core.c["ident"])
                    else:
                        pe.transpose(core.flat(6, 128, ROWS[8]), hd.k[:, 1024:TOK], core.c["ident"])
                        last = pe.transpose(core.flat(6, 256, NS)[:, 128:256], hd.k[:, TP:TOK], core.c["ident"])
                    last.then_inc(k_turned, 1)

            @block.scalar
            def _(act):
                untwist(act, v_turned, v_copied, hd.v, hd.vs[:])
                untwist(act, k_turned, k_copied, k_out, s_out[:])

            @block.gpsimd
            def _(pool):
                for u in range(count):
                    pool.tensor_tensor(dst[u], raw[u][:], core.c["cos"], ALU.mult).then_inc(cosined, 1)

            @block.vector
            def _(dve):
                dve.memset(hd.qs[:].rearrange("p b n -> p (b n)"), 0.0).then_inc(zeroed, 1)
                for u in range(count):
                    dve.wait_ge(partner, u + 1)
                    if u >= 2:
                        dve.wait_ge(roped, u - 1)
                    dve.tensor_tensor(tri(tmp[u % 2][:]), tri(core.c["sin"]), core.acc(u % 2), ALU.mult).then_inc(sined, 1)
                    dve.wait_ge(cosined, u + 1)
                    dve.wait_ge(sined, u + 1)
                    dve.tensor_tensor(dst[u], dst[u], tmp[u % 2][:], ALU.add).then_inc(roped, 1)
                dve.wait_ge(zeroed, 1)
                dve.wait_ge(roped, count)
                for v in range(NKV):
                    p = slice(64 * v, 64 * v + 64)
                    for g in range(G):
                        at = 16 * v + 4 * g
                        dve.tensor_copy(hd.qs[p, :, at:at + 4], hd.q[p, g, TP:TOK].rearrange("p (b t) -> p b t", t=DS))

            @block.sync
            def _(sp):
                def store(out, rows, samples, copied):
                    sp.wait_ge(copied, 3)
                    prompt = core.o[f"{out}_prompt"][0, 0].rearrange("t v d -> t (v d)")
                    sp.dma_start(prompt[0:1024].rearrange("(t p) d -> p t d", p=128), rows[:, 0:8, :]).then_inc(stored, 16)
                    sp.dma_start(prompt[1024:TP], rows[0:QROWS[8], 8, :]).then_inc(stored, 16)
                    sp.dma_start(core.o[f"{out}_sample"][0].rearrange("b s v d -> (b s) (v d)"), samples)\
                        .then_inc(stored, 16)
                store("v", hd.v, hd.vs[:], v_copied)
                store("k", k_out, s_out[:], k_copied)
                sp.wait_ge(stored, 96)


def result_buffers(nc, core):
    core.rh = nc.alloc_sbuf_tensor_at("attention_hi", [128, G, TW], F32R, offset=Map.R0)
    core.rl = nc.alloc_sbuf_tensor_at("attention_lo", [128, G, TW], F32R, offset=Map.R0 + G * TW * 4)


def prompt_attention_stage(nc, core, hd):
    result_buffers(nc, core)
    r1 = At(nc, Map.R1, Map.W)
    probs = [r1(f"probs{s}", [128, TP]) for s in range(2)]
    turned_probs = [r1(f"probs_turned{s}", [128, NT, 128]) for s in range(2)]
    result = r1("result", [128, H * HD])
    top = [r1(f"minus_max{s}", [128, H]) for s in range(2)]
    sums = [r1(f"sums{s}", [128, H]) for s in range(2)]
    inv = r1("inverse_sums", [128, H])
    steps = NT * H
    ident = core.c["ident"]
    with ExitStack() as ctx:
        sem = Sems(nc, ctx, "pa")
        logits, maxed, probs_ok, turned = sem("logits"), sem("maxed"), sem("probs_ok"), sem("turned")
        copied, valued, inverted, normed = sem("copied"), sem("valued"), sem("inverted"), sem("normed")
        r_turned, r_hi, r_lo = sem("r_turned"), sem("r_hi"), sem("r_lo")

        def bank(i):
            return 0 if i // H == NT - 1 else 2 * (i % 2)

        def tbank(j):
            return 5 if j // H == NT - 1 else 4

        with nc.Block() as block:

            @block.tensor
            def _(pe):
                for i in range(steps + 3):
                    if i < steps:
                        qb, h = divmod(i, H)
                        g, v = divmod(h, NKV)
                        n, p = QROWS[qb], slice(64 * v, 64 * v + 64)
                        after(pe, probs_ok, i if qb == NT - 1 else i - 1)
                        for a, width in chunks(NK[qb]):
                            out = core.flat(bank(i), NK[qb], n)[:, a:a + width]
                            pe.matmul(out, core.identb[0:n, 0:n], hd.mask[0:n, MOFF[qb] + a:MOFF[qb] + a + width],
                                      start=True, stop=False)
                            last = pe.matmul(out, hd.q[p, g, 128 * qb:128 * qb + n], hd.k[p, a:a + width],
                                             start=False, stop=True)
                        last.then_inc(logits, 1)
                    if 0 <= i - 1 < steps:
                        j = i - 1
                        qb = j // H
                        n = QROWS[qb]
                        pe.wait_ge(probs_ok, j + 1)
                        after(pe, copied, j)
                        for k in range(qb + 1):
                            rows = min(128, NK[qb] - 128 * k)
                            last = pe.transpose(core.flat(tbank(j), n * (qb + 1), rows)[:, n * k:n * k + n],
                                                probs[j % 2][0:n, 128 * k:128 * k + rows], ident[0:n, 0:n])
                        last.then_inc(turned, 1)
                    if i >= 3 and (i - 3) % H == H - 1:
                        qb = (i - 3) // H
                        n = QROWS[qb]
                        pe.wait_ge(normed, qb + 1)
                        after(pe, r_lo, qb)
                        for g in range(G):
                            last = pe.transpose(core.flat(7, G * n)[:, n * g:n * g + n],
                                                result[0:n, 128 * g:128 * g + 128], ident[0:n, 0:n])
                        last.then_inc(r_turned, 1)
                    if 0 <= i - 2 < steps:
                        j = i - 2
                        qb, h = divmod(j, H)
                        n, v = QROWS[qb], h % NKV
                        pe.wait_ge(copied, j + 1)
                        after(pe, normed, qb)
                        for k in range(qb + 1):
                            rows = min(128, NK[qb] - 128 * k)
                            last = pe.matmul(core.flat(6, 512, n)[:, 64 * h:64 * h + 64],
                                             turned_probs[j % 2][0:rows, k, 0:n],
                                             hd.v[0:rows, k, 64 * v:64 * v + 64], start=(k == 0), stop=(k == qb))
                        last.then_inc(valued, 1)

            @block.scalar
            def _(act):
                for i in range(steps + 4):
                    if i < steps:
                        qb, h = divmod(i, H)
                        n, k = QROWS[qb], NK[qb]
                        act.wait_ge(maxed, i + 1)
                        after(act, turned, i - 1)
                        after(act, normed, qb - 1)
                        act.activation(probs[i % 2][0:n, 0:k], core.flat(bank(i), k, n), ACT.Exp,
                                       bias=top[qb % 2][0:n, h:h + 1],
                                       accum_out=sums[qb % 2][0:n, h:h + 1]).then_inc(probs_ok, 1)
                    if i >= 3 and (i - 3) % H == H - 1:
                        qb = (i - 3) // H
                        n = QROWS[qb]
                        act.wait_ge(r_turned, qb + 1)
                        act.activation(core.rh[:, :, 128 * qb:128 * qb + n],
                                       core.flat(7, G * n).rearrange("p (g n) -> p g n", g=G), ACT.Copy).then_inc(r_hi, 1)

            @block.vector
            def _(dve):
                for i in range(steps + 4):
                    if i < steps:
                        qb, h = divmod(i, H)
                        n, k = QROWS[qb], NK[qb]
                        dve.wait_ge(logits, i + 1)
                        dve.tensor_reduce(top[qb % 2][0:n, h:h + 1], core.flat(bank(i), k, n), AX.X, ALU.max, negate=True)\
                            .then_inc(maxed, 1)
                    if 0 <= i - 1 < steps:
                        j = i - 1
                        qb = j // H
                        n = QROWS[qb]
                        dve.wait_ge(turned, j + 1)
                        after(dve, valued, j - 1)
                        whole = NK[qb] // 128
                        src = core.flat(tbank(j), n * (qb + 1)).rearrange("p (k n) -> p k n", n=n)
                        ins = dve.tensor_copy(turned_probs[j % 2][:, 0:whole, 0:n], src[:, 0:whole, :])
                        if whole <= qb:
                            rows = NK[qb] - 128 * whole
                            ins = dve.tensor_copy(turned_probs[j % 2][0:rows, whole, 0:n], src[0:rows, whole, :])
                        ins.then_inc(copied, 1)
                    if i >= 3 and (i - 3) % H == H - 1:
                        qb = (i - 3) // H
                        n = QROWS[qb]
                        dve.wait_ge(valued, H * (qb + 1))
                        dve.wait_ge(probs_ok, H * (qb + 1))
                        dve.reciprocal(inv[0:n, :], sums[qb % 2][0:n, :]).then_inc(inverted, 1)
                        dve.wait_ge(inverted, qb + 1)
                        after(dve, r_turned, qb)
                        dve.tensor_tensor(result[0:n, :].rearrange("p (h d) -> p h d", h=H),
                                          core.flat(6, 512, n).rearrange("p (h d) -> p h d", h=H),
                                          inv[0:n, :].rearrange("p (h d) -> p h d", d=1).broadcast_to([n, H, HD]), ALU.mult)\
                            .then_inc(normed, 1)
                        dve.wait_ge(r_hi, qb + 1)
                        dve.tensor_tensor(core.rl[:, :, 128 * qb:128 * qb + n],
                                          core.flat(7, G * n).rearrange("p (g n) -> p g n", g=G),
                                          core.rh[:, :, 128 * qb:128 * qb + n].bitcast(F32), ALU.subtract).then_inc(r_lo, 1)


def sample_attention_stage(nc, core, hd):
    r1 = At(nc, Map.R1, Map.W)
    ring = 8
    got = [r1(f"gathered_kv{s}", [128, 4 * 128]) for s in range(ring)]
    kt = r1("keys_turned", [128, 4, GRP])
    probs0 = r1("sample_probs0", [128, PAST + NS])
    probs1 = r1("sample_probs1", [128, PAST + NS])
    probs = [probs0, probs1]
    pt_new = r1("new_probs_turned", [NS, 128])
    r2 = At(nc, hd.end, Map.END)
    pt = [r2(f"sample_probs_turned{s}", [128, 4, 128]) for s in range(2)]
    tops = r2("sample_maxima", [128, 2, NGRP + 1])
    top = r2("sample_top", [128, 2])
    sums = r2("sample_sums", [128, 2])
    inv = r2("sample_inverse", [128, 2])
    assert Map.W >= r1.at
    keys = core.i["cache_k"].rearrange("a n (s q) v d -> (a n s) (q v d)", q=4)
    values = core.i["cache_v"].rearrange("a n (s q) v d -> (a n s) (q v d)", q=4)
    rounds = 2 * NGRP
    items = NGRP + 1
    ident = core.c["ident"]
    place = core.place[:]
    with ExitStack() as ctx:
        sem = Sems(nc, ctx, "sa")
        gathered = [sem(f"gathered{s}") for s in range(ring)]
        turned, copied_a, copied_d = sem("keys_turned"), sem("copied_a"), sem("copied_d")
        logits, kept, maxed, topped = sem("logits"), sem("kept"), sem("maxed"), sem("topped")
        exped, inverted, normed = sem("exped"), sem("inverted"), sem("normed")
        p_turned, p_copied, valued = sem("probs_turned"), sem("probs_copied"), sem("valued")
        r_hi, r_lo, own = sem("r_hi"), sem("r_lo"), sem("own")
        padded = sem("padded")

        def value_item(r):
            return r // NGRP * items + r % NGRP

        def diagonal(result, sg, v):
            p = slice(64 * v, 64 * v + 64)
            src = core.flat(7 - 2 * sg, 128)[p, :].rearrange("p (b v g t) -> p v g b t", b=4, v=NKV, g=G)[:, v]
            at = TP + 16 * sg
            return result[p, :, at:at + 16].rearrange("p g (b t) -> p g b t", t=DS), src

        with nc.Block() as block:

            @block.gpsimd
            def _(pool):
                pool.memset(core.rh[:, :, TOK:TW].bitcast(F32), 0.0)
                pool.memset(core.rl[:, :, TOK:TW].bitcast(F32), 0.0).then_inc(padded, 1)
                for r in range(2 * rounds):
                    for b4 in range(4):
                        slot = 4 * (r % 2) + b4
                        sg, grp = r % rounds // NGRP, r % NGRP
                        if r >= 2:
                            if r - 2 < rounds:
                                pool.wait_ge(turned, 2 * (r - 2) + 1 + b4 // 2)
                            else:
                                pool.wait_ge(valued, value_item(r - 2 - rounds) + 1)
                        at = (4 * sg + b4) * NGRP + grp
                        pool.indirect_dma_start(
                            out=got[slot][:], out_offset=None, in_=keys if r < rounds else values,
                            in_offset=bass.IndirectOffsetOnAxis(ap=core.rows[:, at:at + 1], axis=0),
                        ).then_inc(gathered[slot], 16)
                for slot in range(ring):
                    pool.wait_ge(gathered[slot], 16 * rounds)
                pool.wait_ge(padded, 1)

            @block.tensor
            def _(pe):
                for sg in range(2):
                    out = core.flat(6, 512)[:, NS * sg:NS * sg + NS]
                    pe.matmul(out, place[96:128, sg, :], hd.smask[96:128, SQ:SSW], start=True, stop=False,
                              tile_position=(96, 0))
                    for b4 in range(4):
                        last = pe.matmul(out[32 * b4:32 * b4 + 32, :], hd.qs[:, 4 * sg + b4, :], hd.k[:, TP:TOK],
                                         start=False, stop=True)
                last.then_inc(logits, 1)
                for r in range(rounds + 1):
                    if r < rounds:
                        for b4 in range(4):
                            slot = 4 * (r % 2) + b4
                            if b4 % 2 == 0:
                                after(pe, (copied_a, copied_d)[b4 // 2], r)
                            pe.wait_ge(gathered[slot], 16 * (r // 2 + 1))
                            for s in range(4):
                                last = pe.transpose(core.flat(b4, 512)[:, 128 * s:128 * s + 128],
                                                    got[slot][:, 128 * s:128 * s + 128], ident)
                            if b4 % 2:
                                last.then_inc(turned, 1)
                    if r >= 1:
                        j = r - 1
                        sg, grp = divmod(j, NGRP)
                        q, at = 32 * (grp // 2), grp % 2 * 512
                        pe.wait_ge(copied_a, j + 1)
                        pe.wait_ge(copied_d, j + 1)
                        after(pe, kept, j if j >= 2 else 0)
                        out = core.flat(4 + j % 2, 512)
                        order = hd.smask[q:q + 32, at:at + 512].rearrange("t (p s) -> t s p", s=4)
                        pe.matmul(out, place[q:q + 32, sg, :], order, start=True, stop=False, tile_position=(q, 0))
                        for b4 in range(4):
                            last = pe.matmul(out[32 * b4:32 * b4 + 32, :], hd.qs[:, 4 * sg + b4, :], kt[:, b4, :],
                                             start=False, stop=True)
                        last.then_inc(logits, 1)
                for n in range(2 * items + 1):
                    if n < 2 * items:
                        sg, grp = divmod(n, items)
                        bank = 6 if n % 2 else 4
                        if n < 2:
                            pe.wait_ge(kept, rounds + 1)
                        pe.wait_ge(normed, sg + 1)
                        after(pe, p_copied, n - 1)
                        if grp < NGRP:
                            for s in range(4):
                                at = GRP * grp + 128 * s
                                last = pe.transpose(core.flat(bank, 512)[:, 128 * s:128 * s + 128],
                                                    probs[sg][:, at:at + 128], ident)
                        else:
                            last = pe.transpose(core.flat(bank, 128, NS), probs[sg][:, PAST:PAST + NS], ident)
                        last.then_inc(p_turned, 1)
                    if n >= 1:
                        j = n - 1
                        sg, grp = divmod(j, items)
                        out = core.flat(7 - 2 * sg, 128)
                        pe.wait_ge(p_copied, j + 1)
                        if grp < NGRP:
                            r = rounds + sg * NGRP + grp
                            for b4 in range(4):
                                slot = 4 * (r % 2) + b4
                                pe.wait_ge(gathered[slot], 16 * (r // 2 + 1))
                                for s in range(4):
                                    last = pe.matmul(out[:, 32 * b4:32 * b4 + 32], got[slot][:, 128 * s:128 * s + 128],
                                                     pt[j % 2][:, s, 32 * b4:32 * b4 + 32],
                                                     start=(grp == 0 and b4 == 0 and s == 0), stop=False,
                                                     skip_group_check=True)
                        else:
                            last = pe.matmul(out, hd.vs[:], pt_new[:], start=False, stop=True, skip_group_check=True)
                        last.then_inc(valued, 1)

            @block.scalar
            def _(act):
                act.wait_ge(logits, 1)
                act.activation(probs[0][:, PAST:PAST + NS], core.flat(6, NS), ACT.Copy)
                act.activation(probs[1][:, PAST:PAST + NS], core.flat(6, 2 * NS)[:, NS:2 * NS], ACT.Copy).then_inc(kept, 1)
                for r in range(rounds + 1):
                    if r < rounds:
                        act.wait_ge(turned, 2 * r + 1)
                        after(act, logits, r + 1 if r else 0)
                        act.activation(kt[:, 0:2, :].rearrange("p b n -> p (b n)"), core.flat(0, 1024), ACT.Copy)\
                            .then_inc(copied_a, 1)
                    if r >= 1:
                        sg, grp = divmod(r - 1, NGRP)
                        act.wait_ge(logits, r + 1)
                        act.activation(probs[sg][:, GRP * grp:GRP * grp + GRP], core.flat(4 + (r - 1) % 2, 512), ACT.Copy)\
                            .then_inc(kept, 1)
                    if r in (NGRP, rounds):
                        sg = r // NGRP - 1
                        act.wait_ge(kept, r + 1)
                        act.wait_ge(topped, sg + 1)
                        act.activation(probs[sg][:], probs[sg][:], ACT.Exp, bias=top[:, sg:sg + 1],
                                       accum_out=sums[:, sg:sg + 1]).then_inc(exped, 1)
                for n in range(2 * items):
                    sg, grp = divmod(n, items)
                    act.wait_ge(p_turned, n + 1)
                    after(act, valued, n - 1)
                    bank = 6 if n % 2 else 4
                    if grp < NGRP:
                        act.activation(pt[n % 2][:].rearrange("p s n -> p (s n)"), core.flat(bank, 512), ACT.Copy)\
                            .then_inc(p_copied, 1)
                    else:
                        after(act, valued, n - items)
                        act.activation(pt_new[:], core.flat(bank, 128, NS), ACT.Copy).then_inc(p_copied, 1)
                        act.wait_ge(valued, n + 1)
                        for v in range(NKV):
                            dst, src = diagonal(core.rh, sg, v)
                            ins = act.activation(dst, src, ACT.Copy)
                        ins.then_inc(r_hi, 1)

            @block.vector
            def _(dve):
                dve.wait_ge(kept, 1)
                for sg in range(2):
                    ins = dve.tensor_reduce(tops[:, sg, NGRP:NGRP + 1], probs[sg][:, PAST:PAST + NS], AX.X, ALU.max)
                ins.then_inc(maxed, 1)
                for r in range(rounds + 1):
                    if r < rounds:
                        dve.wait_ge(turned, 2 * r + 2)
                        after(dve, logits, r + 1 if r else 0)
                        dve.tensor_copy(kt[:, 2:4, :].rearrange("p b n -> p (b n)"), core.flat(2, 1024)).then_inc(copied_d, 1)
                    if r >= 1:
                        sg, grp = divmod(r - 1, NGRP)
                        dve.wait_ge(kept, r + 1)
                        dve.tensor_reduce(tops[:, sg, grp:grp + 1], probs[sg][:, GRP * grp:GRP * grp + GRP], AX.X, ALU.max)\
                            .then_inc(maxed, 1)
                    if r in (NGRP, rounds):
                        sg = r // NGRP - 1
                        dve.wait_ge(maxed, r + 1)
                        dve.tensor_reduce(top[:, sg:sg + 1], tops[:, sg, :], AX.X, ALU.max, negate=True).then_inc(topped, 1)
                    if r in (NGRP + 2, rounds):
                        sg = 0 if r < rounds else 1
                        dve.wait_ge(exped, sg + 1)
                        dve.reciprocal(inv[:, sg:sg + 1], sums[:, sg:sg + 1]).then_inc(inverted, 1)
                        dve.wait_ge(inverted, sg + 1)
                        dve.tensor_scalar(probs[sg][:], probs[sg][:], inv[:, sg:sg + 1], None, ALU.mult).then_inc(normed, 1)
                for sg in range(2):
                    dve.wait_ge(r_hi, sg + 1)
                    for v in range(NKV):
                        dst, src = diagonal(core.rl, sg, v)
                        hi, _ = diagonal(core.rh, sg, v)
                        dve.tensor_tensor(dst, src, hi.bitcast(F32), ALU.subtract)


def mix_stage(nc, core):
    r2 = At(nc, Map.R2, Map.END)
    sa = [r2(f"sig_a_in{s}", [128, TW]) for s in range(2)]
    mb = [r2(f"mix_b_in{s}", [128, TW]) for s in range(2)]
    part = [r2(f"gated{s}", [128, TW]) for s in range(2)]
    mixed = [r2(f"mixed{s}", [128, TW]) for s in range(2)]
    PA = KB // 2
    loads = PA + KB

    def products_until(n):
        return 2 * (n + 1) if n < PA else 2 * PA + n - PA + 1

    with ExitStack() as ctx:
        sem = Sems(nc, ctx, "mx")
        gates_in = [sem(f"gates_in{s}") for s in range(2)]
        ready, gated, mixed_ok, hi, lo = sem("acc_ready"), sem("gated"), sem("mixed_ok"), sem("hi"), sem("lo")
        added, x_in = sem("added"), sem("x_in")
        w = Weights(core, sem, lambda n: products_until(n - 3) if n >= 3 else 0)
        wpa = core.i["w_pa"][0].rearrange("(v g d) c -> v d g c", v=NKV, g=G)
        wo = core.i["w_o"][0]
        arrived = [0] * loads
        for n in range(loads):
            arrived[n] = (arrived[n - 3] if n >= 3 else 0) + (32 if n < PA else 16)
        def mix(pool, t):
            pool.wait_ge(gated, t + 1)
            after(pool, lo, t - 1)
            pool.tensor_tensor(mixed[t % 2][:], part[t % 2][:], mb[t % 2][:], ALU.add).then_inc(mixed_ok, 1)
            if t % 2:
                n = t // 2 + 3
                w.lo(pool, n, n % 3)

        with nc.Block() as block:

            @block.sync
            def _(sp):
                for n in range(loads):
                    if n < PA:
                        after(sp, w.lo_done, n - 2)
                        for v in range(NKV):
                            dst = core.wr[n % 3][64 * v:64 * v + 64, :].rearrange("p (g m) -> p g m", g=G)
                            sp.dma_start(dst, wpa[v][:, :, 256 * n:256 * n + 256]).then_inc(w.arrived[n % 3], 16)
                    else:
                        j = n - PA
                        w.fetch(sp, n, n % 3, [((0, 1024, 128), by_rows(wo, slice(128 * j, 128 * j + 128)))])
                sp.wait_ge(ready, KB)
                sp.dma_start(core.x[:].rearrange("p k t -> p (k t)"), core.xsave.ap()).then_inc(x_in, 16)
                sp.wait_ge(x_in, 16)

            @block.tensor
            def _(pe):
                for t in range(2 * KB):
                    if t < KB:
                        n, at = t // 2, 128 * (t % 2)
                        after(pe, gated, t - 1)
                        pe.wait_ge(w.lo_done, n + 1)
                        split_product(pe, core, t % 2, G,
                                      lambda k: core.wh[n % 3][:, 256 * k + at:256 * k + at + 128],
                                      lambda k: core.wl[n % 3][:, 256 * k + at:256 * k + at + 128],
                                      lambda k: core.rh[:, k, :], lambda k: core.rl[:, k, :]).then_inc(ready, 1)
                    else:
                        n = PA + t - KB
                        pe.wait_ge(gated, min(t - 1, KB))
                        if t == KB:
                            pe.wait_ge(lo, KB)
                        after(pe, added, t - KB - 1)
                        w.product(pe, n, n % 3, t % 2).then_inc(ready, 1)

            @block.scalar
            def _(act):
                for n in range(3):
                    w.hi(act, n, n, arrived[n], ready)
                for t in range(KB):
                    act.wait_ge(mixed_ok, t + 1)
                    act.activation(core.ah[:, t, :], mixed[t % 2][:], ACT.Copy).then_inc(hi, 1)
                    if t % 2:
                        n = t // 2 + 3
                        w.hi(act, n, n % 3, arrived[n], ready)
                for n in range(PA + 3, loads):
                    w.hi(act, n, n % 3, arrived[n], ready)

            @block.gpsimd
            def _(pool):
                for t in range(KB):
                    if t >= 2:
                        pool.wait_ge(mixed_ok, t - 1)
                    pool.dma_start(sa[t % 2][:], core.siga.ap()[t]).then_inc(gates_in[t % 2], 16)
                    pool.dma_start(mb[t % 2][:], core.mixb.ap()[t]).then_inc(gates_in[t % 2], 16)
                    if t < 3:
                        w.lo(pool, t, t)
                    if t >= 1:
                        mix(pool, t - 1)
                mix(pool, KB - 1)
                for n in range(PA + 3, loads):
                    w.lo(pool, n, n % 3)

            @block.vector
            def _(dve):
                for t in range(KB + 1):
                    if t < KB:
                        dve.wait_ge(ready, t + 1)
                        dve.wait_ge(gates_in[t % 2], 32 * (t // 2 + 1))
                        after(dve, mixed_ok, t - 1)
                        dve.tensor_tensor(tri(part[t % 2][:]), tri(sa[t % 2][:]), core.acc(t % 2), ALU.mult).then_inc(gated, 1)
                    if t >= 1:
                        dve.wait_ge(hi, t)
                        dve.tensor_tensor(core.al[:, t - 1, :], mixed[(t - 1) % 2][:], core.ah[:, t - 1, :].bitcast(F32),
                                          ALU.subtract).then_inc(lo, 1)
                dve.wait_ge(x_in, 16)
                for j in range(KB):
                    dve.wait_ge(ready, KB + j + 1)
                    x = tri(core.x[:, j, :])
                    dve.tensor_tensor(x, x, core.acc(j % 2), ALU.add).then_inc(added, 1)


def ffn_stage(nc, core):
    r2 = At(nc, Map.R2, Map.END)
    p = r2("ffn_a", [128, TW + 2])
    ub = r2("ffn_b", [128, TW])
    u = r2("ffn_conv", [128, TW])
    s = r2("ffn_silu", [128, TW])
    h = r2("ffn_inner", [128, TW])
    hh = r2("ffn_inner_hi", [128, TW], F32R)
    hl = r2("ffn_inner_lo", [128, TW], F32R)
    taps = r2("ffn_taps", [128, 19])
    p6 = r2("ffn_samples", [128, NB, 6])
    states = r2("ffn_states", [128, FB, 18])
    out = r2("ffn_states_out", [18, FF])
    EARLY = KB
    with ExitStack() as ctx:
        sem = Sems(nc, ctx, "ff")
        up, down, added = sem("up"), sem("down"), sem("added")
        ua_copied, ub_copied, taps_ok = sem("ua_copied"), sem("ub_copied"), sem("taps_ok")
        p6_ok, states_ok, conv, silued = sem("p6_ok"), sem("states_ok"), sem("conv"), sem("silued")
        h_ok, h_hi, h_lo, padded = sem("h_ok"), sem("h_hi"), sem("h_lo"), sem("padded")
        turned, copied, stored = sem("states_turned"), sem("states_copied"), sem("states_stored")
        w = Weights(core, sem, None)
        wup, wdown = core.i["ffn_up"][0], core.i["ffn_down"][0]

        def split_hi(act, slot, turn, *used):
            act.wait_ge(w.arrived[slot], 16 * (turn + 1))
            if used:
                act.wait_ge(*used)
            act.activation(core.wh[slot][:], core.wr[slot][:], ACT.Copy).then_inc(w.hi_done, 1)

        with nc.Block() as block:

            @block.sync
            def _(sp):
                def up_fetch(slot, at, done):
                    after(sp, w.lo_done, done)
                    sp.dma_start(core.wr[slot][:].rearrange("p (k m) -> p k m", m=128), by_rows(wup, bass.ds(at, 128)))\
                        .then_inc(w.arrived[slot], 16)

                def down_fetch(at, done):
                    after(sp, w.lo_done, done)
                    sp.dma_start(core.wr[2][:], wdown[bass.ds(at, 128), :]).then_inc(w.arrived[2], 16)

                up_fetch(0, 0, 0)
                up_fetch(1, FF, 0)
                with sp.Fori(1, FB) as j:
                    up_fetch(0, 128 * j, 3 * j - 2)
                    up_fetch(1, 128 * j + FF, 3 * j - 1)
                    down_fetch(128 * j - 128, 3 * j - 1)
                down_fetch(FF - 128, 3 * FB - 1)
                sp.wait_ge(copied, 1)
                sp.dma_start(core.o["ffn_conv_prompt"][0, 0], out[0:2, :]).then_inc(stored, 16)
                sp.dma_start(core.o["ffn_conv_sample"][0].rearrange("b w c -> (b w) c"), out[2:18, :]).then_inc(stored, 16)
                sp.wait_ge(stored, 32)

            @block.tensor
            def _(pe):
                def project(j):
                    first = isinstance(j, int)
                    for slot in range(2):
                        pe.wait_ge(w.lo_done, slot + 1 if first else 3 * j + slot)
                        if not first:
                            pe.wait_ge(added, EARLY + 8 * j - 9 + slot)
                            pe.wait_ge((ua_copied, ub_copied)[slot], j)
                        split_product(pe, core, slot, KB,
                                      lambda k: core.wh[slot][:, 128 * k:128 * k + 128],
                                      lambda k: core.wl[slot][:, 128 * k:128 * k + 128],
                                      lambda k: core.ah[:, k, :], lambda k: core.al[:, k, :]).then_inc(up, 1)

                def collect(j, ahead):
                    pe.wait_ge(w.lo_done, 3 * j + 5 if ahead else 3 * j + 3)
                    pe.wait_ge(h_lo, j + 1)
                    for d in range(KB):
                        if d >= 2:
                            pe.wait_ge(added, EARLY + 8 * j + d - 1)
                        elif ahead:
                            pe.wait_ge((ua_copied, ub_copied)[d], j + 2)
                        else:
                            pe.wait_ge(added, EARLY + 8 * j - 1 + d)
                        split_product(pe, core, d % 2, 1,
                                      lambda k: core.wh[2][:, 128 * d:128 * d + 128],
                                      lambda k: core.wl[2][:, 128 * d:128 * d + 128],
                                      lambda k: hh[:], lambda k: hl[:]).then_inc(down, 1)

                project(0)
                with pe.Fori(1, FB) as j:
                    project(j)
                    collect(j - 1, True)
                collect(FB - 1, False)
                pe.wait_ge(added, EARLY + 8 * FB)
                pe.wait_ge(states_ok, FB)
                for k in range(FB):
                    last = pe.transpose(core.flat(0, FF, 18)[:, 128 * k:128 * k + 128], states[:, k, :], core.c["ident"])
                last.then_inc(turned, 1)

            @block.scalar
            def _(act):
                def turn(j, last=False):
                    first = isinstance(j, int) and j == 0
                    act.wait_ge(up, 2 * j + 1)
                    if not first:
                        act.wait_ge(conv, 4 * j)
                        act.wait_ge(states_ok, j)
                    act.activation(tri(p[:, 2:2 + TW]), core.acc(0), ACT.Copy).then_inc(ua_copied, 1)
                    if not last:
                        split_hi(act, 0, j + 1, up, 2 * j + 1)
                    act.wait_ge(up, 2 * j + 2)
                    if not first:
                        act.wait_ge(h_ok, j)
                    act.activation(tri(ub[:]), core.acc(1), ACT.Copy).then_inc(ub_copied, 1)
                    if not last:
                        split_hi(act, 1, j + 1, up, 2 * j + 2)
                    act.wait_ge(conv, 4 * j + 4)
                    if first:
                        act.wait_ge(padded, 1)
                    else:
                        act.wait_ge(h_ok, j)
                    act.activation(s[:], u[:], ACT.Silu).then_inc(silued, 1)
                    if first:
                        split_hi(act, 2, j)
                    else:
                        split_hi(act, 2, j, down, 8 * j)
                    act.wait_ge(h_ok, j + 1)
                    if not first:
                        act.wait_ge(down, 8 * j)
                        act.wait_ge(h_lo, j)
                    act.activation(hh[:], h[:], ACT.Copy).then_inc(h_hi, 1)

                split_hi(act, 0, 0)
                split_hi(act, 1, 0)
                turn(0)
                with act.Fori(1, FB - 1) as j:
                    turn(j)
                turn(FB - 1, last=True)
                act.wait_ge(turned, 1)
                act.activation(out[:], core.flat(0, FF, 18), ACT.Copy).then_inc(copied, 1)

            @block.gpsimd
            def _(pool):
                def split_lo(slot, done):
                    pool.wait_ge(w.hi_done, done)
                    pool.tensor_tensor(core.wl[slot][:], core.wr[slot][:], core.wh[slot][:].bitcast(F32), ALU.subtract)\
                        .then_inc(w.lo_done, 1)

                def turn(j, last=False):
                    first = isinstance(j, int) and j == 0
                    if not last:
                        split_lo(0, 3 * j + 3)
                        split_lo(1, 3 * j + 4)
                    pool.wait_ge(silued, j + 1)
                    pool.wait_ge(ub_copied, j + 1)
                    if not first:
                        pool.wait_ge(h_hi, j)
                        pool.wait_ge(h_lo, j)
                    pool.tensor_tensor(h[:], s[:], ub[:], ALU.mult).then_inc(h_ok, 1)
                    split_lo(2, 3 * j + (3 if last else 5))
                    pool.wait_ge(h_hi, j + 1)
                    pool.tensor_tensor(hl[:], h[:], hh[:].bitcast(F32), ALU.subtract).then_inc(h_lo, 1)

                pool.memset(p[:, 0:2], 0.0)
                pool.memset(u[:, TOK:TW], 0.0).then_inc(padded, 1)
                split_lo(0, 1)
                split_lo(1, 2)
                pool.wait_ge(padded, 1)
                turn(0)
                with pool.Fori(1, FB - 1) as j:
                    turn(j)
                turn(FB - 1, last=True)

            @block.vector
            def _(dve):
                def convolve(j):
                    us = u[:, TP:TOK].rearrange("p (b t) -> p b t", t=DS)
                    new = p[:, 2 + TP:2 + TOK].rearrange("p (b t) -> p b t", t=DS)
                    first = isinstance(j, int) and j == 0
                    dve.wait_ge(ua_copied, j + 1)
                    dve.wait_ge(taps_ok, j + 1)
                    dve.tensor_copy(p6[:, :, 0:2], taps[:, 0:16].rearrange("p (b w) -> p b w", w=2))
                    dve.tensor_copy(p6[:, :, 2:6], new).then_inc(p6_ok, 1)
                    row = states[:, bass.ds(j, 1), :]
                    dve.tensor_copy(row[:, :, 0:2], p[:, TP:TP + 2].rearrange("p (a w) -> p a w", a=1))
                    dve.tensor_copy(row[:, :, 2:18].rearrange("p a (b w) -> p (a b) w", w=2), new[:, :, 2:4])\
                        .then_inc(states_ok, 1)
                    dve.wait_ge(p6_ok, j + 1)
                    if not first:
                        dve.wait_ge(silued, j)
                    else:
                        dve.wait_ge(padded, 1)
                    dve.tensor_scalar(u[:, 0:TP], p[:, 0:TP], taps[:, 16:17], None, ALU.mult)
                    dve.tensor_scalar(us, p6[:, :, 0:4], taps[:, 16:17], None, ALU.mult).then_inc(conv, 1)
                    for x in (1, 2):
                        dve.wait_ge(conv, 4 * j + x)
                        dve.scalar_tensor_tensor(u[:, 0:TP], p[:, x:x + TP], taps[:, 16 + x:17 + x], u[:, 0:TP],
                                                 ALU.mult, ALU.add)
                        dve.scalar_tensor_tensor(us, p6[:, :, x:x + 4], taps[:, 16 + x:17 + x], us, ALU.mult, ALU.add)\
                            .then_inc(conv, 1 if x == 1 else 2)
                    dve.wait_ge(conv, 4 * j + 4)

                def fetch_taps(j):
                    dve.tensor_copy(taps[:], core.fconv[:, bass.ds(j, 1), :].rearrange("p a r -> p (a r)"))\
                        .then_inc(taps_ok, 1)

                def add(j):
                    for d in range(KB):
                        dve.wait_ge(down, 8 * j + d + 1)
                        dve.wait_ge(added, EARLY + 8 * j + d - 7)
                        x = tri(core.x[:, d, :])
                        dve.tensor_tensor(x, x, core.acc(d % 2), ALU.add).then_inc(added, 1)

                dve.memset(p6[:, 0, 0:2], 0.0).then_inc(added, EARLY)
                dve.wait_ge(added, EARLY)
                fetch_taps(0)
                convolve(0)
                fetch_taps(1)
                with dve.Fori(1, FB - 1) as j:
                    convolve(j)
                    add(j - 1)
                    fetch_taps(j + 1)
                convolve(FB - 1)
                add(FB - 2)
                add(FB - 1)


def output_stage(nc, core):
    r2 = At(nc, Map.R2, Map.END)
    rows = [r2(f"y_rows{s}", [128, D]) for s in range(3)]
    parts = [2 if t == NT - 1 else 1 for t in range(NT)]
    with ExitStack() as ctx:
        sem = Sems(nc, ctx, "out")
        turned, copied = sem("turned"), sem("copied")
        stored = [sem(f"stored{s}") for s in range(3)]
        with nc.Block() as block:

            @block.tensor
            def _(pe):
                for t in range(NT):
                    after(pe, copied, t - 2)
                    n = ROWS[t]
                    for k in range(KB):
                        last = pe.transpose(core.flat(2 * (t % 3), D, n)[:, 128 * k:128 * k + 128],
                                            core.y[:, k, 128 * t:128 * t + n], core.c["ident"])
                    last.then_inc(turned, 1)

            @block.scalar
            def _(act):
                for t in range(NT):
                    act.wait_ge(turned, t + 1)
                    if t >= 3:
                        act.wait_ge(stored[t % 3], 16 * (t // 3))
                    act.activation(rows[t % 3][0:ROWS[t], :], core.flat(2 * (t % 3), D, ROWS[t]), ACT.Copy)\
                        .then_inc(copied, 1)

            @block.sync
            def _(sp):
                y = core.o["y_prompt"][0]
                for t in range(NT):
                    sp.wait_ge(copied, t + 1)
                    a = META if t == 0 else 0
                    sp.dma_start(y[128 * t + a - META:128 * t + QROWS[t] - META], rows[t % 3][a:QROWS[t], :])\
                        .then_inc(stored[t % 3], 16)
                sp.dma_start(core.o["y_sample"].rearrange("b s d -> (b s) d"), rows[(NT - 1) % 3][QROWS[-1]:ROWS[-1], :])\
                    .then_inc(stored[(NT - 1) % 3], 16)
                for s in range(3):
                    sp.wait_ge(stored[s], 16 * sum(parts[s::3]))


OUTS = {
    "y_prompt": (1, SEQ, D), "y_sample": (NB, DS, D),
    "k_prompt": (1, 1, TP, NKV, HD), "v_prompt": (1, 1, TP, NKV, HD), "kidx_prompt": (1, 1, TP, HD),
    "conv_prompt": (1, 1, 2, CD), "ffn_conv_prompt": (1, 1, 2, FF),
    "k_sample": (1, NB, DS, NKV, HD), "v_sample": (1, NB, DS, NKV, HD), "kidx_sample": (1, NB, DS, HD),
    "conv_sample": (1, NB, 2, CD), "ffn_conv_sample": (1, NB, 2, FF),
}


def program(nc, ins, outs, upto=99):
    core = Core(nc, ins, outs)
    core.hd = Heads(nc)
    stages = [lambda: load_stage(nc, core), lambda: norm_stage(nc, core, 0, "norm1"),
              lambda: index_stage(nc, core, core.hd),
              lambda: sample_index_stage(nc, core, core.hd),
              lambda: gate_stage(nc, core, core.hd),
              lambda: rope_stage(nc, core, core.hd),
              lambda: prompt_attention_stage(nc, core, core.hd),
              lambda: sample_attention_stage(nc, core, core.hd),
              lambda: mix_stage(nc, core),
              lambda: norm_stage(nc, core, 1, "norm2"),
              lambda: ffn_stage(nc, core),
              lambda: norm_stage(nc, core, 2, "norm_final", split=False),
              lambda: output_stage(nc, core)]
    groups = [stages[:5], stages[5:9], stages[9:]]
    done = 0
    for group in groups:
        with nc.cleanup_on_exit():
            for stage in group[:max(0, upto - done)]:
                stage()
        done += len(group)
    return core


def kernel(x_prompt, x_sample, cache_k, cache_v, cache_kidx, state_conv, state_ffn_conv, page_table,
           meta_tokens, w_in, w_pa, w_pb, w_o, conv_w, norm1, norm2, ffn_up, ffn_conv_w, ffn_down, norm_final):
    import concourse.bacc as bacc
    from concourse.bass_utils import run_bass_kernel_spmd

    arrays = dict(x_prompt=x_prompt, x_sample=x_sample, cache_k=cache_k, cache_v=cache_v, cache_kidx=cache_kidx,
                  state_conv=state_conv, state_ffn_conv=state_ffn_conv, page_table=page_table,
                  meta_tokens=meta_tokens, w_in=w_in, w_pa=w_pa, w_pb=w_pb, w_o=w_o, conv_w=conv_w, norm1=norm1,
                  norm2=norm2, ffn_up=ffn_up, ffn_conv_w=ffn_conv_w, ffn_down=ffn_down, norm_final=norm_final)
    arrays = {name: np.ascontiguousarray(a) for name, a in arrays.items()}
    arrays["constants"] = constants()
    nc = bacc.Bacc("TRN2", target_bir_lowering=False, num_devices=1)
    ins = {name: nc.dram_tensor(f"in_{name}", list(a.shape), I32 if name == "page_table" else F32,
                                kind="ExternalInput").ap() for name, a in arrays.items()}
    outs = {name: nc.dram_tensor(f"out_{name}", list(shape), F32, kind="ExternalOutput").ap()
            for name, shape in OUTS.items()}
    program(nc, ins, outs)
    result = run_bass_kernel_spmd(nc, [{f"in_{name}": a for name, a in arrays.items()}], core_ids=[0]).results[0]
    return tuple(result[f"out_{name}"] for name in OUTS)
```

```python
import numpy as np
import concourse.bass as bass
from concourse import mybir
from contextlib import ExitStack

F32 = mybir.dt.float32
F32R = mybir.dt.float32r
BF16 = mybir.dt.bfloat16
U8 = mybir.dt.uint8
I32 = mybir.dt.int32
U32 = mybir.dt.uint32
ACT = mybir.ActivationFunctionType
ALU = mybir.AluOpType
AX = mybir.AxisListType

D = 1024
SEQ = 1024
META = 16
TP = SEQ + META
NB, DS = 8, 4
NS = NB * DS
PAST, PAGE = 4096, 128
NPAGES = PAST // PAGE
NPOOL = NB * NPAGES * 5 // 4
TOK = TP + NS
CH = 358
TW = 3 * CH
KB = D // 128
H, HD, NKV, G = 8, 64, 2, 4
NIH = 4
CD = 512
CB = CD // 128
FF = 2816
FB = FF // 128
EPS = 1e-6
TOPK = 256
SM = HD ** -0.5
NEG = -3.0e38
BIG = 1.0e30
QC, KC, VC, QIC, KIC, WIC = 0, 512, 640, 768, 1024, 1088
CBC, CCC, CXC, GAC, GBC = 1092, 1604, 2116, 2628, 3652
PW = 4676
NT = 9
ROWS = [128] * 8 + [TOK - 1024]
QROWS = [128] * 8 + [TP - 1024]
NK = [min(128 * (i + 1), TP) for i in range(NT)]
QB0 = TOPK // 128
SOFF = {}
_o = 0
for _i in range(QB0, NT):
    SOFF[_i] = _o
    _o += NK[_i]
SW = _o
MOFF = []
_o = 0
for _i in range(NT):
    MOFF.append(_o)
    _o += NK[_i]
MW = _o
SQ = PAST // 4
SSW = SQ + NS
NSEL = NT - QB0 + 1
RUN = 8
GATHER = 128 * RUN
NGA = PAST // GATHER
PPG = GATHER // PAGE
GRP = 512
NGRP = PAST // GRP
BASE = 16640
CONSTS = {}
CONST_W = 0
for _n, _w in (("ident", 128), ("perm", 128), ("fold", 128), ("below", 128), ("place", 256), ("owner", 128),
               ("head", 4), ("newkeep", NS), ("newfill", NS), ("lane", 1), ("page", PPG), ("bit", 1), ("ones", 128), ("cos", TW), ("sin", TW)):
    CONSTS[_n] = (CONST_W, _w)
    CONST_W += _w
SBUF_END = 229368


class Map:

    R0 = BASE
    R1 = R0 + KB * TW * 4
    W = R1 + 2 * KB * TW * 4
    C = W + 9 * 4096
    R2 = C + 33 * 512
    END = SBUF_END
    TOTAL = END // 32 * 32 - 4320


class At:

    def __init__(self, nc, at, end):
        self.nc, self.at, self.end = nc, at, end

    def __call__(self, name, shape, dtype=F32):
        size = {F32: 4, F32R: 4, BF16: 2, I32: 4, U32: 4, U8: 1}[dtype]
        for s in shape[1:]:
            size *= s
        t = self.nc.alloc_sbuf_tensor_at(name, shape, dtype, offset=self.at)
        self.at += (size + 31) // 32 * 32
        assert self.at <= self.end, (name, self.at, self.end)
        return t


class Sems:

    def __init__(self, nc, ctx, stage):
        self.nc, self.ctx, self.stage = nc, ctx, stage

    def __call__(self, name):
        return self.nc.alloc_semaphore(f"{self.stage}_{name}")


class Chain:

    def __init__(self, eng, sem):
        self.eng, self.sem, self.n = eng, sem, 0

    def link(self, ins):
        self.n += 1
        ins.then_inc(self.sem, 1)
        return self.n

    def sync(self, n=None):
        n = self.n if n is None else n
        if n > 0:
            self.eng.wait_ge(self.sem, n)


def after(eng, sem, n):
    if isinstance(n, int):
        if n > 0:
            eng.wait_ge(sem, n)
    else:
        eng.wait_ge(sem, n)


def chunks(n, size=512):
    return [(a, min(size, n - a)) for a in range(0, n, size)]


class Core:

    def __init__(self, nc, ins, outs):
        self.nc, self.i, self.o = nc, ins, outs
        self.ps = nc.alloc_psum_tensor("ps", [128, 8, 512], F32)
        c = At(nc, Map.C, Map.R2)
        self.cbuf = c("constants", [128, CONST_W])
        self.c = {name: self.cbuf[:, at:at + width] for name, (at, width) in CONSTS.items()}
        self.conv = c("conv_w_and_states", [128, CB, 19])
        self.fconv = c("ffn_conv_w_and_states", [128, FB, 19])
        self.gains = c("gains", [128, KB, 2])
        by_token = c("norm_numbers", [128, 4, NT])
        self.ss, self.mean, self.root, self.inv = (by_token[:, x, :] for x in range(4))
        self.place = c("place_bf16", [128, 2, 128], BF16)
        self.identb = c("ident_bf16", [128, 128], BF16)
        self.rows = c("gather_rows", [128, NB * NGA], U32)
        self.wi = c("index_weights", [128, NT, NIH])
        self.wsel = c("index_weights_placed", [128, 2, 2, NS])
        self.x = nc.alloc_sbuf_tensor_at("xt", [128, KB, TW], F32, offset=Map.R0)
        self.ah = nc.alloc_sbuf_tensor_at("act_hi", [128, KB, TW], F32R, offset=Map.R1)
        self.al = nc.alloc_sbuf_tensor_at("act_lo", [128, KB, TW], F32R, offset=Map.R1 + KB * TW * 4)
        w = At(nc, Map.W, Map.C)
        self.wr = [w(f"w_raw{s}", [128, 1024]) for s in range(3)]
        self.wh = [w(f"w_hi{s}", [128, 1024], F32R) for s in range(3)]
        self.wl = [w(f"w_lo{s}", [128, 1024], F32R) for s in range(3)]
        x = At(nc, Map.R0, Map.R1)
        self.kit = x("index_keys", [128, TW])
        self.qit = x("index_queries", [128, 2, TW])
        self.qis = nc.alloc_sbuf_tensor_at("index_queries_samples", [128, NIH, NS], F32, offset=Map.R1 - 4096)
        self.qibd = nc.alloc_sbuf_tensor_at("index_queries_diagonal", [128, NB, 32], F32, offset=Map.R1 - 3072)
        self.wis = nc.alloc_sbuf_tensor_at("index_weights_samples", [NS, NIH], F32, offset=Map.R1 - 2048)
        self.wrow = nc.alloc_sbuf_tensor_at("index_weights_rows", [128, 2], F32, offset=Map.R1 - 1024)
        self.wrow4 = nc.alloc_sbuf_tensor_at("index_weights_rows4", [128, 2, 4], F32, offset=Map.R1 - 1024 + 32)
        self.xsave = nc.dram_tensor("x_save", [128, KB * TW], F32)
        self.mixb = nc.dram_tensor("mix_b", [KB, 128, TW], F32)
        self.siga = nc.dram_tensor("sig_a", [KB, 128, TW], F32)

    def acc(self, s):
        return self.ps[:, 3 * s:3 * s + 3, 0:CH]

    def onerow(self, rows, n):
        return self.c["ones"][0:rows, 0:1].broadcast_to([rows, n])

    def flat(self, bank, n, rows=128):
        return self.ps[:].rearrange("p b c -> p (b c)")[0:rows, 512 * bank:512 * bank + n]


def tri(ap):
    return ap.rearrange("p (c n) -> p c n", c=3)


def split_product(pe, core, out_set, kblocks, wh, wl, bh, bl, rows=128, before=None):
    last = None
    for k in range(kblocks):
        if before:
            before(k)
        for n, (w, b) in enumerate(((wh, bh), (wh, bl), (wl, bh))):
            for c in range(3):
                last = pe.matmul(core.acc(out_set)[0:rows, c, :], w(k), b(k)[:, c * CH:(c + 1) * CH],
                                 start=(k == 0 and n == 0), stop=(k == kblocks - 1 and n == 2))
    return last


def constants():
    p = np.arange(128)
    c = {"ident": np.eye(128), "ones": np.ones((128, 128))}
    half = HD // 8
    perm = np.zeros((128, 128))
    for i in p:
        if i % HD < half:
            perm[i + half, i] = -1
        elif i % HD < 2 * half:
            perm[i - half, i] = 1
    c["perm"] = perm
    same = (p[:, None] % NS) == (p[None, :] % NS)
    c["fold"] = same
    c["below"] = same & (p[:, None] < p[None, :])
    place = np.zeros((128, 2, 128))
    owner = np.zeros((128, 2, 2, NS))
    for r in p:
        b4, par, t = r // 32, r // 16 % 2, r % 4
        for sg in range(2):
            token = (sg * 4 + b4) * DS + t
            place[token::NS, sg, r] = 1
            owner[r, sg, par, token] = 1
    c["place"], c["owner"] = place.reshape(128, 256), owner.reshape(128, 128)
    c["head"] = (p[:, None] // 4 % 4) == np.arange(4)[None, :]
    token, key = p[:, None] % NS, np.arange(NS)[None, :]
    keep = (p[:, None] >= 96) & (token // DS == key // DS) & (key % DS <= token % DS)
    c["newkeep"], c["newfill"] = keep, np.where(keep, 0.0, NEG)
    c["lane"] = p[:, None] % (PAGE // RUN)
    c["page"] = (p[:, None] // (PAGE // RUN)) == np.arange(PPG)[None, :]
    c["bit"] = np.full((128, 1), 2.0)
    pos = np.zeros(TW, np.float32)
    pos[:TP] = np.arange(TP)
    pos[TP:TOK] = PAST + np.arange(NS) % DS
    rot = HD // 4
    inv = np.power(500000.0, -np.arange(half) * 2.0 / rot).astype(np.float32)
    ang = pos[:, None] * inv[None, :]
    cos, sin = np.ones((128, TW)), np.zeros((128, TW))
    for i in p:
        if i % HD < rot:
            cos[i] = np.cos(ang[:, i % half])
            sin[i] = np.sin(ang[:, i % half])
    c["cos"], c["sin"] = cos, sin
    return np.concatenate([np.asarray(c[n], np.float32) for n in CONSTS], 1)


def x_rows(ins, t):
    xp = ins["x_prompt"][0]
    if t == 0:
        return [((0, META), ins["meta_tokens"]), ((META, 128), xp[0:128 - META])]
    if t < NT - 1:
        return [((0, 128), xp[128 * t - META:128 * (t + 1) - META])]
    own = QROWS[-1]
    return [((0, own), xp[SEQ - own:SEQ]), ((own, own + NS), ins["x_sample"].rearrange("b s d -> (b s) d"))]


def load_stage(nc, core, ahead):
    r2 = At(nc, Map.R2, Map.END)
    rows = [r2(f"x_rows{s}", [128, D]) for s in range(3)]
    junk = r2("squares", [128, D])
    conv_rows = r2("conv_rows", [19, CD])
    fconv_rows = r2("ffn_conv_rows", [19, FF])
    gain_rows = r2("gain_rows", [2, D])
    pages = r2("pages", [128, NB * NPAGES], I32)
    picked = r2("pages_picked", [128, NB * NPAGES])
    page = r2("page", [128, NB * NGA])
    with ExitStack() as ctx:
        sem = Sems(nc, ctx, "ld")
        pages_in, own = sem("pages_in"), sem("own")
        ident_in, consts_in, small_in = sem("ident_in"), sem("consts_in"), sem("small_in")
        x_in = [sem(f"x_in{s}") for s in range(3)]
        turned, small_turned, copied, zeroed = sem("turned"), sem("small_turned"), sem("copied"), sem("zeroed")
        saved, small_copied, squared, ss_ok = sem("saved"), sem("small_copied"), sem("squared"), sem("ss_ok")
        ins = core.i
        parts = [len(x_rows(ins, t)) for t in range(NT)]
        x_count = [16 * sum(parts[t % 3:t + 1:3]) for t in range(NT)]
        ident = core.c["ident"]
        with nc.Block() as block:

            @block.sync
            def _(sp):
                sp.dma_start(core.cbuf[:, 0:128], ins["constants"][:, 0:128]).then_inc(ident_in, 16)
                for t in range(NT):
                    if t >= 3:
                        sp.wait_ge(turned, t - 2)
                        sp.wait_ge(squared, t - 2)
                    for (a, b), src in x_rows(ins, t):
                        sp.dma_start(rows[t % 3][a:b, :], src).then_inc(x_in[t % 3], 16)
                ahead.fetch(sp)
                sp.wait_ge(copied, NT)
                sp.wait_ge(zeroed, 1)
                sp.dma_start(core.xsave.ap(), core.x[:].rearrange("p k t -> p (k t)")).then_inc(saved, 16)
                sp.wait_ge(saved, 16)

            @block.scalar
            def _(act):
                for dst, src in (
                    (conv_rows[0:16, :], ins["state_conv"][0].rearrange("b w c -> (b w) c")),
                    (conv_rows[16:19, :], ins["conv_w"][0]),
                    (fconv_rows[0:16, :], ins["state_ffn_conv"][0].rearrange("b w c -> (b w) c")),
                    (fconv_rows[16:19, :], ins["ffn_conv_w"][0]),
                    (gain_rows[0:1, :], ins["norm1"]), (gain_rows[1:2, :], ins["norm2"]),
                ):
                    act.dma_start(dst, src).then_inc(small_in, 16)
                act.dma_start(core.cbuf[:, 128:], ins["constants"][:, 128:]).then_inc(consts_in, 16)
                table = ins["page_table"].rearrange("b n -> (b n)").rearrange("(a n) -> a n", a=1)
                act.dma_start(pages[:], table.broadcast_to([128, NB * NPAGES])).then_inc(pages_in, 16)
                act.wait_ge(ss_ok, 1)
                for t in range(NT):
                    act.wait_ge(x_in[t % 3], x_count[t])
                    after(act, squared, t)
                    act.activation(junk[0:ROWS[t], :], rows[t % 3][0:ROWS[t], :], ACT.Square,
                                   accum_out=core.ss[0:ROWS[t], t:t + 1]).then_inc(squared, 1)
                act.wait_ge(small_turned, 1)
                act.activation(core.conv[:], core.flat(6, CB * 19).rearrange("p (k r) -> p k r", r=19),
                               ACT.Copy).then_inc(small_copied, 1)
                act.activation(core.gains[:], core.flat(6, 200)[:, 100:100 + 2 * KB].rearrange("p (k r) -> p k r", r=2),
                               ACT.Copy).then_inc(small_copied, 1)
                act.activation(core.fconv[:], core.flat(7, FB * 19).rearrange("p (k r) -> p k r", r=19),
                               ACT.Copy).then_inc(small_copied, 1)
                act.wait_ge(consts_in, 16)
                act.mul(core.identb[:], core.c["ident"], -BIG)
                act.mul(core.place[:].rearrange("p s r -> p (s r)"), core.c["place"], -BIG)

            @block.tensor
            def _(pe):
                pe.wait_ge(ident_in, 16)
                for t in range(NT):
                    n = ROWS[t]
                    pe.wait_ge(x_in[t % 3], x_count[t])
                    if t >= 3:
                        pe.wait_ge(copied, t - 2)
                    for k in range(KB):
                        last = pe.transpose(core.flat(2 * (t % 3), 1024)[:, 128 * k:128 * k + n],
                                            rows[t % 3][0:n, 128 * k:128 * k + 128], ident[0:n, 0:n])
                    last.then_inc(turned, 1)
                pe.wait_ge(small_in, 16 * 6)
                for k in range(CB):
                    pe.transpose(core.flat(6, CB * 19)[:, 19 * k:19 * k + 19], conv_rows[:, 128 * k:128 * k + 128],
                                 ident[0:19, 0:19])
                for k in range(KB):
                    pe.transpose(core.flat(6, 200)[:, 100 + 2 * k:102 + 2 * k], gain_rows[:, 128 * k:128 * k + 128],
                                 ident[0:2, 0:2])
                for k in range(FB):
                    last = pe.transpose(core.flat(7, FB * 19)[:, 19 * k:19 * k + 19],
                                        fconv_rows[:, 128 * k:128 * k + 128], ident[0:19, 0:19])
                last.then_inc(small_turned, 1)

            @block.vector
            def _(dve):
                dve.memset(core.ss, float(D)).then_inc(ss_ok, 1)
                dve.memset(core.x[:, :, TOK:TW], 0.0).then_inc(zeroed, 1)
                for t in range(NT):
                    dve.wait_ge(turned, t + 1)
                    src = core.flat(2 * (t % 3), 1024).rearrange("p (k n) -> p k n", k=KB)
                    dve.tensor_copy(core.x[:, :, 128 * t:128 * t + ROWS[t]], src[:, :, 0:ROWS[t]]).then_inc(copied, 1)
                dve.wait_ge(pages_in, 16)
                dve.wait_ge(consts_in, 16)
                dve.tensor_tensor(picked[:].rearrange("p (m q) -> p m q", q=PPG),
                                  pages[:].rearrange("p (m q) -> p m q", q=PPG),
                                  core.c["page"].rearrange("p (m q) -> p m q", m=1).broadcast_to([128, NB * NGA, PPG]),
                                  ALU.mult).then_inc(own, 1)
                dve.wait_ge(own, 1)
                dve.tensor_reduce(page[:], picked[:].rearrange("p (m q) -> p m q", q=PPG), AX.X, ALU.add).then_inc(own, 1)
                dve.wait_ge(own, 2)
                dve.tensor_scalar(core.rows[:], page[:], float(PAGE // RUN), core.c["lane"], ALU.mult, ALU.add)

def inverse_roots(act, dve, core, rooted, own):
    if act:
        act.wait_ge(own, 1)
        act.activation(core.root, core.mean, ACT.Sqrt).then_inc(rooted, 1)
        return
    chain = Chain(dve, own)
    chain.link(dve.tensor_scalar(core.mean, core.ss, 1.0 / D, EPS, ALU.mult, ALU.add))
    dve.wait_ge(rooted, 1)
    chain.link(dve.reciprocal(core.inv, core.root))
    chain.sync()
    chain.link(dve.tensor_tensor(core.root, core.inv, core.inv, ALU.mult))
    chain.sync()
    chain.link(dve.scalar_tensor_tensor(core.root, core.mean, -0.5, core.root, ALU.mult, ALU.mult))
    chain.sync()
    chain.link(dve.scalar_tensor_tensor(core.inv, core.root, 1.5, core.inv, ALU.add, ALU.mult))
    chain.sync()


def sum_features(pe, core, total, summed):
    for t in range(NT):
        last = pe.matmul(core.flat(7, 16, ROWS[t])[:, t:t + 1], total[:, 128 * t:128 * t + ROWS[t]],
                         core.c["ones"][:, 0:1], start=True, stop=True)
    last.then_inc(summed, 1)


def take_sums(dve, core, summed, taken):
    dve.wait_ge(summed, 1)
    dve.tensor_copy(core.ss[:, 0:NT - 1], core.flat(7, NT - 1))
    dve.tensor_copy(core.ss[0:ROWS[-1], NT - 1:NT], core.flat(7, 16, ROWS[-1])[:, NT - 1:NT]).then_inc(taken, 1)
    dve.wait_ge(taken, 1)


def norm_stage(nc, core, which, name, ahead, total=None):
    r2 = At(nc, Map.R2, Map.TOTAL)
    y = [r2(f"{name}_y{k}", [128, TOK]) for k in range(KB)]
    diag = r2(f"{name}_diagonals", [128, NT, 128])
    sem = Sems(nc, None, name)
    summed, taken, rooted, own, spread = sem("summed"), sem("taken"), sem("rooted"), sem("own"), sem("spread")
    diagonal, scaled, hi, lo_even, lo_odd = sem("diagonal"), sem("scaled"), sem("hi"), sem("lo_even"), sem("lo_odd")
    spread_out = core.flat(3, TOK)

    def low(eng, k):
        eng.wait_ge(hi, k + 1)
        eng.tensor_tensor(core.al[:, k, 0:TOK], y[k][:], core.ah[:, k, 0:TOK].bitcast(F32), ALU.subtract)\
            .then_inc(lo_odd if k % 2 else lo_even, 1)

    with nc.Block() as block:

        @block.tensor
        def _(pe):
            if total is not None:
                sum_features(pe, core, total, summed)
            for t in range(NT):
                n = ROWS[t]
                pe.wait_ge(diagonal, t + 1)
                last = pe.matmul(spread_out[:, 128 * t:128 * t + n], core.c["ones"][0:n, :], diag[0:n, t, 0:n],
                                 start=True, stop=True)
            last.then_inc(spread, 1)
            ahead.w.product(pe, 0, 0, 0, m=ahead.m,
                            before=lambda k: pe.wait_ge(lo_odd if k % 2 else lo_even, k // 2 + 1)).then_inc(ahead.ready, 1)

        @block.scalar
        def _(act):
            inverse_roots(act, None, core, rooted, own)
            ahead.hi(act, 0)
            for k in range(KB):
                act.wait_ge(scaled, k + 1)
                act.activation(core.ah[:, k, 0:TOK], y[k][:], ACT.Copy).then_inc(hi, 1)
                if k in (3, 5):
                    ahead.hi(act, k // 2)

        @block.vector
        def _(dve):
            if total is not None:
                take_sums(dve, core, summed, taken)
            inverse_roots(None, dve, core, rooted, own)
            for t in range(NT):
                n = ROWS[t]
                dve.tensor_scalar(diag[0:n, t, :], core.c["ident"][0:n, :], core.inv[0:n, t:t + 1], None, ALU.mult)\
                    .then_inc(diagonal, 1)
            dve.wait_ge(spread, 1)
            for k in range(KB):
                dve.scalar_tensor_tensor(y[k][:], core.x[:, k, 0:TOK], core.gains[:, k, which:which + 1],
                                         spread_out, ALU.mult, ALU.mult).then_inc(scaled, 1)
                if k % 2 == 0 and k:
                    low(dve, k - 1)
            low(dve, KB - 1)

        @block.gpsimd
        def _(pool):
            pool.memset(core.ah[:, :, TOK:TW].bitcast(F32), 0.0)
            pool.memset(core.al[:, :, TOK:TW].bitcast(F32), 0.0)
            ahead.lo(pool, 0)
            for k in range(0, KB, 2):
                low(pool, k)
                if k >= 4:
                    ahead.lo(pool, k // 2 - 1)



class Weights:

    def __init__(self, core, sem, free, start=0):
        self.core, self.free, self.start = core, free, start
        self.arrived = [sem(f"w_arrived{s}") for s in range(3)]
        self.hi_done, self.lo_done = sem("w_hi"), sem("w_lo")
        self.pieces = [0, 0, 0]

    def fetch(self, sp, n, slot, pieces):
        after(sp, self.lo_done, n - 2)
        for (a, b, m), src in pieces:
            dst = self.core.wr[slot][:, a:b].rearrange("p (k m) -> p k m", m=m)
            sp.dma_start(dst, src).then_inc(self.arrived[slot], 16)

    def hi(self, act, n, slot, arrived, used, width=1024):
        act.wait_ge(self.arrived[slot], arrived)
        after(act, used, self.free(n))
        act.activation(self.core.wh[slot][:, 0:width], self.core.wr[slot][:, 0:width], ACT.Copy)\
            .then_inc(self.hi_done, 1)

    def lo(self, eng, n, slot, width=1024):
        eng.wait_ge(self.hi_done, n + 1)
        eng.tensor_tensor(self.core.wl[slot][:, 0:width], self.core.wr[slot][:, 0:width],
                          self.core.wh[slot][:, 0:width].bitcast(F32), ALU.subtract).then_inc(self.lo_done, 1)

    def product(self, pe, n, slot, out_set, kblocks=KB, bh=None, bl=None, m=128, at=0, before=None):
        core = self.core
        pe.wait_ge(self.lo_done, n + 1)
        bh = bh or (lambda k: core.ah[:, k, :])
        bl = bl or (lambda k: core.al[:, k, :])
        return split_product(pe, core, out_set, kblocks,
                             lambda k: core.wh[slot][:, at + k * m:at + (k + 1) * m],
                             lambda k: core.wl[slot][:, at + k * m:at + (k + 1) * m], bh, bl, m, before)


class Ahead:

    def __init__(self, w, loads, ready=None, m=128):
        self.w, self.loads = w, loads
        self.ready, self.m = ready, m

    def fetch(self, sp):
        for n, (_, pieces) in enumerate(self.loads):
            for (parts, cols, m), src in pieces:
                dst = self.w.core.wr[n][parts, cols].rearrange("p (k m) -> p k m", m=m)
                sp.dma_start(dst, src).then_inc(self.w.arrived[n], 16)

    def hi(self, act, n):
        if n < len(self.loads):
            self.w.hi(act, n, n, 16 * len(self.loads[n][1]), None, self.loads[n][0])

    def lo(self, eng, n):
        if n < len(self.loads):
            self.w.lo(eng, n, n, self.loads[n][0])


EVERY = slice(0, 128)
WIDE = HD + NIH


def index_ahead(nc, core):
    win = core.i["w_in"][0]
    sem = Sems(nc, None, "ix")
    w = Weights(core, sem, lambda n: n - 2)
    return Ahead(w, [(WIDE * KB, [((EVERY, slice(0, WIDE * KB), WIDE), by_rows(win, slice(KIC, KIC + WIDE)))])] + [
        (1024, [((EVERY, slice(0, 1024), 128), by_rows(win, slice(QIC + 128 * j, QIC + 128 * j + 128)))]) for j in range(2)],
        sem("acc_ready"), WIDE)


def gate_ahead(nc, core):
    win = core.i["w_in"][0]
    w = Weights(core, Sems(nc, None, "gt"), lambda n: n - 2)
    return Ahead(w, [(1024, [((EVERY, slice(0, 1024), 128), by_rows(win, slice(c, c + 128)))]) for c in (CCC, CXC, CBC)])


PA = KB // 2


def mix_products_until(n):
    return 2 * (n + 1) if n < PA else 2 * PA + n - PA + 1


def pa_pieces(core, n):
    wpa = core.i["w_pa"][0].rearrange("(v g d) c -> v d g c", v=NKV, g=G)
    return [((slice(64 * v, 64 * v + 64), slice(0, 1024), 256), wpa[v][:, :, 256 * n:256 * n + 256]) for v in range(NKV)]


def mix_ahead(nc, core):
    w = Weights(core, Sems(nc, None, "mx"), lambda n: mix_products_until(n - 3) if n >= 3 else 0)
    return Ahead(w, [(1024, pa_pieces(core, n)) for n in range(3)])


def ffn_ahead(nc, core):
    wup = core.i["ffn_up"][0]
    sem = Sems(nc, None, "ff")
    w = Weights(core, sem, lambda n: 0)
    return Ahead(w, [(1024, [((EVERY, slice(0, 1024), 128), by_rows(wup, slice(at, at + 128)))]) for at in (0, FF)],
                 sem("up"))


def by_rows(w, cols):
    return w.rearrange("(k p) c -> p k c", p=128)[:, :, cols]


class Heads:

    def __init__(self, nc):
        a = At(nc, Map.R2, Map.END)
        self.s = a("scores", [128, SW])
        self.ss = a("sample_scores", [128, SSW])
        self.behind_scores = a.at
        b = At(nc, Map.R2, Map.END)
        self.q = b("q", [128, G, TW])
        self.k = b("k", [128, TW])
        self.v = b("v", [128, NT, 128])
        self.vs = b("v_samples", [NS, 128])
        assert b.at <= a.at + 4096
        c = At(nc, max(a.at, b.at), Map.END)
        self.mask = c("mask", [128, MW], BF16)
        self.smask = c("sample_mask", [128, SSW], BF16)
        self.qs = c("q_samples", [128, NB, 32])
        self.vh = c("v_hi", [128, NT, 128], F32R)
        self.vl = c("v_lo", [128, NT, 128], F32R)
        self.end = c.at - 2 * NT * 128 * 4
        d = At(nc, Map.R2 + 26624, Map.END)
        self.row = [d(f"row{u}", [128, TW + 2]) for u in range(6)]
        self.junk = [d(f"count_junk{u}", [128, SSW], U8) for u in range(2)]
        self.count = d("count", [128, NSEL])
        self.kth = d("kth", [128, NSEL], I32)
        self.cand = d("candidate", [128, NSEL], I32)
        self.bit = d("bit", [128, 1], I32)
        self.enough = d("enough", [128, NSEL])
        self.need = d("need", [128, NSEL])
        self.sign = d("sign", [128, NSEL])
        self.need0 = d("need0", [128, NSEL])
        self.need1 = d("need1", [128, NSEL])
        self.p6 = d("conv_samples", [128, NB, 6])
        self.cs = d("conv_states", [128, CB, 18])
        self.after_search = d.at
        self.bh = nc.alloc_sbuf_tensor_at("b_hi", [128, CB, TW], F32R, offset=Map.R0)
        self.raw = [nc.alloc_sbuf_tensor_at(f"raw_qkv{u}", [128, TW], F32, offset=Map.R0 + 4320 * u) for u in range(6)]
        e = At(nc, Map.R1 + 22528, Map.W)
        self.kqh = [e(f"kq_hi{u}", [128, TW], F32R) for u in range(1 + G)]
        self.kql = [e(f"kq_lo{u}", [128, TW], F32R) for u in range(1 + G)]
        self.bl = nc.alloc_sbuf_tensor_at("b_lo", [128, CB, TW], F32R, offset=Map.R0 + CB * TW * 4)

    def part(self, i):
        if i == NSEL - 1:
            return self.ss[:]
        qb = QB0 + i
        return self.s[0:QROWS[qb], SOFF[qb]:SOFF[qb] + NK[qb]]

    def rows(self, i):
        return 128 if i == NSEL - 1 else QROWS[QB0 + i]


def index_stage(nc, core, hd, w, acc_ready, following):
    r = At(nc, hd.behind_scores, Map.END)
    rot = [core.kit[:], core.qit[:, 0, :], core.qit[:, 1, :]]
    raw = [nc.alloc_sbuf_tensor_at(f"raw{u}", [128, TW], F32, offset=Map.R0 + 3 * 4320 + u * 4320) for u in range(3)]
    tmp = [nc.alloc_sbuf_tensor_at(f"rtmp{u}", [128, TW], F32, offset=Map.R0 + 6 * 4320 + u * 4320) for u in range(1)]
    relu = [r(f"relu{s}", [128, TW]) for s in range(2)]
    keys_out = r("keys_out", [128, NT, HD])
    wi_rows = relu[1]
    kqh = [r(f"index_hi{u}", [128, TW], F32R) for u in range(2)]
    kql = [r(f"index_lo{u}", [128, TW], F32R) for u in range(2)]
    kqh.append(nc.alloc_sbuf_tensor_at("index_hi2", [128, TW], F32R, offset=Map.R0 + 3 * 4320))
    kql.append(nc.alloc_sbuf_tensor_at("index_lo2", [128, TW], F32R, offset=Map.R0 + 4 * 4320))
    with ExitStack() as ctx:
        sem = Sems(nc, ctx, "ix")
        raw_copied, acc_free_d = sem("raw_copied"), sem("acc_free_d")
        wi_copied = sem("wi_copied")
        cosined, roped, own = sem("cosined"), sem("roped"), sem("own")
        turned, keys_copied, stored = sem("turned"), sem("keys_copied"), sem("stored")
        scored, relued, summed, masked = sem("scored"), sem("relued"), sem("summed"), sem("masked")
        swapped, hi, lo, doubled = sem("swapped"), sem("hi"), sem("lo"), sem("doubled")
        blocks = range(QB0, NT)
        with nc.Block() as block:

            @block.sync
            def _(sp):
                following.fetch(sp)
                sp.wait_ge(raw_copied, 1)
                sp.dma_start(raw[0][HD:128, :], raw[0][0:HD, :]).then_inc(doubled, 16)
                sp.wait_ge(roped, 3)
                for j in range(2):
                    for half in range(2):
                        for to in range(2):
                            sp.dma_start(core.qis[64 * to:64 * to + 64, 2 * j + half, :],
                                         core.qit[64 * half:64 * half + 64, j, TP:TOK]).then_inc(swapped, 16)
                sp.wait_ge(keys_copied, 1)
                ko = keys_out
                sp.dma_start(core.o["kidx_prompt"][0, 0, 0:1024].rearrange("(t p) d -> p t d", p=128),
                             ko[:, 0:8, :]).then_inc(stored, 16)
                sp.dma_start(core.o["kidx_prompt"][0, 0, 1024:TP], ko[0:QROWS[8], 8, :]).then_inc(stored, 16)
                sp.dma_start(core.o["kidx_sample"][0].rearrange("b s d -> (b s) d"),
                             ko[QROWS[8]:ROWS[8], 8, :]).then_inc(stored, 16)
                sp.wait_ge(stored, 48)
                sp.wait_ge(swapped, 16 * 8)

            @block.tensor
            def _(pe):
                for u in (1, 2):
                    if u == 2:
                        pe.wait_ge(raw_copied, 1)
                    w.product(pe, u, u, u % 2).then_inc(acc_ready, 1)
                pe.wait_ge(raw_copied, 1)
                rows = slice(HD, WIDE)
                for t in range(NT):
                    n = min(128, TW - 128 * t)
                    last = pe.transpose(core.flat(6, 64, n)[:, 4 * t:4 * t + 4], wi_rows[rows, 128 * t:128 * t + n],
                                        core.c["ident"][rows, rows])
                last.then_inc(acc_ready, 1)
                pe.transpose(core.flat(7, 4, NS), wi_rows[rows, TP:TOK], core.c["ident"][rows, rows]).then_inc(acc_ready, 1)
                for u in range(3):
                    s = (u + 1) % 2
                    pe.wait_ge(raw_copied, min(u + 2, 3))
                    if u == 0:
                        pe.wait_ge(doubled, 16)
                    if u == 2:
                        pe.wait_ge(acc_free_d, 1)
                    for c in range(3):
                        last = pe.matmul(core.acc(s)[:, c, :], core.c["perm"], raw[u][:, c * CH:(c + 1) * CH],
                                         start=True, stop=True)
                    last.then_inc(acc_ready, 1)
                pe.wait_ge(roped, 1)
                pe.wait_ge(acc_free_d, 2)
                for t in range(NT):
                    last = pe.transpose(core.flat(0, NT * HD, ROWS[t])[:, HD * t:HD * t + HD] if t < 8 else
                                        core.flat(1, HD, ROWS[t]),
                                        core.kit[0:HD, 128 * t:128 * t + ROWS[t]], core.c["ident"][0:HD, 0:HD])
                last.then_inc(turned, 1)
                pe.wait_ge(wi_copied, 1)
                for sg in range(2):
                    last = pe.matmul(core.flat(7, 8)[:, 4 * sg:4 * sg + 4],
                                     core.c["place"].rearrange("p (s r) -> p s r", s=2)[0:NS, sg, :],
                                     core.wis[:], start=True, stop=True)
                last.then_inc(turned, 1)
                pe.wait_ge(lo, 3)
                pe.wait_ge(acc_free_d, 3)
                pe.wait_ge(keys_copied, 1)
                m = 0
                for qb in blocks:
                    n = QROWS[qb]
                    for h in range(NIH):
                        half = 64 * (h % 2)
                        after(pe, relued, m - 1)
                        for a, width in chunks(NK[qb]):
                            for x, (q, k) in enumerate(((kqh, kqh), (kqh, kql), (kql, kqh))):
                                last = pe.matmul(core.flat(3 * (m % 2), TP, n)[:, a:a + width],
                                                 q[1 + h // 2][half:half + 64, 128 * qb:128 * qb + n],
                                                 k[0][half:half + 64, a:a + width], start=(x == 0), stop=(x == 2))
                        last.then_inc(scored, 1)
                        m += 1

            @block.scalar
            def _(act):
                act.wait_ge(acc_ready, 1)
                act.activation(tri(raw[0][0:HD, :]), core.acc(0)[0:HD], ACT.Copy)
                act.activation(tri(wi_rows[HD:WIDE, :]), core.acc(0)[HD:WIDE], ACT.Copy).then_inc(raw_copied, 1)
                for u in (1, 2):
                    act.wait_ge(acc_ready, u + 1)
                    act.activation(tri(raw[u][:]), core.acc(u % 2), ACT.Copy).then_inc(raw_copied, 1)
                act.wait_ge(acc_ready, 4)
                scale = float((NIH * HD) ** -0.5)
                act.mul(core.wi[:, 0:8, :].rearrange("p t h -> p (t h)"), core.flat(6, 32), scale)
                act.wait_ge(acc_ready, 5)
                act.mul(core.wi[0:ROWS[8], 8, :], core.flat(6, 64, ROWS[8])[:, 32:36], scale)
                act.mul(core.wis[:], core.flat(7, 4, NS), scale).then_inc(wi_copied, 1)
                act.wait_ge(turned, 1)
                act.activation(keys_out[:, 0:8, :].rearrange("p t d -> p (t d)"), core.flat(0, 8 * HD), ACT.Copy)
                act.activation(keys_out[0:ROWS[8], 8, :], core.flat(1, HD, ROWS[8]), ACT.Copy).then_inc(keys_copied, 1)
                for u in range(3):
                    act.wait_ge(roped, u + 1)
                    act.activation(kqh[u][:], rot[u], ACT.Copy).then_inc(hi, 1)
                m = 0
                for qb in blocks:
                    for h in range(NIH):
                        act.wait_ge(scored, m + 1)
                        after(act, summed, m - 1)
                        act.activation(relu[m % 2][0:QROWS[qb], 0:NK[qb]], core.flat(3 * (m % 2), NK[qb], QROWS[qb]),
                                       ACT.Relu).then_inc(relued, 1)
                        m += 1

            @block.vector
            def _(dve):
                for u in range(3):
                    dve.wait_ge(acc_ready, 6 + u)
                    dve.wait_ge(cosined, u + 1)
                    dve.tensor_tensor(tri(tmp[0][:]), tri(core.c["sin"]), core.acc((u + 1) % 2), ALU.mult)\
                        .then_inc(acc_free_d, 1)
                    dve.wait_ge(acc_free_d, u + 1)
                    dve.tensor_tensor(rot[u], rot[u], tmp[0][:], ALU.add).then_inc(roped, 1)
                    dve.wait_ge(roped, u + 1)
                for u in range(3):
                    dve.wait_ge(hi, u + 1)
                    dve.tensor_tensor(kql[u][:], rot[u], kqh[u][:].bitcast(F32), ALU.subtract).then_inc(lo, 1)
                m = 0
                for qb in blocks:
                    n, k = QROWS[qb], NK[qb]
                    s = hd.s[0:n, SOFF[qb]:SOFF[qb] + k]
                    for h in range(NIH):
                        wi = core.wi[0:n, qb, h:h + 1]
                        dve.wait_ge(relued, m + 1)
                        if m == 0:
                            dve.wait_ge(wi_copied, 1)
                        if h == 0:
                            dve.tensor_scalar(s, relu[m % 2][0:n, 0:k], wi, None, ALU.mult).then_inc(summed, 1)
                        else:
                            dve.wait_ge(summed, m)
                            dve.scalar_tensor_tensor(s, relu[m % 2][0:n, 0:k], wi, s, ALU.mult, ALU.add)\
                                .then_inc(summed, 1)
                        m += 1
                dve.wait_ge(turned, 2)
                for sg in range(2):
                    dve.tensor_tensor_reduce(out=core.wrow4[:, sg, :], in0=core.c["head"], in1=core.flat(7, 8)[:, 4 * sg:4 * sg + 4],
                                             scale=1.0, scalar=0.0, op0=ALU.mult, op1=ALU.add,
                                             accum_out=core.wrow[:, sg:sg + 1]).then_inc(own, 1)
                dve.wait_ge(own, 2)
                owner = core.c["owner"].rearrange("p (s h n) -> p s h n", s=2, h=2)
                for sg in range(2):
                    dve.tensor_scalar(core.wsel[:, sg, :, :], owner[:, sg, :, :], core.wrow[:, sg:sg + 1], None, ALU.mult)
                dve.memset(core.qibd[:].rearrange("p b n -> p (b n)"), 0.0).then_inc(own, 1)
                dve.wait_ge(own, 3)
                dve.wait_ge(swapped, 16 * 8)
                for half in range(2):
                    p = slice(64 * half, 64 * half + 64)
                    dst = core.qibd[p, :, 16 * half:16 * half + 16].rearrange("p b (h t) -> p b h t", h=NIH)
                    for h in range(NIH):
                        dve.tensor_copy(dst[:, :, h, :], core.qis[p, h, :].rearrange("p (b t) -> p b t", t=DS))

            @block.gpsimd
            def _(pool):
                pool.wait_ge(doubled, 16)
                for u in range(3):
                    pool.wait_ge(raw_copied, u + 1)
                    pool.tensor_tensor(rot[u], raw[u][:], core.c["cos"], ALU.mult).then_inc(cosined, 1)
                for i, qb in enumerate(blocks):
                    n, k = QROWS[qb], NK[qb]
                    pool.wait_ge(summed, NIH * (i + 1))
                    s = hd.s[0:n, SOFF[qb] + 128 * qb:SOFF[qb] + k]
                    pool.affine_select(out=s, in_=s, compare_op=ALU.is_ge, fill=NEG, base=0,
                                       pattern=[[-1, k - 128 * qb]], channel_multiplier=1).then_inc(masked, 1)


def sample_index_stage(nc, core, hd, ahead):
    r = At(nc, hd.behind_scores, Map.END)
    ring = 8
    kx = [r(f"kidx{s}", [128, RUN * HD]) for s in range(ring)]
    relu = [r(f"sample_relu{s}", [128, 512]) for s in range(4)]
    r0 = At(nc, Map.R0 + 4 * 4320, Map.R1 - 4096)
    kt = r0("kidx_turned", [128, 4, 512])
    new = r0("new_scores", [128, NS])
    src = core.i["cache_kidx"].rearrange("a n (s q) d -> (a n s) (q d)", q=RUN)
    rounds = 2 * NGA
    pairs = RUN // 2
    with ExitStack() as ctx:
        sem = Sems(nc, ctx, "sx")
        gathered = [sem(f"gathered{s}") for s in range(ring)]
        turned, copied_a, copied_d = sem("turned"), sem("copied_a"), sem("copied_d")
        scored, relued, summed, placed, own = sem("scored"), sem("relued"), sem("summed"), sem("placed"), sem("own")

        def weighted(pe, q):
            pe.wait_ge(relued, 2 * q + 2 if q < NGA else 2 * NGA + 1)
            after(pe, placed, q)
            g, width, halves = (q, 512, 2) if q < NGA else (3, NS, 1)
            for half in range(halves):
                for sg in range(2):
                    rows = relu[(2 * q + sg) % 4][:, 0:512] if q < NGA else relu[0][:, NS * sg:NS * sg + NS]
                    last = pe.matmul(core.flat(6 + half, width)[32 * g:32 * g + 32, :],
                                     core.wsel[:, sg, half, :], rows, start=(sg == 0), stop=(sg == 1))
            last.then_inc(summed, 1)

        with nc.Block() as block:

            @block.gpsimd
            def _(pool):
                for n in range(4 * rounds):
                    rnd, b4 = divmod(n, 4)
                    q, sg = divmod(rnd, 2)
                    if n >= ring:
                        pool.wait_ge(turned, 2 * (rnd - 2) + b4 // 2 + 1)
                    at = (4 * sg + b4) * NGA + q
                    pool.indirect_dma_start(
                        out=kx[n % ring][:], out_offset=None, in_=src,
                        in_offset=bass.IndirectOffsetOnAxis(ap=core.rows[:, at:at + 1], axis=0),
                    ).then_inc(gathered[n % ring], 16)
                for x in range(3):
                    ahead.lo(pool, x)
                for x in range(ring):
                    pool.wait_ge(gathered[x], 16 * NGA)

            @block.tensor
            def _(pe):
                for rnd in range(rounds + 1):
                    bank = 4 + rnd % 2
                    after(pe, relued, rnd - 1)
                    if rnd < rounds:
                        for b4 in range(4):
                            slot = (4 * rnd + b4) % ring
                            if b4 % 2 == 0:
                                after(pe, (copied_a, copied_d)[b4 // 2], rnd)
                            pe.wait_ge(gathered[slot], 16 * (rnd // 2 + 1))
                            for j in range(pairs):
                                last = pe.transpose(core.flat(b4, 512)[:, 128 * j:128 * j + 128],
                                                    kx[slot][:, 128 * j:128 * j + 128], core.c["ident"])
                            if b4 % 2:
                                last.then_inc(turned, 1)
                        if rnd % 2 == 0 and rnd:
                            weighted(pe, rnd // 2 - 1)
                        for b4 in range(4):
                            if b4 % 2 == 0:
                                pe.wait_ge((copied_a, copied_d)[b4 // 2], rnd + 1)
                            last = pe.matmul(core.flat(bank, 512)[32 * b4:32 * b4 + 32, :],
                                             core.qibd[:, 4 * (rnd % 2) + b4, :], kt[:, b4, :], start=True, stop=True)
                    else:
                        for sg in range(2):
                            last = pe.matmul(core.flat(bank, 512)[:, NS * sg:NS * sg + NS],
                                             core.qibd[0:HD, 4 * sg:4 * sg + 4, :].rearrange("p b n -> p (b n)"),
                                             core.kit[0:HD, TP:TOK], start=True, stop=True)
                    last.then_inc(scored, 1)
                weighted(pe, NGA - 1)
                weighted(pe, NGA)

            @block.scalar
            def _(act):
                for rnd in range(rounds + 1):
                    if rnd < rounds:
                        act.wait_ge(turned, 2 * rnd + 1)
                        after(act, scored, rnd)
                        act.activation(kt[:, 0:2, :].rearrange("p b n -> p (b n)"), core.flat(0, 1024), ACT.Copy)\
                            .then_inc(copied_a, 1)
                    act.wait_ge(scored, rnd + 1)
                    after(act, summed, rnd // 2 - 1)
                    n = 512 if rnd < rounds else 2 * NS
                    act.activation(relu[rnd % 4][:, 0:n], core.flat(4 + rnd % 2, n), ACT.Relu).then_inc(relued, 1)
                    ahead.hi(act, rnd - 3 if rnd >= 3 else 3)

            @block.vector
            def _(dve):
                dve.memset(hd.ss[0:96, SQ:SSW], NEG)
                for rnd in range(rounds + 1):
                    if rnd < rounds:
                        dve.wait_ge(turned, 2 * rnd + 2)
                        after(dve, scored, rnd)
                        dve.tensor_copy(kt[:, 2:4, :].rearrange("p b n -> p (b n)"), core.flat(2, 1024)).then_inc(copied_d, 1)
                    if rnd and rnd % 2 == 0:
                        q = rnd // 2 - 1
                        dve.wait_ge(summed, q + 1)
                        dst = hd.ss[32 * q:32 * q + 32, 0:SQ].rearrange("t (p j a) -> t a j p", j=pairs, a=2)
                        sums = core.flat(6, 1024)[32 * q:32 * q + 32, :].rearrange("t (a j p) -> t a j p", a=2, j=pairs)
                        dve.tensor_copy(dst, sums).then_inc(placed, 1)
                dve.wait_ge(summed, NGA + 1)
                dve.tensor_tensor(new[96:128, :], core.c["newkeep"][96:128, :], core.flat(6, NS)[96:128, :], ALU.mult)\
                    .then_inc(own, 1)
                dve.wait_ge(own, 1)
                dve.tensor_tensor(hd.ss[96:128, SQ:SSW], new[96:128, :], core.c["newfill"][96:128, :], ALU.add)


class Search:

    LINKS = 5 + NSEL - 1

    def __init__(self, core, hd, dve, own, counted, folded):
        self.core, self.hd, self.dve = core, hd, dve
        self.own, self.counted, self.folded = own, counted, folded
        self.at = 0

    def link(self, ins):
        ins.then_inc(self.own, 1)
        self.at = self.at + 1

    def sync(self):
        self.dve.wait_ge(self.own, self.at)

    def count(self, value, nth):
        hd = self.hd
        for x, i in enumerate([NSEL - 1, *range(NSEL - 1)]):
            n = hd.rows(i)
            part = hd.part(i)
            if x == 2:
                self.dve.wait_ge(self.counted, nth)
            elif x > 2:
                self.dve.wait_ge(self.own, self.at - 1)
            ins = self.dve.tensor_scalar(hd.junk[x % 2][0:n, 0:part.shape[1]], part, value(i, n), None,
                                         ALU.is_ge, ALU.add, accum_out=hd.count[0:n, i:i + 1])
            if x == 0:
                ins.then_inc(self.counted, 1)
            else:
                self.link(ins)

    def judge(self, steps):
        hd, last = self.hd, NSEL - 1
        self.dve.wait_ge(self.folded, steps)
        self.sync()
        self.dve.tensor_tensor(hd.enough[:, 0:last], hd.count[:, 0:last], hd.need[:, 0:last], ALU.is_ge)
        self.link(self.dve.tensor_tensor(hd.enough[:, last:], self.core.flat(6, 1), hd.need[:, last:], ALU.is_ge))
        self.sync()

    def start(self):
        hd, dve = self.hd, self.dve
        dve.memset(hd.count[:], 0.0)
        dve.memset(hd.need[:], float(TOPK))
        for i in range(NSEL):
            w = 4 * SSW if i == NSEL - 1 else NK[QB0 + i]
            dve.memset(hd.need0[:, i:i + 1], float(w - TOPK + 1))
            dve.memset(hd.need1[:, i:i + 1], float(TOPK - (w - TOPK + 1)))
        dve.memset(hd.kth[:], 0)
        self.link(dve.tensor_copy(hd.bit[:].bitcast(F32), self.core.c["bit"]))
        self.sync()
        self.count(lambda i, n: 0.0, 1)
        self.judge(1)
        dve.tensor_scalar(hd.sign[:], hd.enough[:], 2.0, -1.0, ALU.mult, ALU.add)
        self.link(dve.tensor_tensor(hd.need[:], hd.enough[:], hd.need1[:], ALU.mult))
        self.sync()
        self.link(dve.tensor_tensor(hd.need[:], hd.need[:], hd.need0[:], ALU.add))
        self.signed()
        self.propose(2)

    def signed(self):
        for i in range(NSEL):
            part, n = self.hd.part(i), self.hd.rows(i)
            self.link(self.dve.tensor_scalar(part, part, self.hd.sign[0:n, i:i + 1], None, ALU.mult))
        self.sync()

    def propose(self, nth):
        hd = self.hd
        self.link(self.dve.tensor_scalar(hd.cand[:], hd.kth[:], hd.bit[:], None, ALU.bitwise_or))
        self.sync()
        self.count(lambda i, n: hd.cand[0:n, i:i + 1].bitcast(F32), nth)

    def settle(self, steps):
        hd = self.hd
        self.judge(steps)
        self.link(self.dve.tensor_scalar(hd.cand[:], hd.enough[:], -1.0, None, ALU.mult))
        self.sync()
        self.link(self.dve.scalar_tensor_tensor(hd.kth[:], hd.cand[:], hd.bit[:], hd.kth[:], ALU.bitwise_and, ALU.bitwise_or))
        self.sync()
        self.link(self.dve.tensor_scalar(hd.bit[:], hd.bit[:], 1, None, ALU.logical_shift_right))
        self.sync()

    def step(self, steps):
        self.settle(steps)
        self.propose(steps + 1)


SEARCH_A = [1, 3, 5, 7, 9, 11]


def gate_stage(nc, core, hd, w):
    cc, p, u, bf = (hd.row[x][:, 0:TW] for x in range(4))
    p = hd.row[1]
    sg = hd.row[4][:, 0:TW]
    mb = [hd.row[x][:, 0:TW] for x in (5, 0)]
    sa = [hd.row[x][:, 0:TW] for x in (2, 3)]
    eq, cum = hd.row[4], hd.row[5]
    sout = nc.alloc_sbuf_tensor_at("conv_states_out", [18, CD], F32, offset=Map.R1 - 2048)
    r = At(nc, hd.after_search, Map.END)
    above, equal = r("above", [128, NSEL]), r("equal", [128, NSEL])
    opened = r("opened", [128, 4])
    kthf, left = r("kth_signed", [128, NSEL]), r("left", [128, NSEL])
    with ExitStack() as ctx:
        sem = Sems(nc, ctx, "gt")
        ready, free_a, free_d = sem("acc_ready"), sem("acc_free_a"), sem("acc_free_d")
        own, counted, folded = sem("own"), sem("counted"), sem("folded")
        tapped, b_ok, b_hi, b_lo = sem("tapped"), sem("b_ok"), sem("b_hi"), sem("b_lo")
        cx_ok, pads = sem("cx_ok"), sem("pads")
        mix_stored = [sem(f"mix_stored{s}") for s in range(2)]
        sig_stored = [sem(f"sig_stored{s}") for s in range(2)]
        states_turned, states_copied, states_stored = sem("states_turned"), sem("states_copied"), sem("states_stored")
        q_first = sem("q_first")
        states_ok, tied, tie_sums, causal = sem("states_ok"), sem("tied"), sem("tie_sums"), sem("causal")
        win, wpb = core.i["w_in"][0], core.i["w_pb"][0]
        A = 3 * CB
        B = A + 3 * KB
        first = [CCC, CXC, CBC]
        third = 2 + G
        pairs = KB // 2

        def masks(dve, find):
            find.link(dve.tensor_tensor(kthf[:], hd.kth[:].bitcast(F32), hd.sign[:], ALU.mult))
            find.signed()
            for s in range(2):
                dve.wait_ge(mix_stored[s], 16 * pairs + 1)
                dve.wait_ge(sig_stored[s], 16 * pairs + 1)
            dve.wait_ge(free_a, CB + 2 * KB)
            dve.memset(above[:], 0.0)
            find.link(dve.memset(equal[:], 0.0))
            find.sync()
            last = NSEL - 1
            for i in (last, *range(last)):
                part, n = hd.part(i), hd.rows(i)
                width = part.shape[1]
                e, s, kth = eq[0:n, 0:width], cum[0:n, 0:width], kthf[0:n, i:i + 1]
                dve.tensor_scalar(hd.junk[0][0:n, 0:width], part, kth, None, ALU.is_gt, ALU.add, accum_out=above[0:n, i:i + 1])
                ins = dve.tensor_scalar(e, part, kth, None, ALU.is_equal, ALU.add, accum_out=equal[0:n, i:i + 1])
                if i == last:
                    ins.then_inc(tied, 1)
                    dve.wait_ge(tied, 1)
                else:
                    find.link(ins)
                    find.sync()
                if i == last:
                    dve.wait_ge(tie_sums, 1)
                    find.link(dve.tensor_scalar(left[:, i:i + 1], core.flat(6, 2)[:, 0:1], -1.0, float(TOPK), ALU.mult, ALU.add))
                    find.sync()
                    find.link(dve.tensor_tensor(left[:, i:i + 1], left[:, i:i + 1], core.flat(6, 2)[:, 1:2], ALU.subtract))
                else:
                    find.link(dve.tensor_scalar(left[0:n, i:i + 1], above[0:n, i:i + 1], -1.0, float(TOPK), ALU.mult, ALU.add))
                find.link(dve.tensor_tensor_scan(s, core.onerow(n, width), e, 0.0, ALU.mult, ALU.add))
                find.sync()
                find.link(dve.scalar_tensor_tensor(s, s, left[0:n, i:i + 1], e, ALU.is_le, ALU.mult))
                find.sync()
                m = hd.smask[:] if i == last else hd.mask[0:n, MOFF[QB0 + i]:MOFF[QB0 + i] + width]
                find.link(dve.scalar_tensor_tensor(m, part, kth, s, ALU.is_le, ALU.subtract))
                find.sync()

        with nc.Block() as block:

            @block.sync
            def _(sp):
                for n in range(3, A):
                    col = first[n % 3] + 128 * (n // 3)
                    w.fetch(sp, n, n % 3, [((0, 1024, 128), by_rows(win, slice(col, col + 128)))])
                with sp.Fori(0, pairs) as i:
                    for part in range(6):
                        j, n = 2 * i + part // 3, A + 6 * i + part
                        col = 128 * j + (GBC, 0, GAC)[part % 3]
                        if part % 3 == 1:
                            col = (i + 1) * 256 + 128 * (part // 3) - 256
                            w.fetch(sp, n, 1, [((0, CB * 128, 128), by_rows(wpb, bass.ds(col, 128)))])
                        else:
                            w.fetch(sp, n, part % 3, [((0, 1024, 128), by_rows(win, bass.ds(col, 128)))])
                for m in range(2 + G):
                    n = B + m
                    if m < 2:
                        w.fetch(sp, n, n % 3, [((0, 1024, 128), by_rows(win, slice((KC, VC)[m], (KC, VC)[m] + 128)))])
                        continue
                    sp.wait_ge(w.lo_done, n - 2)
                    dst = core.wr[n % 3][:].rearrange("p (k v d) -> p k v d", k=KB, v=NKV)
                    for v in range(NKV):
                        head = QC + HD * (G * v + m - 2)
                        sp.dma_start(dst[:, :, v, :], by_rows(win, slice(head, head + HD)))\
                            .then_inc(w.arrived[n % 3] if v else q_first, 16)
                        if v == 0:
                            sp.wait_ge(q_first, 16 * (m - 1))
                sp.wait_ge(states_copied, 1)
                sp.dma_start(core.o["conv_prompt"][0, 0], sout[0:2, :]).then_inc(states_stored, 16)
                sp.dma_start(core.o["conv_sample"][0].rearrange("b w c -> (b w) c"), sout[2:18, :])\
                    .then_inc(states_stored, 16)
                sp.wait_ge(states_stored, 32)

            def fold(pe, n):
                pe.wait_ge(counted, n)
                pe.matmul(core.flat(6, 1), core.c["fold"], hd.count[:, NSEL - 1:NSEL], start=True, stop=True)\
                    .then_inc(folded, 1)

            @block.tensor
            def _(pe):
                folds = 1
                fold(pe, 1)
                for n in range(A):
                    if n >= 2:
                        c, k = divmod(n - 2, 3)
                        pe.wait_ge(*((free_a, c + 1) if k == 0 else (free_d, 2 * c + k)))
                    w.product(pe, n, n % 3, n % 2).then_inc(ready, 1)
                    if n == 1 or n - 2 in SEARCH_A:
                        folds += 1
                        fold(pe, folds)
                pe.wait_ge(b_lo, CB)
                assert folds == 7
                with pe.Fori(0, pairs) as i:
                    for part in range(6):
                        n = A + 6 * i + part
                        if part in (0, 3):
                            pe.wait_ge(free_d, 2 * CB + 2 * i + part // 3)
                        elif part == 1:
                            pe.wait_ge(free_a, CB + 4 * i)
                            pe.wait_ge(free_d, 2 * CB)
                        else:
                            pe.wait_ge(free_a, CB + 4 * i + {2: 1, 4: 2, 5: 3}[part])
                        if part % 3 == 1:
                            last = w.product(pe, n, 1, part % 2, CB, lambda k: hd.bh[:, k, :], lambda k: hd.bl[:, k, :])
                        elif part % 3 == 0:
                            last = w.product(pe, n, 0, part % 2, before=lambda k: k == 7 and fold(pe, 8 + 6 * i + part))
                        else:
                            last = w.product(pe, n, 2, part % 2, before=lambda k: k == 2 and fold(pe, 7 + 6 * i + part))
                        last.then_inc(ready, 1)
                        if part % 3 == 2:
                            fold(pe, 8 + 6 * i + part)
                for m in range(third):
                    n = B + m
                    if m == 0:
                        pe.wait_ge(free_d, 2 * CB + KB)
                    else:
                        pe.wait_ge(free_a, CB + 2 * KB + m - 1)
                    w.product(pe, n, n % 3, n % 2).then_inc(ready, 1)
                    if m == 1:
                        fold(pe, 8 + 24)
                    if m == 2:
                        pe.wait_ge(tied, 1)
                        pe.matmul(core.flat(6, 2)[:, 0:1], core.c["fold"], above[:, NSEL - 1:NSEL], start=True, stop=True)
                        pe.matmul(core.flat(6, 2)[:, 1:2], core.c["below"], equal[:, NSEL - 1:NSEL], start=True, stop=True)\
                            .then_inc(tie_sums, 1)
                pe.wait_ge(states_ok, CB)
                for c in range(CB):
                    last = pe.transpose(core.flat(7, CD, 18)[:, 128 * c:128 * c + 128], hd.cs[:, c, :], core.c["ident"])
                last.then_inc(states_turned, 1)

            @block.scalar
            def _(act):
                for n in range(A):
                    c, k = divmod(n, 3)
                    if k == 0:
                        act.wait_ge(ready, n + 1)
                        after(act, cx_ok, c)
                        act.activation(tri(cc), core.acc(n % 2), ACT.Copy).then_inc(free_a, 1)
                    if k == 2:
                        act.wait_ge(b_ok, c + 1)
                        act.activation(hd.bh[:, c, :], bf, ACT.Copy).then_inc(b_hi, 1)
                    w.hi(act, n + 3, n % 3, 16 * (n // 3 + 2), ready)
                act.wait_ge(b_lo, CB)
                with act.Fori(0, pairs) as i:
                    for part in range(6):
                        n, k, jj = A + 6 * i + part, part % 3, part // 3
                        if k == 0:
                            act.wait_ge(ready, n + 1)
                            act.wait_ge(free_d, 2 * CB + 2 * i + jj)
                            act.activation(tri(sg), core.acc(part % 2), ACT.Sigmoid).then_inc(free_a, 1)
                        if k == 2:
                            act.wait_ge(ready, n + 1)
                            act.wait_ge(sig_stored[jj], 16 * i + 1)
                            act.activation(tri(sa[jj]), core.acc(part % 2), ACT.Sigmoid).then_inc(free_a, 1)
                        w.hi(act, n + 3, k, 16 * (CB + 2 * i + jj + 2), ready)
                        row = act.snap(2 * i + jj)
                        if k == 1:
                            act.wait_ge(free_d, 2 * CB + 2 * i + jj + 1)
                            act.dma_start(core.mixb.ap()[bass.ds(row, 1)].rearrange("a p n -> p (a n)"), mb[jj])\
                                .then_inc(mix_stored[jj], 16)
                        if k == 2:
                            act.wait_ge(free_a, CB + 4 * i + 2 * jj + 2)
                            act.dma_start(core.siga.ap()[bass.ds(row, 1)].rearrange("a p n -> p (a n)"), sa[jj])\
                                .then_inc(sig_stored[jj], 16)
                for m in range(third):
                    n = B + m
                    act.wait_ge(ready, n + 1)
                    act.mul(tri(hd.raw[m][:]), core.acc(n % 2), 1.0 if m < 2 else SM).then_inc(free_a, 1)
                    if m + 3 < third:
                        w.hi(act, n + 3, n % 3, 16 * (B // 3 + 2), ready)
                act.wait_ge(states_turned, 1)
                act.activation(sout[:], core.flat(7, CD, 18), ACT.Copy).then_inc(states_copied, 1)

            @block.gpsimd
            def _(pool):
                pool.memset(p[:, 0:2], 0.0).then_inc(pads, 1)
                for x, stored in enumerate((*mix_stored, *sig_stored)):
                    pool.memset(opened[:, x:x + 1], 0.0).then_inc(stored, 1)
                for n in range(A):
                    c, k = divmod(n, 3)
                    if k == 1:
                        pool.wait_ge(cx_ok, c + 1)
                        after(pool, b_ok, c)
                        pool.tensor_scalar(u[:, 0:TP], p[:, 0:TP], core.conv[:, c, 16:17], None, ALU.mult)\
                            .then_inc(tapped, 1)
                    if k == 2:
                        pool.wait_ge(b_hi, c + 1)
                        pool.tensor_tensor(hd.bl[:, c, :], bf, hd.bh[:, c, :].bitcast(F32), ALU.subtract)\
                            .then_inc(b_lo, 1)
                    w.lo(pool, n + 3, n % 3)
                with pool.Fori(0, pairs) as i:
                    for part in range(6):
                        n, k, jj = A + 6 * i + part, part % 3, part // 3
                        w.lo(pool, n + 3, k)
                for m in range(3):
                    w.lo(pool, B + m + 3, m)
                for s in range(2):
                    pool.wait_ge(mix_stored[s], 16 * pairs + 1)
                    pool.wait_ge(sig_stored[s], 16 * pairs + 1)
                pool.memset(hd.mask[:, 0:MOFF[QB0]], 0.0).then_inc(causal, 1)
                pool.wait_ge(causal, 1)
                for qb in range(QB0):
                    at = MOFF[qb] + 128 * qb
                    last = pool.affine_select(out=hd.mask[:, at:at + 128], in_=hd.mask[:, at:at + 128], compare_op=ALU.is_ge,
                                              fill=1.0, base=0, pattern=[[-1, 128]], channel_multiplier=1)
                last.then_inc(causal, 1)
                pool.wait_ge(causal, 2)

            @block.vector
            def _(dve):
                find = Search(core, hd, dve, own, counted, folded)
                find.start()
                steps = 1
                dve.wait_ge(pads, 1)
                for n in range(A):
                    c, k = divmod(n, 3)
                    if k == 1:
                        tap = [core.conv[:, c, 16 + x:17 + x] for x in range(3)]
                        dve.wait_ge(ready, n + 1)
                        dve.wait_ge(free_a, c + 1)
                        if c >= 1:
                            find.sync()
                        dve.tensor_tensor(tri(p[:, 2:2 + TW]), tri(cc), core.acc(n % 2), ALU.mult).then_inc(free_d, 1)
                        dve.wait_ge(free_d, 2 * c + 1)
                        dve.tensor_copy(hd.p6[:, :, 0:2], core.conv[:, c, 0:16].rearrange("p (b w) -> p b w", w=2))
                        dve.tensor_copy(hd.p6[:, :, 2:6], p[:, 2 + TP:2 + TOK].rearrange("p (b t) -> p b t", t=DS))\
                            .then_inc(cx_ok, 1)
                        dve.wait_ge(cx_ok, c + 1)
                        dve.tensor_copy(hd.cs[:, c, 0:2], p[:, TP:TP + 2])
                        dve.tensor_copy(hd.cs[:, c, 2:18].rearrange("p (b w) -> p b w", w=2), hd.p6[:, :, 4:6])\
                            .then_inc(states_ok, 1)
                        us = u[:, TP:TOK].rearrange("p (b t) -> p b t", t=DS)
                        if c == 0:
                            find.link(dve.memset(u[:, TOK:TW], 0.0))
                        find.link(dve.tensor_scalar(us, hd.p6[:, :, 0:4], tap[0], None, ALU.mult))
                        dve.wait_ge(tapped, c + 1)
                        for x in (1, 2):
                            find.sync()
                            dve.scalar_tensor_tensor(u[:, 0:TP], p[:, x:x + TP], tap[x], u[:, 0:TP], ALU.mult, ALU.add)
                            find.link(dve.scalar_tensor_tensor(us, hd.p6[:, :, x:x + 4], tap[x], us, ALU.mult, ALU.add))
                    if k == 2:
                        dve.wait_ge(ready, n + 1)
                        find.sync()
                        after(dve, b_lo, c)
                        dve.tensor_tensor(tri(bf), tri(u), core.acc(n % 2), ALU.mult).then_inc(free_d, 1)
                        dve.wait_ge(free_d, 2 * c + 2)
                        dve.tensor_copy(hd.p6[:, 0, 0:1], hd.p6[:, 0, 0:1]).then_inc(b_ok, 1)
                    if n in SEARCH_A:
                        steps += 1
                        find.step(steps)
                at0 = find.at
                with dve.Fori(0, pairs) as i:
                    find.at = at0 + 6 * Search.LINKS * i
                    for part in range(6):
                        n, k, jj = A + 6 * i + part, part % 3, part // 3
                        if k == 1:
                            dve.wait_ge(ready, n + 1)
                            dve.wait_ge(free_a, CB + 4 * i + 2 * jj + 1)
                            dve.wait_ge(mix_stored[jj], 16 * i + 1)
                            dve.tensor_tensor(tri(mb[jj]), tri(sg), core.acc(part % 2), ALU.mult).then_inc(free_d, 1)
                        find.step(8 + 6 * i + part)
                find.at = at0 + 6 * Search.LINKS * pairs
                find.settle(8 + 24)
                masks(dve, find)


def rope_stage(nc, core, hd):
    r1 = At(nc, Map.R1, Map.R1 + 22528)
    tmp = [r1(f"sined{u}", [128, TW]) for u in range(2)]
    k_out = r1("k_out", [128, NT, 128])
    s_out = r1("k_samples_out", [NS, 128])
    raw = [hd.raw[0], *hd.raw[2:]]
    dst = [hd.k[:], *(hd.q[:, g, :] for g in range(G))]
    count = len(raw)
    with ExitStack() as ctx:
        sem = Sems(nc, ctx, "ro")
        partner, sined, cosined, roped = sem("partner"), sem("sined"), sem("cosined"), sem("roped")
        v_turned, v_copied, k_turned, k_copied = sem("v_turned"), sem("v_copied"), sem("k_turned"), sem("k_copied")
        stored, zeroed, hi, v_hi = sem("stored"), sem("zeroed"), sem("hi"), sem("v_hi")
        v_parts = [(slice(0, 128), slice(0, NT - 1)), (slice(0, QROWS[-1]), slice(NT - 1, NT))]

        def low(dve, u):
            dve.wait_ge(hi, u + 1)
            dve.tensor_tensor(hd.kql[u][:], dst[u], hd.kqh[u][:].bitcast(F32), ALU.subtract)

        def turn(pe, src, turned, copied):
            for i in range(3):
                if i == 2:
                    pe.wait_ge(copied, 1)
                if i < 2:
                    for t in range(4):
                        last = pe.transpose(core.flat(6 + i, 512)[:, 128 * t:128 * t + 128],
                                            src[:, 512 * i + 128 * t:512 * i + 128 * t + 128], core.c["ident"])
                else:
                    pe.transpose(core.flat(6, 128, ROWS[8]), src[:, 1024:TOK], core.c["ident"])
                    last = pe.transpose(core.flat(6, 256, NS)[:, 128:256], src[:, TP:TOK], core.c["ident"])
                last.then_inc(turned, 1)

        def untwist(act, turned, copied, dst, samples):
            for i in range(2):
                act.wait_ge(turned, i + 1)
                act.activation(dst[:, 4 * i:4 * i + 4, :].rearrange("p t d -> p (t d)"), core.flat(6 + i, 512), ACT.Copy)\
                    .then_inc(copied, 1)
            act.wait_ge(turned, 3)
            act.activation(dst[0:ROWS[8], 8, :], core.flat(6, 128, ROWS[8]), ACT.Copy)
            act.activation(samples, core.flat(6, 256, NS)[:, 128:256], ACT.Copy).then_inc(copied, 1)

        with nc.Block() as block:

            @block.tensor
            def _(pe):
                for u in range(count):
                    if u >= 2:
                        pe.wait_ge(sined, u - 1)
                    for c in range(3):
                        last = pe.matmul(core.acc(u % 2)[:, c, :], core.c["perm"], raw[u][:, c * CH:(c + 1) * CH],
                                         start=True, stop=True)
                    last.then_inc(partner, 1)
                    if u == 1:
                        turn(pe, hd.raw[1], v_turned, v_copied)
                pe.wait_ge(roped, 1)
                pe.wait_ge(v_copied, 3)
                turn(pe, hd.k, k_turned, k_copied)

            @block.scalar
            def _(act):
                for u in range(count):
                    act.wait_ge(roped, u + 1)
                    act.activation(hd.kqh[u][:], dst[u], ACT.Copy).then_inc(hi, 1)
                    if u == 0:
                        untwist(act, v_turned, v_copied, hd.v, hd.vs[:])
                act.wait_ge(v_copied, 3)
                for rows, tiles in v_parts:
                    ins = act.activation(hd.vh[rows, tiles, :], hd.v[rows, tiles, :], ACT.Copy)
                ins.then_inc(v_hi, 1)
                untwist(act, k_turned, k_copied, k_out, s_out[:])

            @block.gpsimd
            def _(pool):
                for u in range(count):
                    pool.tensor_tensor(dst[u], raw[u][:], core.c["cos"], ALU.mult).then_inc(cosined, 1)
                low(pool, 0)
                low(pool, 1)
                pool.wait_ge(v_hi, 1)
                for rows, tiles in v_parts:
                    pool.tensor_tensor(hd.vl[rows, tiles, :], hd.v[rows, tiles, :],
                                       hd.vh[rows, tiles, :].bitcast(F32), ALU.subtract)

            @block.vector
            def _(dve):
                dve.memset(hd.qs[:].rearrange("p b n -> p (b n)"), 0.0).then_inc(zeroed, 1)
                for u in range(count):
                    dve.wait_ge(partner, u + 1)
                    if u >= 2:
                        dve.wait_ge(roped, u - 1)
                    dve.tensor_tensor(tri(tmp[u % 2][:]), tri(core.c["sin"]), core.acc(u % 2), ALU.mult).then_inc(sined, 1)
                    dve.wait_ge(cosined, u + 1)
                    dve.wait_ge(sined, u + 1)
                    dve.tensor_tensor(dst[u], dst[u], tmp[u % 2][:], ALU.add).then_inc(roped, 1)
                    if u >= 3:
                        low(dve, u - 1)
                low(dve, count - 1)
                dve.wait_ge(zeroed, 1)
                dve.wait_ge(roped, count)
                for v in range(NKV):
                    p = slice(64 * v, 64 * v + 64)
                    for g in range(G):
                        at = 16 * v + 4 * g
                        dve.tensor_copy(hd.qs[p, :, at:at + 4], hd.q[p, g, TP:TOK].rearrange("p (b t) -> p b t", t=DS))

            @block.sync
            def _(sp):
                def store(out, rows, samples, copied):
                    sp.wait_ge(copied, 3)
                    prompt = core.o[f"{out}_prompt"][0, 0].rearrange("t v d -> t (v d)")
                    sp.dma_start(prompt[0:1024].rearrange("(t p) d -> p t d", p=128), rows[:, 0:8, :]).then_inc(stored, 16)
                    sp.dma_start(prompt[1024:TP], rows[0:QROWS[8], 8, :]).then_inc(stored, 16)
                    sp.dma_start(core.o[f"{out}_sample"][0].rearrange("b s v d -> (b s) (v d)"), samples)\
                        .then_inc(stored, 16)
                store("v", hd.v, hd.vs[:], v_copied)
                store("k", k_out, s_out[:], k_copied)
                sp.wait_ge(stored, 96)


def result_buffers(nc, core):
    core.rh = nc.alloc_sbuf_tensor_at("attention_hi", [128, G, TW], F32R, offset=Map.R0)
    core.rl = nc.alloc_sbuf_tensor_at("attention_lo", [128, G, TW], F32R, offset=Map.R0 + G * TW * 4)


def prompt_attention_stage(nc, core, hd):
    result_buffers(nc, core)
    steps = NT * H
    r1 = At(nc, Map.R1, Map.R1 + 22528)
    probs = [r1(f"probs{s}", [128, TP]) for s in range(4)]
    top, sums, inv = (r1(name, [128, steps]) for name in ("minus_max", "sums", "inverse_sums"))
    w = At(nc, Map.W, Map.C)
    ph = w("probs_turned_hi", [128, NT, G, 128], F32R)
    pl = w("probs_turned_lo", [128, NT, G, 128], F32R)
    ident = core.c["ident"]
    with ExitStack() as ctx:
        sem = Sems(nc, ctx, "pa")
        logits, maxed, probs_ok, inverted, normed = (
            sem("logits"), sem("maxed"), sem("probs_ok"), sem("inverted"), sem("normed"))
        turned, hi, lo, valued = sem("turned"), sem("hi"), sem("lo"), sem("valued")
        r_hi, r_lo = sem("r_hi"), sem("r_lo")

        def of(i):
            qb, h = divmod(i, H)
            return qb, h // G, h % G

        def bank(i):
            return 0 if of(i)[0] == NT - 1 else 2 * (i % 2)

        def pieces(j):
            qb = of(j)[0]
            if qb < 4:
                return [(4, range(0, qb + 1), 128)]
            if qb < NT - 1:
                return [(4, range(0, 4), 128), (5, range(4, qb + 1), 128)]
            return [(4, range(0, qb), 128), (5, range(qb, qb + 1), NK[qb] - 128 * qb)]

        before = [0]
        for j in range(steps):
            before.append(before[-1] + len(pieces(j)))

        def piece(j, x):
            b, tiles, rows = pieces(j)[x]
            qb, v, g = of(j)
            n, count = QROWS[qb], len(tiles)
            src = core.flat(b, count * n, rows).rearrange("p (k n) -> p k n", n=n)
            at = (slice(0, rows), slice(tiles[0], tiles[-1] + 1), g, slice(0, n))
            return src, ph[at], pl[at]

        def result(of_what, group):
            qb, v = divmod(group, NKV)
            n, p = QROWS[qb], slice(64 * v, 64 * v + 64)
            src = core.flat(6 + group % 2, G * n)[p, :].rearrange("p (g n) -> p g n", g=G)
            return of_what[p, :, 128 * qb:128 * qb + n], src

        with nc.Block() as block:

            @block.tensor
            def _(pe):
                for i in range(steps + 5):
                    if i < steps:
                        qb, v, g = of(i)
                        n, p = QROWS[qb], slice(64 * v, 64 * v + 64)
                        after(pe, probs_ok, i if qb == NT - 1 else i - 1)
                        for a, width in chunks(NK[qb]):
                            out = core.flat(bank(i), NK[qb], n)[:, a:a + width]
                            pe.matmul(out, core.identb[0:n, 0:n], hd.mask[0:n, MOFF[qb] + a:MOFF[qb] + a + width],
                                      start=True, stop=False)
                            for x, (q, k) in enumerate(((hd.kqh, hd.kqh), (hd.kqh, hd.kql), (hd.kql, hd.kqh))):
                                last = pe.matmul(out, q[1 + g][p, 128 * qb:128 * qb + n], k[0][p, a:a + width],
                                                 start=False, stop=(x == 2))
                        last.then_inc(logits, 1)
                    if i >= 4 and (i - 4) % G == G - 1:
                        group = (i - 4) // G
                        qb = group // NKV
                        n = QROWS[qb]
                        pe.wait_ge(lo, before[G * (group + 1)])
                        after(pe, r_lo, group - 1)
                        for k in range(qb + 1):
                            rows = min(128, NK[qb] - 128 * k)
                            for x, (a, b) in enumerate(((hd.vh, ph), (hd.vh, pl), (hd.vl, ph))):
                                last = pe.matmul(core.flat(6 + group % 2, G * n).rearrange("p (g n) -> p g n", g=G),
                                                 a[0:rows, k, :], b[0:rows, k, :, 0:n],
                                                 start=(k == 0 and x == 0), stop=(k == qb and x == 2))
                        last.then_inc(valued, 1)
                    if 0 <= i - 3 < steps:
                        j = i - 3
                        n = QROWS[of(j)[0]]
                        pe.wait_ge(normed, j + 1)
                        after(pe, lo, before[j])
                        for b, tiles, rows in pieces(j):
                            for k in tiles:
                                at = n * (k - tiles[0])
                                last = pe.transpose(core.flat(b, 512, rows)[:, at:at + n],
                                                    probs[j % 4][0:n, 128 * k:128 * k + rows], ident[0:n, 0:n])
                            last.then_inc(turned, 1)

            @block.scalar
            def _(act):
                for i in range(steps + 5):
                    if 0 <= i - 4 < steps:
                        j = i - 4
                        after(act, valued, j // G)
                        for x in range(len(pieces(j))):
                            act.wait_ge(turned, before[j] + x + 1)
                            src, high, _ = piece(j, x)
                            act.activation(high, src, ACT.Copy).then_inc(hi, 1)
                    if 0 <= i - 1 < steps:
                        j = i - 1
                        qb = of(j)[0]
                        n, k = QROWS[qb], NK[qb]
                        act.wait_ge(maxed, j + 1)
                        if j >= 4:
                            act.wait_ge(turned, before[j - 3])
                        act.activation(probs[j % 4][0:n, 0:k], core.flat(bank(j), k, n), ACT.Exp,
                                       bias=top[0:n, j:j + 1], accum_out=sums[0:n, j:j + 1]).then_inc(probs_ok, 1)
                    if i >= 4 and (i - 4) % G == G - 1:
                        group = (i - 4) // G
                        act.wait_ge(valued, group + 1)
                        dst, src = result(core.rh, group)
                        act.activation(dst, src, ACT.Copy).then_inc(r_hi, 1)

            @block.vector
            def _(dve):
                for i in range(steps + 5):
                    if 0 <= i - 4 < steps:
                        j = i - 4
                        for x in range(len(pieces(j))):
                            dve.wait_ge(hi, before[j] + x + 1)
                            src, high, low = piece(j, x)
                            dve.tensor_tensor(low, src, high.bitcast(F32), ALU.subtract).then_inc(lo, 1)
                    if i < steps:
                        qb = of(i)[0]
                        n, k = QROWS[qb], NK[qb]
                        dve.wait_ge(logits, i + 1)
                        dve.tensor_reduce(top[0:n, i:i + 1], core.flat(bank(i), k, n), AX.X, ALU.max, negate=True)\
                            .then_inc(maxed, 1)
                    if 0 <= i - 2 < steps:
                        j = i - 2
                        qb = of(j)[0]
                        n = QROWS[qb]
                        row = probs[j % 4][0:n, 0:NK[qb]]
                        dve.wait_ge(probs_ok, j + 1)
                        dve.reciprocal(inv[0:n, j:j + 1], sums[0:n, j:j + 1]).then_inc(inverted, 1)
                        dve.wait_ge(inverted, j + 1)
                        dve.tensor_scalar(row, row, inv[0:n, j:j + 1], None, ALU.mult).then_inc(normed, 1)
                    if i >= 4 and (i - 4) % G == G - 1:
                        group = (i - 4) // G
                        dve.wait_ge(r_hi, group + 1)
                        dst, src = result(core.rl, group)
                        high, _ = result(core.rh, group)
                        dve.tensor_tensor(dst, src, high.bitcast(F32), ALU.subtract).then_inc(r_lo, 1)


def sample_attention_stage(nc, core, hd, ahead):
    r1 = At(nc, Map.R1, Map.W)
    ring = 8
    got = [r1(f"gathered_kv{s}", [128, RUN * 128]) for s in range(ring)]
    probs0 = r1("sample_probs0", [128, PAST + NS])
    probs1 = r1("sample_probs1", [128, PAST + NS])
    probs = [probs0, probs1]
    pt_new = r1("new_probs_turned", [NS, 128])
    r2 = At(nc, hd.end, Map.END)
    kt = r2("keys_turned", [128, 4, GRP])
    pt = [r2(f"sample_probs_turned{s}", [128, 4, 128]) for s in range(2)]
    tops = r2("sample_maxima", [128, 2, NGRP + 1])
    top = r2("sample_top", [128, 2])
    sums = r2("sample_sums", [128, 2])
    inv = r2("sample_inverse", [128, 2])
    assert Map.W >= r1.at
    keys = core.i["cache_k"].rearrange("a n (s q) v d -> (a n s) (q v d)", q=RUN)
    values = core.i["cache_v"].rearrange("a n (s q) v d -> (a n s) (q v d)", q=RUN)
    rounds = 2 * NGRP
    items = NGRP + 1
    ident = core.c["ident"]
    place = core.place[:]
    with ExitStack() as ctx:
        sem = Sems(nc, ctx, "sa")
        gathered = [sem(f"gathered{s}") for s in range(ring)]
        turned, copied_a, copied_d = sem("keys_turned"), sem("copied_a"), sem("copied_d")
        logits, kept, maxed, topped = sem("logits"), sem("kept"), sem("maxed"), sem("topped")
        exped, inverted, normed = sem("exped"), sem("inverted"), sem("normed")
        p_turned, p_copied, valued = sem("probs_turned"), sem("probs_copied"), sem("valued")
        r_hi, r_lo, own = sem("r_hi"), sem("r_lo"), sem("own")
        padded = sem("padded")

        def half(r, s):
            at = 128 * (4 * (r % 2) + s)
            return slice(at, at + 128)

        def value_item(r):
            return r // NGRP * items + r % NGRP

        def diagonal(result, sg, v):
            p = slice(64 * v, 64 * v + 64)
            src = core.flat(7 - 2 * sg, 128)[p, :].rearrange("p (b v g t) -> p v g b t", b=4, v=NKV, g=G)[:, v]
            at = TP + 16 * sg
            return result[p, :, at:at + 16].rearrange("p g (b t) -> p g b t", t=DS), src

        with nc.Block() as block:

            @block.sync
            def _(sp):
                sp.wait_ge(logits, rounds + 1)
                ahead.fetch(sp)

            @block.gpsimd
            def _(pool):
                pool.memset(core.rh[:, :, TOK:TW].bitcast(F32), 0.0)
                pool.memset(core.rl[:, :, TOK:TW].bitcast(F32), 0.0).then_inc(padded, 1)
                for n in range(2 * rounds // 2):
                    for b4 in range(4):
                        slot = 4 * (n % 2) + b4
                        sg, grp = divmod(n % NGRP, NGA)
                        if n >= 2:
                            if n - 2 < NGRP:
                                pool.wait_ge(turned, 2 * (2 * (n - 2) + 1) + 1 + b4 // 2)
                            else:
                                pool.wait_ge(valued, value_item(2 * (n - 2 - NGRP) + 1) + 1)
                        at = (4 * sg + b4) * NGA + grp
                        pool.indirect_dma_start(
                            out=got[slot][:], out_offset=None, in_=keys if n < NGRP else values,
                            in_offset=bass.IndirectOffsetOnAxis(ap=core.rows[:, at:at + 1], axis=0),
                        ).then_inc(gathered[slot], 16)
                for n in range(3):
                    ahead.lo(pool, n)
                for slot in range(ring):
                    pool.wait_ge(gathered[slot], 16 * NGRP)
                pool.wait_ge(padded, 1)

            @block.tensor
            def _(pe):
                for sg in range(2):
                    out = core.flat(6, 512)[:, NS * sg:NS * sg + NS]
                    pe.matmul(out, place[96:128, sg, :], hd.smask[96:128, SQ:SSW], start=True, stop=False,
                              tile_position=(96, 0))
                    for b4 in range(4):
                        last = pe.matmul(out[32 * b4:32 * b4 + 32, :], hd.qs[:, 4 * sg + b4, :], hd.k[:, TP:TOK],
                                         start=False, stop=True)
                last.then_inc(logits, 1)
                for r in range(rounds + 1):
                    if r < rounds:
                        for b4 in range(4):
                            slot = 4 * (r // 2 % 2) + b4
                            if b4 % 2 == 0:
                                after(pe, (copied_a, copied_d)[b4 // 2], r)
                            pe.wait_ge(gathered[slot], 16 * (r // 4 + 1))
                            for s in range(4):
                                last = pe.transpose(core.flat(b4, 512)[:, 128 * s:128 * s + 128],
                                                    got[slot][:, half(r, s)], ident)
                            if b4 % 2:
                                last.then_inc(turned, 1)
                    if r >= 1:
                        j = r - 1
                        sg, grp = divmod(j, NGRP)
                        q = 32 * (grp // 2)
                        pe.wait_ge(copied_a, j + 1)
                        pe.wait_ge(copied_d, j + 1)
                        after(pe, kept, j if j >= 2 else 0)
                        out = core.flat(4 + j % 2, 512)
                        order = hd.smask[q:q + 32, 0:SQ].rearrange("t (p h s) -> t h s p", h=2, s=4)[:, grp % 2]
                        pe.matmul(out, place[q:q + 32, sg, :], order, start=True, stop=False, tile_position=(q, 0))
                        for b4 in range(4):
                            last = pe.matmul(out[32 * b4:32 * b4 + 32, :], hd.qs[:, 4 * sg + b4, :], kt[:, b4, :],
                                             start=False, stop=True)
                        last.then_inc(logits, 1)
                for n in range(2 * items + 1):
                    if n < 2 * items:
                        sg, grp = divmod(n, items)
                        bank = 6 if n % 2 else 4
                        if n < 2:
                            pe.wait_ge(kept, rounds + 1)
                        pe.wait_ge(normed, sg + 1)
                        after(pe, p_copied, n - 1)
                        if grp < NGRP:
                            for s in range(4):
                                at = GRP * grp + 128 * s
                                last = pe.transpose(core.flat(bank, 512)[:, 128 * s:128 * s + 128],
                                                    probs[sg][:, at:at + 128], ident)
                        else:
                            last = pe.transpose(core.flat(bank, 128, NS), probs[sg][:, PAST:PAST + NS], ident)
                        last.then_inc(p_turned, 1)
                    if n >= 1:
                        j = n - 1
                        sg, grp = divmod(j, items)
                        out = core.flat(7 - 2 * sg, 128)
                        pe.wait_ge(p_copied, j + 1)
                        if grp < NGRP:
                            r = rounds + sg * NGRP + grp
                            for b4 in range(4):
                                slot = 4 * (r // 2 % 2) + b4
                                pe.wait_ge(gathered[slot], 16 * (r // 4 + 1))
                                for s in range(4):
                                    last = pe.matmul(out[:, 32 * b4:32 * b4 + 32], got[slot][:, half(r, s)],
                                                     pt[j % 2][:, s, 32 * b4:32 * b4 + 32],
                                                     start=(grp == 0 and b4 == 0 and s == 0), stop=False,
                                                     skip_group_check=True)
                        else:
                            last = pe.matmul(out, hd.vs[:], pt_new[:], start=False, stop=True, skip_group_check=True)
                        last.then_inc(valued, 1)

            @block.scalar
            def _(act):
                act.wait_ge(logits, 1)
                act.activation(probs[0][:, PAST:PAST + NS], core.flat(6, NS), ACT.Copy)
                act.activation(probs[1][:, PAST:PAST + NS], core.flat(6, 2 * NS)[:, NS:2 * NS], ACT.Copy).then_inc(kept, 1)
                for r in range(rounds + 1):
                    if r < rounds:
                        act.wait_ge(turned, 2 * r + 1)
                        after(act, logits, r + 1 if r else 0)
                        act.activation(kt[:, 0:2, :].rearrange("p b n -> p (b n)"), core.flat(0, 1024), ACT.Copy)\
                            .then_inc(copied_a, 1)
                    if r >= 1:
                        sg, grp = divmod(r - 1, NGRP)
                        act.wait_ge(logits, r + 1)
                        act.activation(probs[sg][:, GRP * grp:GRP * grp + GRP], core.flat(4 + (r - 1) % 2, 512), ACT.Copy)\
                            .then_inc(kept, 1)
                    if r in (NGRP, rounds):
                        sg = r // NGRP - 1
                        act.wait_ge(kept, r + 1)
                        act.wait_ge(topped, sg + 1)
                        act.activation(probs[sg][:], probs[sg][:], ACT.Exp, bias=top[:, sg:sg + 1],
                                       accum_out=sums[:, sg:sg + 1]).then_inc(exped, 1)
                for n in range(2 * items):
                    if n >= items:
                        ahead.hi(act, n - items)
                    sg, grp = divmod(n, items)
                    act.wait_ge(p_turned, n + 1)
                    after(act, valued, n - 1)
                    bank = 6 if n % 2 else 4
                    if grp < NGRP:
                        act.activation(pt[n % 2][:].rearrange("p s n -> p (s n)"), core.flat(bank, 512), ACT.Copy)\
                            .then_inc(p_copied, 1)
                    else:
                        after(act, valued, n - items)
                        act.activation(pt_new[:], core.flat(bank, 128, NS), ACT.Copy).then_inc(p_copied, 1)
                        act.wait_ge(valued, n + 1)
                        for v in range(NKV):
                            dst, src = diagonal(core.rh, sg, v)
                            ins = act.activation(dst, src, ACT.Copy)
                        ins.then_inc(r_hi, 1)

            @block.vector
            def _(dve):
                dve.wait_ge(kept, 1)
                for sg in range(2):
                    ins = dve.tensor_reduce(tops[:, sg, NGRP:NGRP + 1], probs[sg][:, PAST:PAST + NS], AX.X, ALU.max)
                ins.then_inc(maxed, 1)
                for r in range(rounds + 1):
                    if r < rounds:
                        dve.wait_ge(turned, 2 * r + 2)
                        after(dve, logits, r + 1 if r else 0)
                        dve.tensor_copy(kt[:, 2:4, :].rearrange("p b n -> p (b n)"), core.flat(2, 1024)).then_inc(copied_d, 1)
                    if r >= 1:
                        sg, grp = divmod(r - 1, NGRP)
                        dve.wait_ge(kept, r + 1)
                        dve.tensor_reduce(tops[:, sg, grp:grp + 1], probs[sg][:, GRP * grp:GRP * grp + GRP], AX.X, ALU.max)\
                            .then_inc(maxed, 1)
                    if r in (NGRP, rounds):
                        sg = r // NGRP - 1
                        dve.wait_ge(maxed, r + 1)
                        dve.tensor_reduce(top[:, sg:sg + 1], tops[:, sg, :], AX.X, ALU.max, negate=True).then_inc(topped, 1)
                    if r in (NGRP + 2, rounds):
                        sg = 0 if r < rounds else 1
                        dve.wait_ge(exped, sg + 1)
                        dve.reciprocal(inv[:, sg:sg + 1], sums[:, sg:sg + 1]).then_inc(inverted, 1)
                        dve.wait_ge(inverted, sg + 1)
                        dve.tensor_scalar(probs[sg][:], probs[sg][:], inv[:, sg:sg + 1], None, ALU.mult).then_inc(normed, 1)
                for sg in range(2):
                    dve.wait_ge(r_hi, sg + 1)
                    for v in range(NKV):
                        dst, src = diagonal(core.rl, sg, v)
                        hi, _ = diagonal(core.rh, sg, v)
                        dve.tensor_tensor(dst, src, hi.bitcast(F32), ALU.subtract)


def total_up(dve, k, total, square, squared, totalled):
    dve.wait_ge(squared, k + 1)
    if k == 0:
        dve.tensor_copy(total[:], square[:]).then_inc(totalled, 1)
    else:
        dve.wait_ge(totalled, k)
        dve.tensor_tensor(total[:], total[:], square[:], ALU.add).then_inc(totalled, 1)


def mix_stage(nc, core, w, ahead):
    r2 = At(nc, Map.R2, Map.END)
    sa = [r2(f"sig_a_in{s}", [128, TW]) for s in range(2)]
    mb = [r2(f"mix_b_in{s}", [128, TW]) for s in range(2)]
    part = [r2(f"gated{s}", [128, TW]) for s in range(2)]
    mixed = [r2(f"mixed{s}", [128, TW]) for s in range(2)]
    total = core.total = nc.alloc_sbuf_tensor_at("squares_total", [128, TW], F32, offset=Map.TOTAL)
    loads = PA + KB
    with ExitStack() as ctx:
        sem = Sems(nc, ctx, "mx")
        gates_in = [sem(f"gates_in{s}") for s in range(2)]
        ready, gated, mixed_ok, hi, lo = sem("acc_ready"), sem("gated"), sem("mixed_ok"), sem("hi"), sem("lo")
        added, x_in, squared, totalled = sem("added"), sem("x_in"), sem("squared"), sem("totalled")
        wo = core.i["w_o"][0]
        arrived = [0] * loads
        for n in range(loads):
            arrived[n] = (arrived[n - 3] if n >= 3 else 0) + (32 if n < PA else 16)
        def mix(pool, t):
            pool.wait_ge(gated, t + 1)
            after(pool, lo, t - 1)
            pool.tensor_tensor(mixed[t % 2][:], part[t % 2][:], mb[t % 2][:], ALU.add).then_inc(mixed_ok, 1)
            if t % 2:
                n = t // 2 + 3
                w.lo(pool, n, n % 3)

        with nc.Block() as block:

            @block.sync
            def _(sp):
                for n in range(3, loads):
                    if n < PA:
                        sp.wait_ge(w.lo_done, n - 2)
                        for (parts, cols, m), src in pa_pieces(core, n):
                            dst = core.wr[n % 3][parts, cols].rearrange("p (g m) -> p g m", m=m)
                            sp.dma_start(dst, src).then_inc(w.arrived[n % 3], 16)
                    else:
                        j = n - PA
                        w.fetch(sp, n, n % 3, [((0, 1024, 128), by_rows(wo, slice(128 * j, 128 * j + 128)))])
                assert loads % 3 == 0
                sp.wait_ge(w.lo_done, loads - 1)
                ahead.fetch(sp)

            @block.tensor
            def _(pe):
                for t in range(2 * KB):
                    if t < KB:
                        n, at = t // 2, 128 * (t % 2)
                        after(pe, gated, t - 1)
                        pe.wait_ge(w.lo_done, n + 1)
                        split_product(pe, core, t % 2, G,
                                      lambda k: core.wh[n % 3][:, 256 * k + at:256 * k + at + 128],
                                      lambda k: core.wl[n % 3][:, 256 * k + at:256 * k + at + 128],
                                      lambda k: core.rh[:, k, :], lambda k: core.rl[:, k, :]).then_inc(ready, 1)
                    else:
                        n = PA + t - KB
                        pe.wait_ge(gated, min(t - 1, KB))
                        after(pe, added, t - KB - 1)
                        w.product(pe, n, n % 3, t % 2,
                                  before=(lambda k: pe.wait_ge(lo, k + 1)) if t == KB else None).then_inc(ready, 1)

            @block.scalar
            def _(act):
                def gates(t):
                    act.dma_start(sa[t % 2][:], core.siga.ap()[t]).then_inc(gates_in[t % 2], 16)
                    act.dma_start(mb[t % 2][:], core.mixb.ap()[t]).then_inc(gates_in[t % 2], 16)

                gates(0)
                gates(1)
                for t in range(KB):
                    act.wait_ge(mixed_ok, t + 1)
                    if t + 2 < KB:
                        gates(t + 2)
                    act.activation(core.ah[:, t, :], mixed[t % 2][:], ACT.Copy).then_inc(hi, 1)
                    if t % 2:
                        n = t // 2 + 3
                        w.hi(act, n, n % 3, arrived[n], ready)
                for j in range(KB):
                    n = PA + 3 + j
                    if n < loads:
                        w.hi(act, n, n % 3, arrived[n], ready)
                    act.wait_ge(added, j + 1)
                    act.wait_ge(lo, KB)
                    after(act, totalled, j - 1)
                    act.activation(mixed[j % 2][:], core.x[:, j, :], ACT.Square).then_inc(squared, 1)

            @block.gpsimd
            def _(pool):
                for t in range(KB - 1):
                    mix(pool, t)
                pool.wait_ge(ready, KB)
                pool.dma_start(core.x[:].rearrange("p k t -> p (k t)"), core.xsave.ap()).then_inc(x_in, 16)
                mix(pool, KB - 1)
                for n in range(PA + 3, loads):
                    w.lo(pool, n, n % 3)
                pool.wait_ge(x_in, 16)

            @block.vector
            def _(dve):
                for t in range(KB + 1):
                    if t < KB:
                        dve.wait_ge(ready, t + 1)
                        dve.wait_ge(gates_in[t % 2], 32 * (t // 2 + 1))
                        after(dve, mixed_ok, t - 1)
                        dve.tensor_tensor(tri(part[t % 2][:]), tri(sa[t % 2][:]), core.acc(t % 2), ALU.mult).then_inc(gated, 1)
                    if t >= 1:
                        dve.wait_ge(hi, t)
                        dve.tensor_tensor(core.al[:, t - 1, :], mixed[(t - 1) % 2][:], core.ah[:, t - 1, :].bitcast(F32),
                                          ALU.subtract).then_inc(lo, 1)
                dve.wait_ge(x_in, 16)
                for j in range(KB):
                    dve.wait_ge(ready, KB + j + 1)
                    x = tri(core.x[:, j, :])
                    dve.tensor_tensor(x, x, core.acc(j % 2), ALU.add).then_inc(added, 1)
                    if j >= 1:
                        total_up(dve, j - 1, total, mixed[(j - 1) % 2], squared, totalled)
                total_up(dve, KB - 1, total, mixed[(KB - 1) % 2], squared, totalled)


def ffn_stage(nc, core, w, up):
    r2 = At(nc, Map.R2, Map.TOTAL)
    p = r2("ffn_a", [128, TW + 2])
    ub = r2("ffn_b", [128, TW])
    u = r2("ffn_conv", [128, TW])
    s = r2("ffn_silu", [128, TW])
    h = r2("ffn_inner", [128, TW])
    hh = r2("ffn_inner_hi", [128, TW], F32R)
    hl = r2("ffn_inner_lo", [128, TW], F32R)
    taps = r2("ffn_taps", [128, 19])
    p6 = r2("ffn_samples", [128, NB, 6])
    states = r2("ffn_states", [128, FB, 18])
    out = r2("ffn_states_out", [18, FF])
    EARLY = KB
    with ExitStack() as ctx:
        sem = Sems(nc, ctx, "ff")
        down, added = sem("down"), sem("added")
        ua_copied, ub_copied, taps_ok = sem("ua_copied"), sem("ub_copied"), sem("taps_ok")
        p6_ok, states_ok, conv, silued = sem("p6_ok"), sem("states_ok"), sem("conv"), sem("silued")
        h_ok, h_hi, h_lo, padded = sem("h_ok"), sem("h_hi"), sem("h_lo"), sem("padded")
        turned, copied, stored = sem("states_turned"), sem("states_copied"), sem("states_stored")
        squared, totalled = sem("squared"), sem("totalled")
        wup, wdown = core.i["ffn_up"][0], core.i["ffn_down"][0]

        def split_hi(act, slot, turn, *used):
            act.wait_ge(w.arrived[slot], 16 * (turn + 1))
            if used:
                act.wait_ge(*used)
            act.activation(core.wh[slot][:], core.wr[slot][:], ACT.Copy).then_inc(w.hi_done, 1)

        with nc.Block() as block:

            @block.sync
            def _(sp):
                def up_fetch(slot, at, done):
                    after(sp, w.lo_done, done)
                    sp.dma_start(core.wr[slot][:].rearrange("p (k m) -> p k m", m=128), by_rows(wup, bass.ds(at, 128)))\
                        .then_inc(w.arrived[slot], 16)

                def down_fetch(at, done):
                    after(sp, w.lo_done, done)
                    sp.dma_start(core.wr[2][:], wdown[bass.ds(at, 128), :]).then_inc(w.arrived[2], 16)

                with sp.Fori(1, FB) as j:
                    up_fetch(0, 128 * j, 3 * j - 2)
                    up_fetch(1, 128 * j + FF, 3 * j - 1)
                    down_fetch(128 * j - 128, 3 * j - 1)
                down_fetch(FF - 128, 3 * FB - 1)
                sp.wait_ge(copied, 1)
                sp.dma_start(core.o["ffn_conv_prompt"][0, 0], out[0:2, :]).then_inc(stored, 16)
                sp.dma_start(core.o["ffn_conv_sample"][0].rearrange("b w c -> (b w) c"), out[2:18, :]).then_inc(stored, 16)
                sp.wait_ge(stored, 32)

            @block.tensor
            def _(pe):
                def project(j):
                    first = isinstance(j, int)
                    for slot in range(1 if first else 0, 2):
                        pe.wait_ge(w.lo_done, slot + 1 if first else 3 * j + slot)
                        if not first:
                            pe.wait_ge(added, EARLY + 8 * j - 9 + slot)
                            pe.wait_ge((ua_copied, ub_copied)[slot], j)
                        split_product(pe, core, slot, KB,
                                      lambda k: core.wh[slot][:, 128 * k:128 * k + 128],
                                      lambda k: core.wl[slot][:, 128 * k:128 * k + 128],
                                      lambda k: core.ah[:, k, :], lambda k: core.al[:, k, :]).then_inc(up, 1)

                def collect(j, ahead):
                    pe.wait_ge(w.lo_done, 3 * j + 5 if ahead else 3 * j + 3)
                    pe.wait_ge(h_lo, j + 1)
                    for d in range(KB):
                        if d >= 2:
                            pe.wait_ge(added, EARLY + 8 * j + d - 1)
                        elif ahead:
                            pe.wait_ge((ua_copied, ub_copied)[d], j + 2)
                        else:
                            pe.wait_ge(added, EARLY + 8 * j - 1 + d)
                        split_product(pe, core, d % 2, 1,
                                      lambda k: core.wh[2][:, 128 * d:128 * d + 128],
                                      lambda k: core.wl[2][:, 128 * d:128 * d + 128],
                                      lambda k: hh[:], lambda k: hl[:]).then_inc(down, 1)

                project(0)
                with pe.Fori(1, FB) as j:
                    project(j)
                    collect(j - 1, True)
                collect(FB - 1, False)
                pe.wait_ge(added, EARLY + 8 * FB)
                pe.wait_ge(states_ok, FB)
                for k in range(FB):
                    last = pe.transpose(core.flat(0, FF, 18)[:, 128 * k:128 * k + 128], states[:, k, :], core.c["ident"])
                last.then_inc(turned, 1)

            @block.scalar
            def _(act):
                def turn(j, last=False):
                    first = isinstance(j, int) and j == 0
                    act.wait_ge(up, 2 * j + 1)
                    if not first:
                        act.wait_ge(conv, 4 * j)
                        act.wait_ge(states_ok, j)
                    act.activation(tri(p[:, 2:2 + TW]), core.acc(0), ACT.Copy).then_inc(ua_copied, 1)
                    if not last:
                        split_hi(act, 0, j + 1, up, 2 * j + 1)
                    act.wait_ge(up, 2 * j + 2)
                    if not first:
                        act.wait_ge(h_ok, j)
                    act.activation(tri(ub[:]), core.acc(1), ACT.Copy).then_inc(ub_copied, 1)
                    if not last:
                        split_hi(act, 1, j + 1, up, 2 * j + 2)
                    act.wait_ge(conv, 4 * j + 4)
                    if first:
                        act.wait_ge(padded, 1)
                    else:
                        act.wait_ge(h_ok, j)
                    act.activation(s[:], u[:], ACT.Silu).then_inc(silued, 1)
                    if first:
                        split_hi(act, 2, j)
                    else:
                        split_hi(act, 2, j, down, 8 * j)
                    act.wait_ge(h_ok, j + 1)
                    if not first:
                        act.wait_ge(down, 8 * j)
                        act.wait_ge(h_lo, j)
                    act.activation(hh[:], h[:], ACT.Copy).then_inc(h_hi, 1)

                turn(0)
                with act.Fori(1, FB - 1) as j:
                    turn(j)
                turn(FB - 1, last=True)
                for k in range(KB):
                    act.wait_ge(added, EARLY + 8 * (FB - 1) + k + 1)
                    after(act, totalled, k - 1)
                    act.activation((s, ub)[k % 2][:], core.x[:, k, :], ACT.Square).then_inc(squared, 1)
                act.wait_ge(turned, 1)
                act.activation(out[:], core.flat(0, FF, 18), ACT.Copy).then_inc(copied, 1)

            @block.gpsimd
            def _(pool):
                def split_lo(slot, done):
                    pool.wait_ge(w.hi_done, done)
                    pool.tensor_tensor(core.wl[slot][:], core.wr[slot][:], core.wh[slot][:].bitcast(F32), ALU.subtract)\
                        .then_inc(w.lo_done, 1)

                def turn(j, last=False):
                    first = isinstance(j, int) and j == 0
                    if not last:
                        split_lo(0, 3 * j + 3)
                        split_lo(1, 3 * j + 4)
                    pool.wait_ge(silued, j + 1)
                    pool.wait_ge(ub_copied, j + 1)
                    if not first:
                        pool.wait_ge(h_hi, j)
                        pool.wait_ge(h_lo, j)
                    pool.tensor_tensor(h[:], s[:], ub[:], ALU.mult).then_inc(h_ok, 1)
                    split_lo(2, 3 * j + (3 if last else 5))
                    pool.wait_ge(h_hi, j + 1)
                    pool.tensor_tensor(hl[:], h[:], hh[:].bitcast(F32), ALU.subtract).then_inc(h_lo, 1)

                pool.memset(p[:, 0:2], 0.0)
                pool.memset(u[:, TOK:TW], 0.0).then_inc(padded, 1)
                pool.wait_ge(padded, 1)
                turn(0)
                with pool.Fori(1, FB - 1) as j:
                    turn(j)
                turn(FB - 1, last=True)

            @block.vector
            def _(dve):
                def convolve(j):
                    us = u[:, TP:TOK].rearrange("p (b t) -> p b t", t=DS)
                    new = p[:, 2 + TP:2 + TOK].rearrange("p (b t) -> p b t", t=DS)
                    first = isinstance(j, int) and j == 0
                    dve.wait_ge(ua_copied, j + 1)
                    dve.wait_ge(taps_ok, j + 1)
                    dve.tensor_copy(p6[:, :, 0:2], taps[:, 0:16].rearrange("p (b w) -> p b w", w=2))
                    dve.tensor_copy(p6[:, :, 2:6], new).then_inc(p6_ok, 1)
                    row = states[:, bass.ds(j, 1), :]
                    dve.tensor_copy(row[:, :, 0:2], p[:, TP:TP + 2].rearrange("p (a w) -> p a w", a=1))
                    dve.tensor_copy(row[:, :, 2:18].rearrange("p a (b w) -> p (a b) w", w=2), new[:, :, 2:4])\
                        .then_inc(states_ok, 1)
                    dve.wait_ge(p6_ok, j + 1)
                    if not first:
                        dve.wait_ge(silued, j)
                    else:
                        dve.wait_ge(padded, 1)
                    dve.tensor_scalar(u[:, 0:TP], p[:, 0:TP], taps[:, 16:17], None, ALU.mult)
                    dve.tensor_scalar(us, p6[:, :, 0:4], taps[:, 16:17], None, ALU.mult).then_inc(conv, 1)
                    for x in (1, 2):
                        dve.wait_ge(conv, 4 * j + x)
                        dve.scalar_tensor_tensor(u[:, 0:TP], p[:, x:x + TP], taps[:, 16 + x:17 + x], u[:, 0:TP],
                                                 ALU.mult, ALU.add)
                        dve.scalar_tensor_tensor(us, p6[:, :, x:x + 4], taps[:, 16 + x:17 + x], us, ALU.mult, ALU.add)\
                            .then_inc(conv, 1 if x == 1 else 2)
                    dve.wait_ge(conv, 4 * j + 4)

                def fetch_taps(j):
                    dve.tensor_copy(taps[:], core.fconv[:, bass.ds(j, 1), :].rearrange("p a r -> p (a r)"))\
                        .then_inc(taps_ok, 1)

                def add(j, last=False):
                    for d in range(KB):
                        dve.wait_ge(down, 8 * j + d + 1)
                        dve.wait_ge(added, EARLY + 8 * j + d - 7)
                        x = tri(core.x[:, d, :])
                        dve.tensor_tensor(x, x, core.acc(d % 2), ALU.add).then_inc(added, 1)
                        if last and d >= 1:
                            total_up(dve, d - 1, core.total, (s, ub)[(d - 1) % 2], squared, totalled)
                    if last:
                        total_up(dve, KB - 1, core.total, (s, ub)[(KB - 1) % 2], squared, totalled)

                dve.memset(p6[:, 0, 0:2], 0.0).then_inc(added, EARLY)
                dve.wait_ge(added, EARLY)
                fetch_taps(0)
                convolve(0)
                fetch_taps(1)
                with dve.Fori(1, FB - 1) as j:
                    convolve(j)
                    add(j - 1)
                    fetch_taps(j + 1)
                convolve(FB - 1)
                add(FB - 2)
                add(FB - 1, last=True)


def output_stage(nc, core):
    r2 = At(nc, Map.R2, Map.TOTAL)
    rows = [r2(f"y_rows{s}", [128, D]) for s in range(3)]
    gain = r2("gain_of_every_token", [128, D])
    parts = [2 if t == NT - 1 else 1 for t in range(NT)]
    sem = Sems(nc, None, "out")
    summed, taken, rooted, own, gain_in = sem("summed"), sem("taken"), sem("rooted"), sem("own"), sem("gain_in")
    turned, copied = sem("turned"), sem("copied")
    stored = [sem(f"stored{s}") for s in range(3)]
    with nc.Block() as block:

        @block.tensor
        def _(pe):
            sum_features(pe, core, core.total, summed)
            for t in range(NT):
                after(pe, copied, t - 2)
                n = ROWS[t]
                for k in range(KB):
                    last = pe.transpose(core.flat(2 * (t % 3), D, n)[:, 128 * k:128 * k + 128],
                                        core.x[:, k, 128 * t:128 * t + n], core.c["ident"])
                last.then_inc(turned, 1)

        @block.scalar
        def _(act):
            act.dma_start(gain[:], core.i["norm_final"].rearrange("(a d) -> a d", a=1).broadcast_to([128, D]))\
                .then_inc(gain_in, 16)
            inverse_roots(act, None, core, rooted, own)
            act.wait_ge(gain_in, 16)

        @block.vector
        def _(dve):
            take_sums(dve, core, summed, taken)
            inverse_roots(None, dve, core, rooted, own)
            dve.wait_ge(gain_in, 16)
            for t in range(NT):
                n = ROWS[t]
                dve.wait_ge(turned, t + 1)
                if t >= 3:
                    dve.wait_ge(stored[t % 3], 16 * (t // 3))
                dve.scalar_tensor_tensor(rows[t % 3][0:n, :], core.flat(2 * (t % 3), D, n), core.inv[0:n, t:t + 1],
                                         gain[0:n, :], ALU.mult, ALU.mult).then_inc(copied, 1)

        @block.sync
        def _(sp):
            y = core.o["y_prompt"][0]
            for t in range(NT):
                sp.wait_ge(copied, t + 1)
                a = META if t == 0 else 0
                sp.dma_start(y[128 * t + a - META:128 * t + QROWS[t] - META], rows[t % 3][a:QROWS[t], :])\
                    .then_inc(stored[t % 3], 16)
            sp.dma_start(core.o["y_sample"].rearrange("b s d -> (b s) d"), rows[(NT - 1) % 3][QROWS[-1]:ROWS[-1], :])\
                .then_inc(stored[(NT - 1) % 3], 16)
            for s in range(3):
                sp.wait_ge(stored[s], 16 * sum(parts[s::3]))


OUTS = {
    "y_prompt": (1, SEQ, D), "y_sample": (NB, DS, D),
    "k_prompt": (1, 1, TP, NKV, HD), "v_prompt": (1, 1, TP, NKV, HD), "kidx_prompt": (1, 1, TP, HD),
    "conv_prompt": (1, 1, 2, CD), "ffn_conv_prompt": (1, 1, 2, FF),
    "k_sample": (1, NB, DS, NKV, HD), "v_sample": (1, NB, DS, NKV, HD), "kidx_sample": (1, NB, DS, HD),
    "conv_sample": (1, NB, 2, CD), "ffn_conv_sample": (1, NB, 2, FF),
}


def program(nc, ins, outs):
    core = Core(nc, ins, outs)
    core.hd = Heads(nc)
    hd = core.hd

    def first():
        ix = index_ahead(nc, core)
        gt = gate_ahead(nc, core)
        return [lambda: load_stage(nc, core, ix), lambda: norm_stage(nc, core, 0, "norm1", ix),
                lambda: index_stage(nc, core, hd, ix.w, ix.ready, gt), lambda: sample_index_stage(nc, core, hd, gt),
                lambda: gate_stage(nc, core, hd, gt.w)]

    def second():
        mx = mix_ahead(nc, core)
        ff = ffn_ahead(nc, core)
        return [lambda: rope_stage(nc, core, hd), lambda: prompt_attention_stage(nc, core, hd),
                lambda: sample_attention_stage(nc, core, hd, mx), lambda: mix_stage(nc, core, mx.w, ff),
                lambda: norm_stage(nc, core, 1, "norm2", ff, core.total),
                lambda: ffn_stage(nc, core, ff.w, ff.ready), lambda: output_stage(nc, core)]

    for group in (first, second):
        with nc.cleanup_on_exit():
            for stage in group():
                stage()
    return core


def kernel(x_prompt, x_sample, cache_k, cache_v, cache_kidx, state_conv, state_ffn_conv, page_table,
           meta_tokens, w_in, w_pa, w_pb, w_o, conv_w, norm1, norm2, ffn_up, ffn_conv_w, ffn_down, norm_final):
    import concourse.bacc as bacc
    from concourse.bass_utils import run_bass_kernel_spmd

    arrays = dict(x_prompt=x_prompt, x_sample=x_sample, cache_k=cache_k, cache_v=cache_v, cache_kidx=cache_kidx,
                  state_conv=state_conv, state_ffn_conv=state_ffn_conv, page_table=page_table,
                  meta_tokens=meta_tokens, w_in=w_in, w_pa=w_pa, w_pb=w_pb, w_o=w_o, conv_w=conv_w, norm1=norm1,
                  norm2=norm2, ffn_up=ffn_up, ffn_conv_w=ffn_conv_w, ffn_down=ffn_down, norm_final=norm_final)
    arrays = {name: np.ascontiguousarray(a) for name, a in arrays.items()}
    arrays["constants"] = constants()
    nc = bacc.Bacc("TRN2", target_bir_lowering=False, num_devices=1)
    ins = {name: nc.dram_tensor(f"in_{name}", list(a.shape), I32 if name == "page_table" else F32,
                                kind="ExternalInput").ap() for name, a in arrays.items()}
    outs = {name: nc.dram_tensor(f"out_{name}", list(shape), F32, kind="ExternalOutput").ap()
            for name, shape in OUTS.items()}
    program(nc, ins, outs)
    result = run_bass_kernel_spmd(nc, [{f"in_{name}": a for name, a in arrays.items()}], core_ids=[0]).results[0]
    return tuple(result[f"out_{name}"] for name in OUTS)
```
